# Optimizing a Trainium2 kernel written in Bass

```python
import math
import jax, jax.numpy as jnp
from jax import lax
import numpy as np

D_MODEL = 1024
BATCH = 1
SEQ = 512
DEPTH = 1
DEC_BATCH = 1
DEC_SEQ = 64
PAST_LEN = 256

CHUNK = 64
Q_BLOCK = 128
A_QK_DIM = 64
A_V_DIM = 2 * A_QK_DIM
A_HEADS = D_MODEL // 256
A_WIDTH = A_HEADS * A_V_DIM
B_DIM = 64
B_HEADS = D_MODEL // 128
B_WIDTH = B_HEADS * B_DIM
MIX_WIDTH = A_WIDTH + B_WIDTH
IN_SPLITS = [A_WIDTH, 2 * A_WIDTH, 3 * A_WIDTH, 3 * A_WIDTH + B_WIDTH, 3 * A_WIDTH + 2 * B_WIDTH]
IN_COLS = 3 * A_WIDTH + 3 * B_WIDTH
N_EXPERTS = 64
TOP_K = 6
N_GROUPS = 8
TOPK_GROUPS = 4
EXPERTS_PER_GROUP = N_EXPERTS // N_GROUPS
D_EXPERT = D_MODEL // 4
D_SHARED = D_MODEL // 4
ROUTED_SCALE = 2.5
EPS = 1e-6
NEG_INF = -1e30

kernel_name = "hymba_diffattn_stickbreak_moe_adaln_stream_step"

def rms(x):
    xf = x.astype(jnp.float32)
    y = xf * lax.rsqrt(jnp.mean(xf * xf, axis=-1, keepdims=True) + EPS)
    return y.astype(x.dtype)

def lambda_init_of(layer):
    return 0.8 - 0.6 * math.exp(-0.3 * layer)

def alibi_slopes():
    return jnp.exp2(-8.0 * (jnp.arange(A_HEADS, dtype=jnp.float32) + 1.0) / A_HEADS)

def diff_attention(q, k, v, qpos, kpos, lam):
    s = jnp.einsum('bqhmd,bkhmd->bmhqk', q, k).astype(jnp.float32) * (A_QK_DIM ** -0.5)
    dist = jnp.abs(qpos[:, None] - kpos[None, :]).astype(jnp.float32)
    bias = -alibi_slopes()[:, None, None] * dist
    visible = (kpos[None, :] // CHUNK) <= (qpos[:, None] // CHUNK)
    s = jnp.where(visible, s + bias, NEG_INF)
    p = jax.nn.softmax(s, axis=-1)
    w = p[:, 0] - lam * p[:, 1]
    return jnp.einsum('bhqk,bkhd->bqhd', w.astype(v.dtype), v)

def stick_breaking(q, k, v, qpos, kpos):
    z = jnp.einsum('bqhd,bkhd->bhqk', q, k).astype(jnp.float32) * (B_DIM ** -0.5)
    before = kpos[None, :] < qpos[:, None]
    log_keep = jnp.where(before, jax.nn.log_sigmoid(-z), 0.0)
    rev = lax.cumsum(log_keep, axis=3, reverse=True)
    after = jnp.concatenate([rev[..., 1:], jnp.zeros_like(rev[..., :1])], axis=-1)
    a = jnp.where(before, jnp.exp(jax.nn.log_sigmoid(z) + after), 0.0)
    return jnp.einsum('bhqk,bkhd->bqhd', a.astype(v.dtype), v)

def sweep_queries(fn, q, qpos):
    b, t = q.shape[:2]
    if t % Q_BLOCK != 0 or t <= Q_BLOCK:
        return fn(q, qpos)
    nb = t // Q_BLOCK
    qb = jnp.moveaxis(q.reshape((b, nb, Q_BLOCK) + q.shape[2:]), 1, 0)
    pb = qpos.reshape(nb, Q_BLOCK)
    out = lax.map(lambda blk: fn(blk[0], blk[1]), (qb, pb))
    out = jnp.moveaxis(out, 0, 1)
    return out.reshape((b, t) + out.shape[3:])

def moe_ffn(h, p):
    t = h.shape[0]
    scores = jax.nn.sigmoid((h @ p['w_router']).astype(jnp.float32))
    sel = scores + p['b_router'].astype(jnp.float32)
    group_score = lax.top_k(sel.reshape(t, N_GROUPS, EXPERTS_PER_GROUP), 2)[0].sum(-1)
    _, gidx = lax.top_k(group_score, TOPK_GROUPS)
    gkeep = jnp.any(gidx[..., None] == jnp.arange(N_GROUPS), axis=-2)
    sel = jnp.where(jnp.repeat(gkeep, EXPERTS_PER_GROUP, axis=-1), sel, NEG_INF)
    _, eidx = lax.top_k(sel, TOP_K)
    wts = jnp.take_along_axis(scores, eidx, axis=-1)
    wts = wts / jnp.sum(wts, axis=-1, keepdims=True) * ROUTED_SCALE
    comb = jnp.sum((eidx[..., None] == jnp.arange(N_EXPERTS)) * wts[..., None], axis=-2)
    g = jnp.einsum('td,edf->tef', h, p['w_gate'])
    u = jnp.einsum('td,edf->tef', h, p['w_up'])
    a = jax.nn.silu(g) * u * comb[..., None].astype(h.dtype)
    routed = jnp.einsum('tef,efd->td', a, p['w_down'])
    shared = (jax.nn.silu(h @ p['w_sg']) * (h @ p['w_su'])) @ p['w_sd']
    return routed + shared

def trunk_layer(x, c, past, layer, p):
    b, t, _ = x.shape
    mod = jax.nn.silu(c) @ p['w_ada'] + p['b_ada']
    sh1, sc1, g1, sh2, sc2, g2 = jnp.split(mod, 6, axis=-1)
    h = rms(x) * (1 + sc1[:, None]) + sh1[:, None]
    proj = h @ p['w_in']
    qa, ka, va, qb, kb, vb = jnp.split(proj, IN_SPLITS, axis=-1)
    ka = ka.reshape(b, t, A_HEADS, 2 * A_QK_DIM)
    va = va.reshape(b, t, A_HEADS, A_V_DIM)
    kb = kb.reshape(b, t, B_HEADS, B_DIM)
    vb = vb.reshape(b, t, B_HEADS, B_DIM)
    new_rows = (ka, va, kb, vb)
    if past is None:
        pos0 = 0
        ka_all, va_all, kb_all, vb_all = ka, va, kb, vb
    else:
        pk_a, pv_a, pk_b, pv_b = past
        pos0 = pk_a.shape[1]
        ka_all = jnp.concatenate([pk_a, ka], axis=1)
        va_all = jnp.concatenate([pv_a, va], axis=1)
        kb_all = jnp.concatenate([pk_b, kb], axis=1)
        vb_all = jnp.concatenate([pv_b, vb], axis=1)
    qpos = pos0 + jnp.arange(t, dtype=jnp.int32)
    kpos = jnp.arange(pos0 + t, dtype=jnp.int32)

    lam_init = lambda_init_of(layer)
    lp = p['lam'].astype(jnp.float32)
    lam = jnp.exp(jnp.sum(lp[0] * lp[1])) - jnp.exp(jnp.sum(lp[2] * lp[3])) + lam_init
    qa5 = qa.reshape(b, t, A_HEADS, 2, A_QK_DIM)
    ka5 = ka_all.reshape(b, pos0 + t, A_HEADS, 2, A_QK_DIM)
    oa = sweep_queries(lambda qq, pp: diff_attention(qq, ka5, va_all, pp, kpos, lam), qa5, qpos)
    oa = rms(oa) * p['g_sub_a'] * (1.0 - lam_init)

    qb4 = qb.reshape(b, t, B_HEADS, B_DIM)
    ob = sweep_queries(lambda qq, pp: stick_breaking(qq, kb_all, vb_all, pp, kpos), qb4, qpos)
    ob = rms(ob) * p['g_sub_b']

    o = jnp.concatenate([oa.reshape(b, t, A_WIDTH), ob.reshape(b, t, B_WIDTH)], axis=-1) @ p['w_out']
    x = x + g1[:, None] * o

    h2 = rms(x) * (1 + sc2[:, None]) + sh2[:, None]
    x = x + g2[:, None] * lax.map(lambda hs: moe_ffn(hs, p), h2)
    return x, new_rows

def setup_inputs(seed: int = 0) -> dict:
    key = jax.random.key(seed)
    ks = jax.random.split(key, 26)
    f32 = jnp.float32
    nrm = lambda k, shape, s: jax.random.normal(k, shape, f32) * s
    d = D_MODEL
    return {
        'x_prompt': nrm(ks[0], (BATCH, SEQ, d), 1.0),
        'x_sample': nrm(ks[1], (DEC_BATCH, DEC_SEQ, d), 1.0),
        'cache_a_k': nrm(ks[2], (DEPTH, DEC_BATCH, PAST_LEN, A_HEADS, 2 * A_QK_DIM), 1.0),
        'cache_a_v': nrm(ks[3], (DEPTH, DEC_BATCH, PAST_LEN, A_HEADS, A_V_DIM), 1.0),
        'cache_b_k': nrm(ks[4], (DEPTH, DEC_BATCH, PAST_LEN, B_HEADS, B_DIM), 1.0),
        'cache_b_v': nrm(ks[5], (DEPTH, DEC_BATCH, PAST_LEN, B_HEADS, B_DIM), 1.0),
        'c_prompt': nrm(ks[6], (BATCH, d), 1.0),
        'c_sample': nrm(ks[7], (DEC_BATCH, d), 1.0),
        'w_ada': nrm(ks[8], (DEPTH, d, 6 * d), 0.5 * d ** -0.5),
        'b_ada': nrm(ks[9], (DEPTH, 6 * d), 0.02),
        'w_in': nrm(ks[10], (DEPTH, d, IN_COLS), d ** -0.5),
        'lam_params': nrm(ks[11], (DEPTH, 4, A_QK_DIM), 0.1),
        'g_sub_a': 1.0 + nrm(ks[12], (DEPTH, A_V_DIM), 0.02),
        'g_sub_b': 1.0 + nrm(ks[13], (DEPTH, B_DIM), 0.02),
        'w_out': nrm(ks[14], (DEPTH, MIX_WIDTH, d), MIX_WIDTH ** -0.5),
        'w_router': nrm(ks[15], (DEPTH, d, N_EXPERTS), d ** -0.5),
        'b_router': nrm(ks[16], (DEPTH, N_EXPERTS), 0.01),
        'w_gate': nrm(ks[17], (DEPTH, N_EXPERTS, d, D_EXPERT), d ** -0.5),
        'w_up': nrm(ks[18], (DEPTH, N_EXPERTS, d, D_EXPERT), d ** -0.5),
        'w_down': nrm(ks[19], (DEPTH, N_EXPERTS, D_EXPERT, d), D_EXPERT ** -0.5),
        'w_shared_gate': nrm(ks[20], (DEPTH, d, D_SHARED), d ** -0.5),
        'w_shared_up': nrm(ks[21], (DEPTH, d, D_SHARED), d ** -0.5),
        'w_shared_down': nrm(ks[22], (DEPTH, D_SHARED, d), D_SHARED ** -0.5),
        'g_final': 1.0 + nrm(ks[23], (d,), 0.02),
    }

def reference(x_prompt, x_sample, cache_a_k, cache_a_v, cache_b_k, cache_b_v, c_prompt, c_sample,
              w_ada, b_ada, w_in, lam_params, g_sub_a, g_sub_b, w_out, w_router, b_router,
              w_gate, w_up, w_down, w_shared_gate, w_shared_up, w_shared_down, g_final):
    xp, xs = x_prompt, x_sample
    rows_p, rows_s = [], []
    for l in range(DEPTH):
        p = {'w_ada': w_ada[l], 'b_ada': b_ada[l], 'w_in': w_in[l], 'lam': lam_params[l],
             'g_sub_a': g_sub_a[l], 'g_sub_b': g_sub_b[l], 'w_out': w_out[l],
             'w_router': w_router[l], 'b_router': b_router[l], 'w_gate': w_gate[l],
             'w_up': w_up[l], 'w_down': w_down[l], 'w_sg': w_shared_gate[l],
             'w_su': w_shared_up[l], 'w_sd': w_shared_down[l]}
        xp, rp = trunk_layer(xp, c_prompt, None, l, p)
        xs, rs = trunk_layer(xs, c_sample, (cache_a_k[l], cache_a_v[l], cache_b_k[l], cache_b_v[l]), l, p)
        rows_p.append(rp)
        rows_s.append(rs)
    y_prompt = rms(xp) * g_final
    y_sample = rms(xs) * g_final
    new_a_k_p = jnp.stack([r[0] for r in rows_p])
    new_a_v_p = jnp.stack([r[1] for r in rows_p])
    new_b_k_p = jnp.stack([r[2] for r in rows_p])
    new_b_v_p = jnp.stack([r[3] for r in rows_p])
    new_a_k_s = jnp.stack([r[0] for r in rows_s])
    new_a_v_s = jnp.stack([r[1] for r in rows_s])
    new_b_k_s = jnp.stack([r[2] for r in rows_s])
    new_b_v_s = jnp.stack([r[3] for r in rows_s])
    return (y_prompt, y_sample, new_a_k_p, new_a_v_p, new_b_k_p, new_b_v_p, new_a_k_s, new_a_v_s, new_b_k_s, new_b_v_s)


_drawn_inputs = setup_inputs


def setup_inputs(seed=0):
    import zlib

    import numpy as np

    out = dict(_drawn_inputs(seed))
    spreads = {}
    factors = {'cache_b_k': 3.176, 'g_sub_a': 4.39, 'g_sub_b': 3.524, 'g_final': 2.908}
    for name, (base, spread) in spreads.items():
        noise = np.random.default_rng([zlib.crc32(name.encode()), seed]).standard_normal(out[name].shape)
        drawn = base * np.exp(spread * noise) if base else spread * noise
        out[name] = __import__('jax').numpy.asarray(drawn.astype(out[name].dtype))
    for name, factor in factors.items():
        out[name] = (out[name] * factor).astype(out[name].dtype)
    return out
```

```python
from contextlib import ExitStack

import concourse.bass as bass
from concourse import mybir

F32 = mybir.dt.float32
I32 = mybir.dt.int32
U32 = mybir.dt.uint32
ALU = mybir.AluOpType
ACT = mybir.ActivationFunctionType
AX = mybir.AxisListType.X

P = 128
D = 1024
KC = D // P
TP, TS = 512, 64
T = TP + TS
NT = TP // P + 1
ROWS = [P, P, P, P, TS]
PAST = 256
PT = PAST // P
HA, HB = 4, 8
DB = 64
NE, NG, EG = 64, 8, 8
TOPK, TOPG = 6, 4
FE = 256
EPS = 1e-6
BIG = 1e30
LAM0 = 0.8 - 0.6
ADA_FIRST = 4
SLOT = 64
NI = NE + T * TOPK // SLOT
IC = NI + 3
YK = 8
NONE = 1 << 20


def build(nc, x_prompt, x_sample, cache_a_k, cache_a_v, cache_b_k, cache_b_v, c_prompt, c_sample, w_ada, b_ada,
          w_in, lam_params, g_sub_a, g_sub_b, w_out, w_router, b_router, w_gate, w_up, w_down, w_sg, w_su, w_sd,
          g_final, y_prompt, y_sample, ak_p, av_p, bk_p, bv_p, ak_s, av_s, bk_s, bv_s):
    ctx = ExitStack()
    with ctx:
        sem = lambda name: ctx.enter_context(nc.semaphore(name))

        N_ARENA = 53000
        arena = ctx.enter_context(nc.sbuf_tensor("arena", [P, N_ARENA], F32))
        bank = [ctx.enter_context(nc.psum_tensor(f"bank{i}", [P, 512], F32)) for i in range(8)]
        top = [0]

        def take(n):
            top[0] += n
            assert top[0] <= N_ARENA, top[0]
            return top[0] - n

        def at(base, *shape, dt=F32):
            n = 1
            for s in shape:
                n *= s
            v = arena[:, base:base + n]
            if dt != F32:
                v = v.bitcast(dt)
            if len(shape) == 2:
                v = v.rearrange("p (a b) -> p a b", b=shape[1])
            elif len(shape) == 3:
                v = v.rearrange("p (a b c) -> p a b c", b=shape[1], c=shape[2])
            return v

        a_x = take(NT * D)
        a_h = take(NT * D)
        a_ring = take(3 * 4096)
        a_att = take(KC * T * 2 + KC * PAST + NT * D + PT * D)
        a_tmp = take(7168)
        X = at(a_x, NT, D)
        HT = at(a_h, KC, T)
        OA = at(a_h, NT, D)
        YA = at(a_h, NT, D)
        RING = [at(a_ring + 4096 * i, KC, 512) for i in range(3)]
        QT = at(a_att, KC, T)
        OT = QT
        a_kt = a_att + KC * T
        KT = at(a_kt, KC, T)
        GO = KT
        a_ckt = a_kt + KC * T
        CKT = at(a_ckt, KC, PAST)
        a_v = a_ckt + KC * PAST
        V = at(a_v, NT, D)
        XN = V
        CV = at(a_v + NT * D, PT, D)
        BIAS = at(a_tmp, HA, 512)
        KO = at(a_tmp + 2048, 3, 512)
        CK = at(a_tmp + 3584, PT, D)
        SE = at(a_tmp + 3584, 2, 2, 512)
        WT = at(a_tmp + 5632, 2, 512)
        LK = at(a_tmp, 2, 1536)
        AT = at(a_tmp + 3072, 2, 1536)
        SQ = at(a_tmp, 2, D)
        H2S = at(a_tmp, 2, D)
        SG = at(a_tmp + 2048, 2, T)
        AS = at(a_tmp + 3200, 2, T)
        WSD = at(a_tmp + 5120, 2, D)
        GU = [RING[0], RING[1], RING[2], at(a_att, KC, 512)]
        DN = [at(a_att + 4096 + 2048 * i, 2, D) for i in range(4)]
        HG = at(a_tmp, D)
        HGT = at(a_tmp + 1024, KC, SLOT)
        YT = at(a_tmp + 1536, KC, SLOT)
        YO = at(a_tmp + 2048, D)
        SI = at(a_tmp + 3072, 2 * SLOT)
        AE = at(a_tmp + 3200, 2, SLOT)
        G2 = at(a_tmp + 3328, 2, D)
        GF = at(a_tmp + 5376, D)
        YB = [at(a_ring + 6144 * i, TOPK, D) for i in range(2)]
        IDENT = at(take(P), P)
        NTRI = at(take(P), P)
        NONES = at(take(P), P)
        UP = at(take(P), P)
        ONES = at(take(P), P)
        SMT = at(take(66), 66)
        CT = at(take(16), 16)
        MOD = at(take(96), 48, 2)
        WR = at(take(KC * NE), KC, NE)
        BR = at(take(NE), NE)
        GA = at(take(2), 2)
        SS = at(take(NT), NT)
        RS = at(take(NT), NT)
        HALF = at(take(60), NT, 12)
        SUMS = at(take(NT * HA * 2), NT, HA, 2)
        MINS = at(take(4), 2, 2)
        CO = at(take(2), 2, 1)
        OS = at(take(60), NT, 12)
        OR = at(take(60), NT, 12)
        LAM = at(take(2), 2)
        NLAM = at(take(1), 1)
        a_route = a_v
        small = at(take(P), 1, P)
        SMALL = small[:, 0, :]
        IDX = at(take(2 * IC), 2, IC, dt=U32)
        ICUR = at(take(2), 2, dt=U32)
        START = at(take(NE + 2), NE + 2, dt=I32)
        W6 = at(take(NT * YK), NT, YK)
        LPX = at(take(256), 256)
        LPM = at(take(128), 128)
        r0 = [a_att + 4096 + 4 * 2048]

        def rt(*shape, dt=F32):
            n = 1
            for s in shape:
                n *= s
            r0[0] += n
            assert r0[0] <= a_tmp
            return at(r0[0] - n, *shape, dt=dt)

        SC = rt(NT, NE)
        SEL = rt(NT, NE)
        G8 = rt(NT * NG, 8)
        GS = rt(NT, 12)
        GTOP = rt(NT, 8)
        GREP = rt(NT, 8)
        GOUT = rt(NT, 12)
        KEEP = rt(NT, NG)
        NEGK = rt(NT, NG)
        SELX = rt(NT, NE + 2)
        ETOP = rt(NT, 8)
        EREP = rt(NT, 8)
        EOUT = rt(NT, NE + 2)
        M = rt(NT, NE)
        COMB = rt(NT, NE)
        DEN = rt(NT)
        RDEN = rt(NT)
        NB_I = rt(NE, dt=I32)
        NB_J = rt(NE, dt=I32)
        NB = rt(NE)
        ZE = rt(NE)
        INC = rt(NE)
        STF = rt(NE + 2)
        SB = rt(NE)
        SL = rt(NT, NE)
        S8 = rt(NT, 8)
        SIDX = rt(NT, 8, dt=I32)
        REC = rt(NT, 8, dt=I32)
        TI = rt(SLOT, dt=I32)
        TF = rt(SLOT)
        EJ = rt(NE)
        G2C = [rt(KC, P) for _ in range(2)]

        h2_rows = nc.dram_tensor("h2_rows", (T, D), F32, kind="Internal").ap()
        y_rows = nc.dram_tensor("y_rows", (T * YK, D), F32, kind="Internal").ap()
        slots = nc.dram_tensor("slots", (IC * SLOT, 1), I32, kind="Internal").ap()

        pe_mark, pool_mark = sem("pe_mark"), sem("pool_mark")
        small_ld, x_ld, misc_ld, ck_ld, cv_ld, wsd_ld = map(sem, ("small_ld", "x_ld", "misc_ld", "ck_ld", "cv_ld", "wsd_ld"))
        ring_ld = [sem(f"ring_ld{i}") for i in range(3)]
        pool_c, pool_s, dve_s, act_s = map(sem, ("pool_c", "pool_s", "dve_s", "act_s"))
        small_t, smt_ready, c_ready = map(sem, ("small_t", "smt_ready", "c_ready"))
        lam_sum, lam_exp, lam_neg, lam_bc, nlam_ready = map(sem, ("lam_sum", "lam_exp", "lam_neg", "lam_bc", "nlam_ready"))
        mod_mm, mod_ready = sem("mod_mm"), sem("mod_ready")
        sq_done, ms_ready, rs_ready, xn_ready = map(sem, ("sq_done", "ms_ready", "rs_ready", "xn_ready"))
        tr_done, tr_dve, tr_act = map(sem, ("tr_done", "tr_dve", "tr_act"))
        proj_done, proj_act, proj_dve = map(sem, ("proj_done", "proj_act", "proj_dve"))
        kb_done, kb_evac, new_stored = map(sem, ("kb_done", "kb_evac", "new_stored"))
        ko_stored = [sem(f"ko_stored{i}") for i in range(3)]
        h2_stored = [sem(f"h2_stored{i}") for i in range(2)]
        bias_ready, sa_done, sa_read, ea_done, wa_ready, wta_done, wta_evac, pva_done, oa_evac = map(
            sem, ("bias_ready", "sa_done", "sa_read", "ea_done", "wa_ready", "wta_done", "wta_evac", "pva_done", "oa_evac"))
        z_half = sem("z_half")
        z_done, lk_ready, p_done, eb_done, at_ready, pvb_done, ob_evac, lk_ln = map(
            sem, ("z_done", "lk_ready", "p_done", "eb_done", "at_ready", "pvb_done", "ob_evac", "lk_ln"))
        os_ready, or_ready, on_ready = map(sem, ("os_ready", "or_ready", "on_ready"))
        wo_done, wo_act, wo_dve, got_done, x1_ready = map(sem, ("wo_done", "wo_act", "wo_dve", "got_done", "x1_ready"))
        logit_done, sc_ready, h2t_done, h2_evac = map(sem, ("logit_done", "sc_ready", "h2t_done", "h2_evac"))
        sg_done, sg_silu, as_ready, sd_done, sd_evac = map(sem, ("sg_done", "sg_silu", "as_ready", "sd_done", "sd_evac"))
        mask_ready, pos_done, start_ready, sidx_ready, slots_init, slots_put, slots_ld, tf_ready, tt_done, idx_ready = map(
            sem, ("mask_ready", "pos_done", "start_ready", "sidx_ready", "slots_init", "slots_put", "slots_ld", "tf_ready",
                  "tt_done", "idx_ready"))
        g2c_ready, g2_mm, g2_ready = map(sem, ("g2c_ready", "g2_mm", "g2_ready"))
        exp_ld = [sem(f"exp_ld{i}") for i in range(4)]
        cur_tok, cur_row, gathered, hgt_done, hgt_ready, gu_done, silu_done, ae_ready, dn_done, yt_ready, yo_done, yo_ready, \
            scattered = map(sem, ("cur_tok", "cur_row", "gathered", "hgt_done", "hgt_ready", "gu_done", "silu_done", "ae_ready",
                                  "dn_done", "yt_ready", "yo_done", "yo_ready", "scattered"))
        gf_ld, yb_ld0, yb_ld1, yb_used, fin_sq, fin_ms, fin_rs, y_ready, y_stored, fin_x, init_ready, sc_clear = map(
            sem, ("gf_ld", "yb_ld0", "yb_ld1", "yb_used", "fin_sq", "fin_ms", "fin_rs", "y_ready", "y_stored", "fin_x", "init_ready", "sc_clear"))
        yb_ld = [yb_ld0, yb_ld1]

        block = ctx.enter_context(nc.Block())

        def kp(w):
            return w.rearrange("(k p) n -> p k n", p=P)

        ada_v, in_v, out_v = kp(w_ada[0]), kp(w_in[0]), kp(w_out[0])
        cols = lambda v, n: v[:, :, 512 * n:512 * n + 512]
        groups = [[(cols(ada_v, n), 0, 512)] for n in range(ADA_FIRST)]
        G_IN = len(groups)
        groups += [[(cols(in_v, n), 0, 512)] for n in range(6)]
        G_ADA = len(groups)
        groups += [[(cols(ada_v, n), 0, 512)] for n in range(ADA_FIRST, 12)]
        G_OUT = len(groups)
        groups += [[(cols(out_v, n), 0, 512)] for n in range(2)]
        G_SH = len(groups)
        groups += [[(kp(w_sg[0]), 0, FE), (kp(w_su[0]), FE, 2 * FE)]]

        def ring_count(g):
            return sum(16 * len(groups[i]) for i in range(g % 3, g + 1, 3))

        def used(g):
            if g < G_IN:
                return mod_mm, g + 1
            if g < G_ADA:
                return proj_done, 5 * (g - G_IN + 1)
            if g < G_OUT:
                return mod_mm, ADA_FIRST + g - G_ADA + 1
            if g < G_SH:
                return wo_done, 5 * (g - G_OUT + 1)
            return sg_done, 5

        KEYS = [P, 2 * P, 3 * P, 4 * P, PAST + TS]
        BOFF = [384, 256, 128, 0, 128]
        UNITS = [(i, h) for i in range(NT) for h in range(HA)]
        ZO = [0, 512, 896, 1152]
        ZW = [512, 384, 256, 128]
        ZS = [(0, 512), (512, 384), (896, 384)]

        def zbank(h, j):
            b = 3 * (h % 2) + min(j, 2)
            o = 256 if j == 3 else 0
            return bank[b][:, o:o + ZW[j]]

        @block.sync
        def _(sp):
            sp.dma_start(SMALL[0:8, :], c_prompt.rearrange("b (k p) -> (b k) p", p=P)).then_inc(small_ld, 16)
            sp.dma_start(SMALL[8:16, :], c_sample.rearrange("b (k p) -> (b k) p", p=P)).then_inc(small_ld, 16)
            sp.dma_start(SMALL[16:64, :], b_ada.rearrange("b (k p) -> (b k) p", p=P)).then_inc(small_ld, 16)
            sp.dma_start(SMALL[64:65, :], g_sub_a).then_inc(small_ld, 16)
            sp.dma_start(SMALL[65:66, 0:DB], g_sub_b).then_inc(small_ld, 16)
            sp.dma_start(SMALL[65:66, DB:P], g_sub_b).then_inc(small_ld, 16)
            sp.dma_start(X[:, 0:4, :], x_prompt[0].rearrange("(t p) d -> p t d", p=P)).then_inc(x_ld, 16)
            sp.dma_start(X[0:TS, 4, :], x_sample[0]).then_inc(x_ld, 16)
            sp.dma_start(LPX[0:1, :], lam_params.rearrange("l a d -> l (a d)")).then_inc(misc_ld, 16)
            sp.dma_start(WR, kp(w_router[0])).then_inc(misc_ld, 16)
            sp.dma_start(BR, b_router.to_broadcast([P, NE])).then_inc(misc_ld, 16)
            for g, parts in enumerate(groups):
                if g == 3:
                    sp.dma_start(CK[:, :, 0:512], cache_a_k[0, 0].rearrange("(j p) h d -> p j (h d)", p=P)).then_inc(ck_ld, 16)
                    sp.dma_start(CK[:, :, 512:D], cache_b_k[0, 0].rearrange("(j p) h d -> p j (h d)", p=P)).then_inc(ck_ld, 16)
                    sp.dma_start(CV[:, :, 0:512], cache_a_v[0, 0].rearrange("(j p) h d -> p j (h d)", p=P)).then_inc(cv_ld, 16)
                    sp.dma_start(CV[:, :, 512:D], cache_b_v[0, 0].rearrange("(j p) h d -> p j (h d)", p=P)).then_inc(cv_ld, 16)
                if g >= 3:
                    sp.wait_ge(*used(g - 3))
                for view, a, b in parts:
                    sp.dma_start(RING[g % 3][:, :, a:b], view).then_inc(ring_ld[g % 3], 16)
            sp.wait_ge(pvb_done, 9)
            sp.dma_start(WSD, w_sd[0].rearrange("(f p) n -> p f n", p=P)).then_inc(wsd_ld, 16)

            def load_expert(e, j):
                sp.dma_start(GU[j][:, :, 0:FE], w_gate[0, bass.ds(e, 1)].rearrange("e (k p) n -> p (e k) n", p=P)).then_inc(exp_ld[j], 16)
                sp.dma_start(GU[j][:, :, FE:2 * FE], w_up[0, bass.ds(e, 1)].rearrange("e (k p) n -> p (e k) n", p=P)).then_inc(exp_ld[j], 16)
                sp.dma_start(DN[j], w_down[0, bass.ds(e, 1)].rearrange("e (f p) n -> p (e f) n", p=P)).then_inc(exp_ld[j], 16)

            sp.wait_ge(tr_done, 27)
            sp.wait_ge(wo_done, 10)
            for j in (0, 1, 3):
                load_expert(j, j)
            sp.wait_ge(*used(G_SH))
            load_expert(2, 2)
            sp.wait_ge(start_ready, 1)
            with sp.Fori(0, NE // 4 - 1) as g:
                e = g * 4
                for j in range(4):
                    done = sp.value_load(START[0:1, bass.ds(e + (j + 1), 1)], min_val=0, max_val=NI)
                    sp.wait_ge(dn_done, done)
                    load_expert(e + (j + 4), j)
            sp.wait_ge(sd_evac, NT)
            sp.dma_start(GF, g_final.rearrange("(a n) -> a n", a=1).to_broadcast([P, D])).then_inc(gf_ld, 16)
            items = sp.value_load(START[0:1, NE:NE + 1], min_val=0, max_val=NI)
            sp.wait_ge(scattered, (items + 2) * 16)
            for t in range(NT):
                if t >= 2:
                    sp.wait_ge(yb_used, t - 1)
                r = ROWS[t]
                sp.dma_start(YB[t % 2][0:r], y_rows[t * P * YK:(t * P + r) * YK, :].rearrange("(p k) d -> p k d", k=YK)[:, 0:TOPK, :]).then_inc(yb_ld[t % 2], 16)
            for t in range(NT):
                sp.wait_ge(y_ready, t + 1)
                r = ROWS[t]
                dst = y_prompt[0, t * P:t * P + P, :] if t < 4 else y_sample[0]
                sp.dma_start(dst, X[0:r, t, :]).then_inc(y_stored, 16)
            sp.wait_ge(y_stored, 16 * NT)

        @block.gpsimd
        def _(pool):
            n = [0]

            def chain(ins):
                n[0] += 1
                ins.then_inc(pool_s, 1)
                pool.wait_ge(pool_s, n[0])

            pool.memset(IDENT, 0.0)
            pool.memset(NTRI, -1.0)
            pool.memset(UP, 1.0)
            pool.memset(NONES, -1.0)
            pool.memset(ONES, 1.0)
            chain(pool.memset(HALF, -0.5))
            pool.affine_select(out=IDENT, in_=IDENT, compare_op=ALU.not_equal, fill=1.0, base=0, pattern=[[-1, P]], channel_multiplier=1)
            pool.affine_select(out=NTRI, in_=NTRI, compare_op=ALU.is_ge, fill=0.0, base=0, pattern=[[-1, P]], channel_multiplier=1)
            pool.affine_select(out=UP, in_=UP, compare_op=ALU.is_gt, fill=0.0, base=0, pattern=[[1, P]], channel_multiplier=-1)
            pool.iota(BIAS[:, 0, :], pattern=[[-1, 512]], base=384, channel_multiplier=1, allow_small_or_imprecise_dtypes=True).then_inc(pool_c, 1)
            pool.wait_ge(ms_ready, 1)
            pool.tensor_tensor(RS, SS, HALF[:, 0, 0:NT], ALU.pow).then_inc(rs_ready, 1)
            for a, (kp_o, ks_o, vp_o, vs_o) in enumerate(((ak_p, ak_s, av_p, av_s), (bk_p, bk_s, bv_p, bv_s))):
                if a == 0:
                    pool.wait_ge(proj_act, 10)
                else:
                    pool.wait_ge(proj_dve, 15)
                c = slice(512 * a, 512 * a + 512)
                pool.dma_start(vp_o[0, 0].rearrange("(t p) h d -> p t (h d)", p=P), V[:, 0:4, c]).then_inc(new_stored, 16)
                pool.dma_start(vs_o[0, 0].rearrange("s h d -> s (h d)"), V[0:TS, 4, c]).then_inc(new_stored, 16)
                for t in range(NT):
                    u = NT * a + t
                    pool.wait_ge(kb_evac, u + 1)
                    dst = kp_o[0, 0, t * P:t * P + P] if t < 4 else ks_o[0, 0]
                    pool.dma_start(dst.rearrange("s h d -> s (h d)"), KO[0:ROWS[t], u % 3, :]).then_inc(ko_stored[u % 3], 16)
            for h in range(HB + 1):
                for s in range(3):
                    pool.wait_ge(eb_done, 3 * h + s + 1)
                    if h < HB:
                        blocks = [ZO[j] for j in ([2, 3], [1], [0])[s]]
                        for o in blocks:
                            v = AT[:, h % 2, o:o + P]
                            last = pool.affine_select(out=v, in_=v, compare_op=ALU.is_gt, fill=0.0, base=0, pattern=[[1, P]], channel_multiplier=-1)
                        last.then_inc(at_ready, 1)
                    elif s == 0:
                        v = AT[0:TS, h % 2, 1024:1536].rearrange("p (h q) -> p h q", q=TS)
                        pool.affine_select(out=v, in_=v, compare_op=ALU.is_gt, fill=0.0, base=0, pattern=[[0, HB], [1, TS]], channel_multiplier=-1).then_inc(at_ready, 1)
            pool.wait_ge(os_ready, 1)
            pool.tensor_tensor(OR, OS, HALF, ALU.pow).then_inc(or_ready, 1)
            for t in range(NT):
                pool.wait_ge(ms_ready, 2 + t)
                pool.tensor_tensor(RS[:, t:t + 1], SS[:, t:t + 1], HALF[:, 0, 0:1], ALU.pow).then_inc(rs_ready, 1)
            pool.wait_ge(tr_done, 27)
            chain(pool.memset(TI[0:IC, :], NONE))
            pool.dma_start(slots.rearrange("(i s) o -> i (s o)", s=SLOT), TI[0:IC, :]).then_inc(slots_init, 16)
            chain(pool.iota(REC, pattern=[[P * YK, NT], [1, 8]], base=0, channel_multiplier=YK))
            pool.wait_ge(slots_init, 16)
            pool.wait_ge(sidx_ready, 1)
            for t in range(NT):
                for k in range(TOPK):
                    r = ROWS[t]
                    pool.indirect_dma_start(slots, bass.IndirectOffsetOnAxis(ap=SIDX[0:r, t, k:k + 1].bitcast(U32), axis=0), REC[0:r, t, k:k + 1], None,
                                            bounds_check=IC * SLOT - 1, oob_is_err=False).then_inc(slots_put, 16)
            pool.wait_ge(slots_put, 16 * NT * TOPK)
            pool.dma_start(TI[0:IC, :], slots.rearrange("(i s) o -> i (s o)", s=SLOT)).then_inc(slots_ld, 16)
            pool.wait_ge(h2_stored[0], 48)
            pool.wait_ge(h2_stored[1], 32)
            chain(pool.memset(HG, 0.0))
            pool.wait_ge(idx_ready, 1)
            items = pool.value_load(START[0:1, NE:NE + 1], min_val=1, max_val=NI)

            def gather(i):
                pool.tensor_copy(ICUR[0:SLOT, 0:1], IDX[0:SLOT, 0, bass.ds(i + 1, 1)] if not isinstance(i, int) else IDX[0:SLOT, 0, i + 1:i + 2]).then_inc(cur_tok, 1)
                pool.wait_ge(cur_tok, i + 1)
                pool.sem_inc(pool_mark)
                pool.indirect_dma_start(HG[0:SLOT, :], None, h2_rows, bass.IndirectOffsetOnAxis(ap=ICUR[0:SLOT, 0:1], axis=0),
                                        bounds_check=T - 1, oob_is_err=False).then_inc(gathered, 16)

            def scatter(i):
                pool.tensor_copy(ICUR[0:SLOT, 1:2], IDX[0:SLOT, 1, bass.ds(i, 1)]).then_inc(cur_row, 1)
                pool.wait_ge(cur_row, i + 1)
                pool.sem_inc(pool_mark)
                pool.indirect_dma_start(y_rows, bass.IndirectOffsetOnAxis(ap=ICUR[0:SLOT, 1:2], axis=0), YO[0:SLOT, :], None,
                                        bounds_check=T * YK - 1, oob_is_err=False).then_inc(scattered, 16)

            gather(0)
            pool.wait_ge(yo_ready, 1)
            pool.indirect_dma_start(y_rows, bass.IndirectOffsetOnAxis(ap=IDX[0:SLOT, 1, 0:1], axis=0), YO[0:SLOT, :], None,
                                    bounds_check=T * YK - 1, oob_is_err=False).then_inc(scattered, 16)
            pool.wait_ge(hgt_done, 1)
            gather(1)
            with pool.Fori(0, items) as i:
                pool.wait_ge(hgt_done, i + 2)
                pool.sem_inc(pool_mark)
                gather(i + 2)
                pool.wait_ge(yo_ready, i + 2)
                pool.sem_inc(pool_mark)
                scatter(i)
            pool.wait_ge(yo_ready, items + 2)
            pool.sem_inc(pool_mark)
            scatter(items)
            pool.wait_ge(gathered, (items + 2) * 16)
            for t in range(NT):
                pool.wait_ge(fin_ms, t + 1)
                pool.tensor_tensor(RS[:, t:t + 1], SS[:, t:t + 1], HALF[:, 0, 0:1], ALU.pow).then_inc(fin_rs, 1)
            pool.wait_ge(new_stored, 64)
            for b, c in enumerate((4, 3, 3)):
                pool.wait_ge(ko_stored[b], 16 * c)

        @block.tensor
        def _(pe):
            def back(src, r, b):
                for k in range(KC):
                    last = pe.transpose(bank[b + k // 4][0:r, (k % 4) * P:(k % 4 + 1) * P], src(k), IDENT)
                return last

            def turn(src, r):
                for k in range(KC):
                    if k >= 4:
                        pe.wait_ge(tr_act if k % 2 else tr_dve, (4 if k % 2 else 5) * r + (k - 4) // 2 + 1)
                    for t in range(4):
                        last = pe.transpose(bank[k % 4][:, t * P:t * P + P], src[:, t, k * P:k * P + P], IDENT)
                    last.then_inc(tr_done, 1)
                for k in range(KC):
                    last = pe.transpose(bank[4][:, k * TS:k * TS + TS], src[0:TS, 4, k * P:k * P + P], IDENT[0:TS, 0:TS])
                last.then_inc(tr_done, 1)

            def turned(r):
                pe.wait_ge(tr_dve, 5 * (r + 1))
                pe.wait_ge(tr_act, 4 * (r + 1))

            def ada(a, g):
                pe.wait_ge(ring_ld[g % 3], ring_count(g))
                if a:
                    pe.wait_ge(mod_ready, a)
                else:
                    pe.wait_ge(c_ready, 1)
                w = RING[g % 3]
                cv = CT.rearrange("p (s k) -> p k s", k=KC)
                for m in range(4):
                    for k in range(KC):
                        last = pe.matmul(bank[6][:, 2 * m:2 * m + 2], w[:, k, m * P:m * P + P], cv[:, k, :], start=(k == 0), stop=(k == KC - 1))
                last.then_inc(mod_mm, 1)

            def wide(w, src, m, prompt, sample, done, last_m):
                for k in range(KC):
                    lw = w[:, k, m * P:m * P + P]
                    a = pe.matmul(prompt, lw, src[:, k, 0:TP], start=(k == 0), stop=(k == KC - 1))
                    b = pe.matmul(sample, lw, src[:, k, TP:T], start=(k == 0), stop=(k == KC - 1))
                a.then_inc(done, 1)
                if m == last_m:
                    b.then_inc(done, 1)
                return b

            pe.wait_ge(pool_c, 1)
            pe.wait_ge(small_ld, 96)
            pe.transpose(bank[7][:, 0:66], SMALL[0:66, :], IDENT[0:66, 0:66]).then_inc(small_t, 1)
            for a in range(ADA_FIRST):
                ada(a, a)
            pe.wait_ge(lam_neg, 1)
            pe.wait_ge(smt_ready, 1)
            pe.matmul(bank[7][:, 0:1], ONES[0:1, :], LAM[0:1, 0:1], start=True, stop=True).then_inc(lam_bc, 1)
            pe.wait_ge(xn_ready, NT)
            turn(XN, 0)
            turned(0)
            for n in range(6):
                g = G_IN + n
                pe.wait_ge(ring_ld[g % 3], ring_count(g))
                w = RING[g % 3]
                for t in range(NT):
                    if n % 3 < 2 and t == 4:
                        continue
                    if n:
                        pe.wait_ge(proj_dve if n % 2 == 0 else proj_act, 5 * ((n - 1) // 2) + t + 1)
                    if n % 3 < 2:
                        if n and t == 0:
                            pe.wait_ge(proj_dve if n % 2 == 0 else proj_act, 5 * ((n - 1) // 2) + 5)
                        wide(w, HT, t, bank[t][:, :], bank[4][:, t * TS:t * TS + TS], proj_done, 3)
                    else:
                        r = ROWS[t]
                        for k in range(KC):
                            last = pe.matmul(bank[t][0:r, :], HT[:, k, t * P:t * P + r], w[:, k, :], start=(k == 0), stop=(k == KC - 1))
                        last.then_inc(proj_done, 1)
                if n % 3 == 2:
                    a = n // 3
                    pe.wait_ge(proj_dve if a == 0 else proj_act, 5 if a == 0 else 15)
                    for t in range(NT):
                        q = NT * a + t
                        if q >= 2:
                            pe.wait_ge(kb_evac, q - 1)
                        else:
                            pe.wait_ge(nlam_ready, 1)
                        b = bank[5 + 2 * (q % 2)]
                        r = ROWS[t]
                        for m in range(4):
                            last = pe.transpose(b[0:r, m * P:m * P + P], KT[:, 4 * a + m, t * P:t * P + r], IDENT)
                        last.then_inc(kb_done, 1)
            pe.wait_ge(ck_ld, 32)
            for j in range(PT):
                for a in range(2):
                    q = 2 * NT + 2 * j + a
                    pe.wait_ge(kb_evac, q - 1)
                    b = bank[5 + 2 * (q % 2)]
                    for m in range(4):
                        last = pe.transpose(b[:, m * P:m * P + P], CK[:, j, 512 * a + m * P:512 * a + m * P + P], IDENT)
                    last.then_inc(kb_done, 1)

            def a_scores(u):
                i, h = UNITS[u]
                r = ROWS[i]
                if u == 0:
                    pe.wait_ge(proj_dve, 15)
                    pe.wait_ge(proj_act, 15)
                if u >= 2:
                    pe.wait_ge(sa_read, 2 * (u - 1))
                if i == 4 and h == 0:
                    pe.wait_ge(kb_evac, 14)
                for m in range(2):
                    b = bank[2 * (u % 2) + m]
                    q = QT[m * DB:m * DB + DB, h, i * P:i * P + r]
                    if i < 4:
                        last = pe.matmul(b[:, 0:KEYS[i]], q, KT[m * DB:m * DB + DB, h, 0:KEYS[i]], start=True, stop=True)
                    else:
                        pe.matmul(b[0:r, 0:PAST], q, CKT[m * DB:m * DB + DB, h, :], start=True, stop=True)
                        last = pe.matmul(b[0:r, PAST:PAST + TS], q, KT[m * DB:m * DB + DB, h, TP:T], start=True, stop=True)
                last.then_inc(sa_done, 1)

            def a_turn(u):
                i, h = UNITS[u]
                r = ROWS[i]
                if u >= 2:
                    pe.wait_ge(wta_evac, u - 1)
                else:
                    pe.wait_ge(kb_evac, 14)
                pe.wait_ge(wa_ready, u + 1)
                for j in range((KEYS[i] + P - 1) // P):
                    w = min(P, KEYS[i] - j * P)
                    last = pe.transpose(bank[4 + u % 2][0:w, j * P:j * P + r], SE[0:r, u % 2, 1, j * P:j * P + w], IDENT[0:r, 0:r])
                last.then_inc(wta_done, 1)

            def a_values(u):
                i, h = UNITS[u]
                r = ROWS[i]
                nj = (KEYS[i] + P - 1) // P
                if u >= 2:
                    pe.wait_ge(oa_evac, u - 1)
                pe.wait_ge(wta_evac, u + 1)
                for j in range(nj):
                    w = min(P, KEYS[i] - j * P)
                    v = V[:, j, h * P:h * P + P] if i < 4 else (CV[:, j, h * P:h * P + P] if j < PT else V[0:TS, 4, h * P:h * P + P])
                    last = pe.matmul(bank[6 + u % 2][0:r, 0:P], WT[0:w, u % 2, j * P:j * P + r], v, start=(j == 0), stop=(j == nj - 1))
                last.then_inc(pva_done, 1)

            pe.wait_ge(cv_ld, 32)
            for u in range(len(UNITS) + 2):
                if u < len(UNITS):
                    a_scores(u)
                if 1 <= u <= len(UNITS):
                    a_turn(u - 1)
                if u >= 2:
                    a_values(u - 2)

            def b_scores(h):
                if h == 0:
                    pe.wait_ge(oa_evac, len(UNITS))
                if h >= 2:
                    pe.wait_ge(eb_done, 3 * (h - 1))
                for j in ((2, 3, 1, 0) if h < HB else (2, 1, 0)):
                    if h < HB:
                        o = h % 2 * DB
                        last = pe.matmul(zbank(h, j), KT[o:o + DB, 4 + h // 2, j * P:j * P + P], QT[o:o + DB, 4 + h // 2, j * P:TP],
                                         start=(j < 3), stop=True, skip_group_check=True)
                        if j != 2:
                            last.then_inc(z_done, 1)
                    else:
                        r = P if j < PT else TS
                        for x, g in enumerate((0, 2, 4, 6, 1, 3, 5, 7)):
                            o = g % 2 * DB
                            if x == 4:
                                last.then_inc(z_half, 1)
                                pe.wait_ge(z_half, 3 - j)
                            k = CKT[o:o + DB, 4 + g // 2, j * P:j * P + P] if j < PT else KT[o:o + DB, 4 + g // 2, TP:T]
                            last = pe.matmul(bank[3 * (h % 2) + j][0:r, g * TS:g * TS + TS], k, QT[o:o + DB, 4 + g // 2, TP:T],
                                             start=(g == 0), stop=True, skip_group_check=True)
                        last.then_inc(z_done, 1)

            def b_sums(h):
                for j in ((3, 2, 1, 0) if h < HB else (2, 1, 0)):
                    s = min(j, 2)
                    pe.wait_ge(lk_ready, 3 * h + 3 - s)
                    if h < HB:
                        out = zbank(h, j)
                        last = pe.matmul(out, NTRI, LK[:, h % 2, ZO[j]:ZO[j] + ZW[j]], start=False, stop=True, skip_group_check=True)
                        for l in range(j + 1, 4):
                            last = pe.matmul(out[:, (l - j) * P:ZW[j]], NONES, LK[:, h % 2, ZO[l]:ZO[l] + ZW[l]], start=False, stop=True, skip_group_check=True)
                        if j != 3:
                            last.then_inc(p_done, 1)
                    else:
                        r = P if j < PT else TS
                        out = bank[3 * (h % 2) + j][0:r, :]
                        last = pe.matmul(out, NTRI[0:r, 0:r], LK[0:r, h % 2, j * 512:j * 512 + 512], start=False, stop=True, skip_group_check=True)
                        for l in range(j + 1, 3):
                            rl = P if l < PT else TS
                            last = pe.matmul(out, NONES[0:rl, 0:r], LK[0:rl, h % 2, l * 512:l * 512 + 512], start=False, stop=True, skip_group_check=True)
                        last.then_inc(p_done, 1)

            def b_values(h):
                if h >= 1:
                    pe.wait_ge(ob_evac, h)
                pe.wait_ge(at_ready, 3 * h + 3 if h < HB else 3 * HB + 1)
                if h < HB:
                    for i in range(4):
                        for j in range(i + 1):
                            o = ZO[j] + (i - j) * P
                            last = pe.matmul(bank[7][:, i * DB:i * DB + DB], AT[:, h % 2, o:o + P], V[:, j, 512 + h * DB:512 + h * DB + DB],
                                             start=(j == 0), stop=(j == i))
                else:
                    pe.wait_ge(eb_done, 3 * HB + 3)
                    for g in range(HB):
                        c = slice(512 + g * DB, 512 + g * DB + DB)
                        for j in range(3):
                            r = P if j < PT else TS
                            v = CV[:, j, c] if j < PT else V[0:TS, 4, c]
                            last = pe.matmul(bank[7][0:TS, g * DB:g * DB + DB], AT[0:r, h % 2, j * 512 + g * TS:j * 512 + g * TS + TS], v,
                                             start=(j == 0), stop=(j == 2))
                last.then_inc(pvb_done, 1)

            for h in range(HB + 3):
                if h < HB:
                    if h == 0:
                        pe.wait_ge(oa_evac, len(UNITS))
                    ada(ADA_FIRST + h, G_ADA + h)
                if h <= HB:
                    b_scores(h)
                if h >= 2:
                    b_values(h - 2)
                if 1 <= h <= HB + 1:
                    b_sums(h - 1)

            pe.wait_ge(on_ready, NT)
            turn(OA, 1)
            turned(1)
            for m in range(8):
                g = G_OUT + m // 4
                if m % 4 == 0:
                    pe.wait_ge(ring_ld[g % 3], ring_count(g))
                if m >= 4:
                    pe.wait_ge(wo_act, m - 3)
                wide(RING[g % 3], OT, m % 4, bank[m % 4][:, :], bank[4 + m // 4][:, (m % 4) * TS:(m % 4) * TS + TS], wo_done, 3)
            pe.wait_ge(wo_act, 8)
            pe.wait_ge(wo_dve, 2)
            for t in range(NT):
                if t >= 2:
                    pe.wait_ge(x1_ready, t - 1)
                r = ROWS[t]
                back(lambda k: GO[:, k, t * P:t * P + r], r, 6 if t % 2 == 0 else 0).then_inc(got_done, 1)
            pe.wait_ge(xn_ready, 2 * NT)
            turn(XN, 2)
            turned(2)
            pe.wait_ge(misc_ld, 48)
            for t in range(NT):
                r = ROWS[t]
                for k in range(KC):
                    last = pe.matmul(bank[5][0:r, t * NE:t * NE + NE], HT[:, k, t * P:t * P + r], WR[:, k, :], start=(k == 0), stop=(k == KC - 1))
            last.then_inc(logit_done, 1)
            for t in range(NT):
                if t >= 2:
                    pe.wait_ge(h2_evac, t - 1)
                r = ROWS[t]
                back(lambda k: HT[:, k, t * P:t * P + r], r, 6 if t % 2 == 0 else 0).then_inc(h2t_done, 1)
            pe.wait_ge(ring_ld[G_SH % 3], ring_count(G_SH))
            pe.wait_ge(h2_evac, NT)
            for m in range(4):
                wide(RING[G_SH % 3], HT, m, bank[m][:, :], bank[4][:, m * TS:m * TS + TS], sg_done, 3)
            pe.wait_ge(mask_ready, 1)
            for t in range(NT):
                pe.matmul(bank[6][:, t * NE:t * NE + NE], UP, M[:, t, :], start=True, stop=(t == 0))
                for l in range(t):
                    pe.matmul(bank[6][:, t * NE:t * NE + NE], ONES, M[:, l, :], start=False, stop=(l == t - 1))
            for t in range(NT):
                last = pe.matmul(bank[7][:, 0:NE], ONES, M[:, t, :], start=(t == 0), stop=(t == NT - 1))
            last.then_inc(pos_done, 1)
            pe.wait_ge(wsd_ld, 16)
            pe.wait_ge(as_ready, 1)
            for t in range(NT):
                if t >= 2:
                    pe.wait_ge(sd_evac, t - 1)
                r = ROWS[t]
                for n in range(2):
                    for f in range(2):
                        last = pe.matmul(bank[2 * (t % 2) + n][0:r, :], AS[:, f, t * P:t * P + r], WSD[:, f, 512 * n:512 * n + 512], start=(f == 0), stop=(f == 1))
                last.then_inc(sd_done, 1)
            pe.wait_ge(sd_evac, NT)
            for s in range(2):
                pe.wait_ge(g2c_ready, s + 1)
                for k in range(KC):
                    last = pe.matmul(bank[2 * s + k // 4][:, (k % 4) * P:(k % 4 + 1) * P], G2C[s][:, k, :], IDENT, start=True, stop=True)
                last.then_inc(g2_mm, 1)
            pe.wait_ge(tf_ready, 1)
            pe.transpose(bank[7][0:SLOT, 0:IC], TF[0:IC, :], IDENT[0:IC, 0:IC]).then_inc(tt_done, 1)

            def turn_in():
                for k in range(KC):
                    last = pe.transpose(bank[1][:, k * SLOT:k * SLOT + SLOT], HG[0:SLOT, k * P:k * P + P], IDENT[0:SLOT, 0:SLOT])
                last.then_inc(hgt_done, 1)

            def turn_out():
                for k in range(KC):
                    last = pe.transpose(bank[2 + k // 4][0:SLOT, (k % 4) * P:(k % 4 + 1) * P], YT[:, k, :], IDENT)
                last.then_inc(yo_done, 1)

            pe.wait_ge(g2_ready, 2)
            pe.wait_ge(gathered, 16)
            turn_in()
            pe.wait_ge(yt_ready, 1)
            with pe.Fori(0, NE // 4) as g:
                e = g * 4
                for j in range(4):
                    lo = pe.value_load(START[0:1, bass.ds(e + j, 1)], min_val=0, max_val=NI - 1)
                    hi = pe.value_load(START[0:1, bass.ds(e + (j + 1), 1)], min_val=1, max_val=NI)
                    with pe.Fori(lo, hi) as i:
                        pe.wait_ge(exp_ld[j], (g + 1) * 48)
                        pe.wait_ge(hgt_ready, i + 1)
                        for m in range(4):
                            for k in range(KC):
                                last = pe.matmul(bank[0][:, m * SLOT:m * SLOT + SLOT], GU[j][:, k, m * P:m * P + P], HGT[:, k, :], start=(k == 0), stop=(k == KC - 1))
                        last.then_inc(gu_done, 1)
                        pe.wait_ge(gathered, (i + 2) * 16)
                        pe.sem_inc(pe_mark)
                        turn_in()
                        pe.wait_ge(yt_ready, i + 1)
                        pe.wait_ge(yo_ready, i + 1)
                        pe.sem_inc(pe_mark)
                        turn_out()
                        pe.wait_ge(ae_ready, i + 2)
                        for k in range(KC):
                            for f in range(2):
                                last = pe.matmul(bank[4][:, k * SLOT:k * SLOT + SLOT], DN[j][:, f, k * P:k * P + P], AE[:, f, :], start=(f == 0), stop=(f == 1))
                        last.then_inc(dn_done, 1)
            items = pe.value_load(START[0:1, NE:NE + 1], min_val=1, max_val=NI)
            pe.wait_ge(yt_ready, items + 1)
            pe.wait_ge(yo_ready, items + 1)
            pe.sem_inc(pe_mark)
            turn_out()

        @block.scalar
        def _(act):
            n = [0]

            def chain(ins):
                n[0] += 1
                ins.then_inc(act_s, 1)
                act.wait_ge(act_s, n[0])

            def squares(t, junk, done, before):
                r = ROWS[t]
                act.wait_ge(done, before)
                act.activation(at(junk, D)[0:r, :], X[0:r, t, :], ACT.Square, accum_out=SS[0:r, t:t + 1]).then_inc(done, 1)

            def turned(r, dst, scale, shift):
                for k in range(1, KC, 2):
                    act.wait_ge(tr_done, 9 * r + k + 1)
                    act.activation(dst[:, k, 0:TP], bank[k % 4][:, :], ACT.Identity, scale=scale(k), bias=shift(k) if shift else 0.0).then_inc(tr_act, 1)

            act.wait_ge(x_ld, 32)
            act.wait_ge(init_ready, 1)
            for t in range(NT):
                squares(t, a_tmp + 5632, sq_done, t)
            act.wait_ge(smt_ready, 1)
            act.activation(CT, SMT[:, 0:16], ACT.Silu).then_inc(c_ready, 1)
            act.wait_ge(lam_sum, 1)
            act.activation(LAM[0:1, :], LAM[0:1, :], ACT.Exp).then_inc(lam_exp, 1)
            act.wait_ge(mod_ready, ADA_FIRST)
            turned(0, HT, lambda k: MOD[:, 8 + k, 0:1], lambda k: MOD[:, k, 0:1])

            def keys_out(q):
                act.wait_ge(kb_done, q + 1)
                b = bank[5 + 2 * (q % 2)]
                if q < 2 * NT:
                    if q >= 3:
                        act.wait_ge(ko_stored[q % 3], 16 * (q // 3))
                    r = ROWS[q % NT]
                    act.copy(KO[0:r, q % 3, :], b[0:r, :]).then_inc(kb_evac, 1)
                else:
                    j, a = divmod(q - 2 * NT, 2)
                    act.copy(CKT[:, 4 * a:4 * a + 4, j * P:j * P + P], b.rearrange("p (m c) -> p m c", c=P)).then_inc(kb_evac, 1)

            for n_g in (0, 2, 4):
                for t in range(NT):
                    act.wait_ge(proj_done, 5 * n_g + t + 1)
                    if n_g == 2:
                        r = ROWS[t]
                        ins = act.copy(V[0:r, t, 0:512], bank[t][0:r, :])
                    else:
                        dst, scale = (QT[:, 0:4], -DB ** -0.5) if n_g == 0 else (KT[:, 4:8], 1.0)
                        if t < 4:
                            ins = act.activation(dst[:, t, 0:TP], bank[t][:, :], ACT.Copy, scale=scale)
                        else:
                            ins = act.activation(dst[:, :, TP:T], bank[4][:, 0:256].rearrange("p (m c) -> p m c", c=TS), ACT.Copy, scale=scale)
                    ins.then_inc(proj_act, 1)
                if n_g == 2:
                    for q in range(NT):
                        keys_out(q)
            for q in range(NT, 2 * NT + 4):
                keys_out(q)

            def a_exp(u):
                i, h = UNITS[u]
                r = ROWS[i]
                for m in range(2):
                    act.wait_ge(sa_read, 2 * u + m + 1)
                    s = SE[0:r, u % 2, m, 0:KEYS[i]]
                    act.activation(s, s, ACT.Exp, scale=-1.0, bias=MINS[0:r, u % 2, m:m + 1], accum_out=SUMS[0:r, i, h, m:m + 1]).then_inc(ea_done, 1)

            def a_turned(u):
                i, h = UNITS[u]
                act.wait_ge(wta_done, u + 1)
                if u >= 2:
                    act.wait_ge(pva_done, u - 1)
                b = bank[4 + u % 2]
                if i < 4:
                    act.copy(WT[:, u % 2, 0:KEYS[i]], b[:, 0:KEYS[i]]).then_inc(wta_evac, 1)
                else:
                    for j in range(3):
                        w = P if j < PT else TS
                        ins = act.copy(WT[0:w, u % 2, j * P:j * P + TS], b[0:w, j * P:j * P + TS])
                    ins.then_inc(wta_evac, 1)

            def a_out(u):
                i, h = UNITS[u]
                r = ROWS[i]
                act.wait_ge(pva_done, u + 1)
                act.copy(OA[0:r, i, h * P:h * P + P], bank[6 + u % 2][0:r, 0:P]).then_inc(oa_evac, 1)

            for u in range(len(UNITS) + 2):
                if u < len(UNITS):
                    a_exp(u)
                if 1 <= u <= len(UNITS):
                    a_turned(u - 1)
                if u >= 2:
                    a_out(u - 2)

            def b_part(h, s):
                if h < HB:
                    return P, ZS[s][0], ZS[s][1], bank[3 * (h % 2) + s]
                return P if s < PT else TS, s * 512, 512, bank[3 * (h % 2) + s]

            for b, c in enumerate((4, 3, 3)):
                act.wait_ge(ko_stored[b], 16 * c)

            def b_log(h):
                for x, s in enumerate((2, 1, 0)):
                    r, o, w, b = b_part(h, s)
                    v = LK[0:r, h % 2, o:o + w]
                    act.wait_ge(z_done, 3 * h + x + 1)
                    if h >= 2 and x == 0:
                        act.wait_ge(p_done, 3 * (h - 1))
                    chain(act.activation(v, b[0:r, 0:w], ACT.Abs))
                    chain(act.activation(v, v, ACT.Exp, scale=-1.0))
                    act.activation(v, v, ACT.Ln, bias=1.0).then_inc(lk_ln, 1)

            def b_exp(h):
                for x, s in enumerate((2, 1, 0)):
                    r, o, w, b = b_part(h, s)
                    act.wait_ge(p_done, 3 * h + x + 1)
                    if h >= 2 and x == 0:
                        act.wait_ge(pvb_done, h - 1)
                    act.activation(AT[0:r, h % 2, o:o + w], b[0:r, 0:w], ACT.Exp).then_inc(eb_done, 1)

            def b_out(h):
                act.wait_ge(pvb_done, h + 1)
                if h < HB:
                    act.copy(OA[:, 0:4, 512 + h * DB:512 + h * DB + DB], bank[7][:, 0:4 * DB].rearrange("p (t d) -> p t d", d=DB)).then_inc(ob_evac, 1)
                else:
                    act.copy(OA[0:TS, 4, 512:D], bank[7][0:TS, :]).then_inc(ob_evac, 1)

            for h in range(HB + 3):
                if h <= HB:
                    b_log(h)
                if h >= 2:
                    b_out(h - 2)
                if 1 <= h <= HB + 1:
                    b_exp(h - 1)

            turned(1, OT, lambda k: GA[:, k // 4:k // 4 + 1], None)
            for m in range(8):
                act.wait_ge(wo_done, m + m // 4 + 1)
                act.activation(GO[:, m, 0:TP], bank[m % 4][:, :], ACT.Identity, scale=MOD[:, 16 + m, 0:1]).then_inc(wo_act, 1)
            for t in range(NT):
                act.wait_ge(x1_ready, t + 1)
                squares(t, a_tmp + 2048, sq_done, NT + t)
            turned(2, HT, lambda k: MOD[:, 32 + k, 0:1], lambda k: MOD[:, 24 + k, 0:1])
            act.wait_ge(logit_done, 1)
            act.wait_ge(sc_clear, 1)
            act.activation(SC[:, 0:4, :], bank[5][:, 0:4 * NE].rearrange("p (t e) -> p t e", e=NE), ACT.Sigmoid)
            act.activation(SC[0:TS, 4, :], bank[5][0:TS, 4 * NE:NT * NE], ACT.Sigmoid).then_inc(sc_ready, 1)
            for t in range(NT):
                r = ROWS[t]
                b = 6 if t % 2 == 0 else 0
                act.wait_ge(h2t_done, t + 1)
                if t >= 2:
                    act.wait_ge(h2_stored[t % 2], 16 * (t // 2))
                act.copy(H2S[0:r, t % 2, 0:512], bank[b][0:r, :])
                act.copy(H2S[0:r, t % 2, 512:D], bank[b + 1][0:r, :]).then_inc(h2_evac, 1)
                act.wait_ge(h2_evac, t + 1)
                act.dma_start(h2_rows[t * P:t * P + r, :], H2S[0:r, t % 2, :]).then_inc(h2_stored[t % 2], 16)
            for m in range(2):
                act.wait_ge(sg_done, m + 1)
                act.activation(SG[:, m, 0:TP], bank[m][:, :], ACT.Silu).then_inc(sg_silu, 1)
            act.wait_ge(sg_done, 5)
            act.activation(SG[:, :, TP:T], bank[4][:, 0:2 * TS].rearrange("p (m c) -> p m c", c=TS), ACT.Silu).then_inc(sg_silu, 1)
            for t in range(NT):
                r = ROWS[t]
                act.wait_ge(sd_done, t + 1)
                act.copy(YA[0:r, t, 0:512], bank[2 * (t % 2)][0:r, :])
                act.copy(YA[0:r, t, 512:D], bank[2 * (t % 2) + 1][0:r, :]).then_inc(sd_evac, 1)
            act.wait_ge(yo_ready, 1)
            act.copy(YT[:, 0, 0:1], YT[:, 0, 0:1]).then_inc(yt_ready, 1)
            items = act.value_load(START[0:1, NE:NE + 1], min_val=1, max_val=NI)
            with act.Fori(0, items) as i:
                act.wait_ge(gu_done, i + 1)
                act.wait_ge(ae_ready, i + 1)
                act.activation(SI, bank[0][:, 0:2 * SLOT], ACT.Silu).then_inc(silu_done, 1)
                act.wait_ge(dn_done, i + 1)
                act.copy(YT.rearrange("p k s -> p (k s)"), bank[4][:, :]).then_inc(yt_ready, 1)
            for t in range(NT):
                act.wait_ge(fin_x, t + 1)
                squares(t, a_tmp, fin_sq, t)

        @block.vector
        def _(dve):
            n = [0]

            def chain(ins):
                n[0] += 1
                ins.then_inc(dve_s, 1)
                dve.wait_ge(dve_s, n[0])

            def mod(a):
                dve.wait_ge(mod_mm, a + 1)
                dve.scalar_tensor_tensor(out=MOD[:, 4 * a:4 * a + 4, :], in0=bank[6][:, 0:8].rearrange("p (m s) -> p m s", s=2),
                                         scalar=1.0 if a in (2, 3, 8, 9) else 0.0,
                                         in1=SMT[:, 16 + 4 * a:20 + 4 * a].unsqueeze(2).to_broadcast([P, 4, 2]), op0=ALU.add, op1=ALU.add).then_inc(mod_ready, 1)

            def means(t0, t1):
                dve.tensor_scalar(SS[:, t0:t1], SS[:, t0:t1], 1.0 / D, EPS, ALU.mult, ALU.add).then_inc(ms_ready, 1)

            def norm(t):
                r = ROWS[t]
                dve.tensor_scalar(XN[0:r, t, :], X[0:r, t, :], RS[0:r, t:t + 1], None, ALU.mult).then_inc(xn_ready, 1)

            def turned(r, dst, scale, shift):
                for k in range(0, KC, 2):
                    dve.wait_ge(tr_done, 9 * r + k + 1)
                    if shift:
                        dve.tensor_scalar(dst[:, k, 0:TP], bank[k % 4][:, :], scale(k, 0), shift(k, 0), ALU.mult, ALU.add).then_inc(tr_dve, 1)
                    else:
                        dve.tensor_scalar(dst[:, k, 0:TP], bank[k % 4][:, :], scale(k, 0), None, ALU.mult).then_inc(tr_dve, 1)
                dve.wait_ge(tr_done, 9 * r + 9)
                for k in range(KC):
                    b = bank[4][:, k * TS:k * TS + TS]
                    if shift:
                        ins = dve.tensor_scalar(dst[:, k, TP:T], b, scale(k, 1), shift(k, 1), ALU.mult, ALU.add)
                    else:
                        ins = dve.tensor_scalar(dst[:, k, TP:T], b, scale(k, 1), None, ALU.mult)
                ins.then_inc(tr_dve, 1)

            dve.memset(SUMS, 1.0)
            dve.memset(OS, 1.0)
            dve.memset(SS, 1.0).then_inc(init_ready, 1)
            dve.wait_ge(small_t, 1)
            dve.tensor_copy(SMT, bank[7][:, 0:66]).then_inc(smt_ready, 1)
            dve.wait_ge(misc_ld, 48)
            lp = LPX[0:1, :].rearrange("o (a b d) -> o a b d", b=2, d=DB)
            lm = LPM[0:1, :].rearrange("o (a d) -> o a d", d=DB)
            chain(dve.tensor_tensor(lm, lp[:, :, 0, :], lp[:, :, 1, :], ALU.mult))
            dve.tensor_reduce(LAM[0:1, :], lm, AX, ALU.add).then_inc(lam_sum, 1)
            dve.wait_ge(smt_ready, 1)
            dve.tensor_scalar(GA[:, 0:1], SMT[:, 64:65], 1.0 - LAM0, None, ALU.mult)
            dve.tensor_copy(GA[:, 1:2], SMT[:, 65:66])
            dve.wait_ge(pool_c, 1)
            chain(dve.scalar_tensor_tensor(out=BIAS[:, 0, :], in0=BIAS[:, 0, :], scalar=-1.0, in1=BIAS[:, 0, :], op0=ALU.mult, op1=ALU.max))
            for h in (1, 2, 3):
                ins = dve.tensor_scalar(BIAS[:, h, :], BIAS[:, 0, :], 2.0 ** (-8.0 * (h + 1) / HA), None, ALU.mult)
            chain(ins)
            chain(dve.tensor_scalar(BIAS[:, 0, :], BIAS[:, 0, :], 2.0 ** (-8.0 / HA), None, ALU.mult))
            chain(dve.memset(BIAS[0:DB, :, 448:512], BIG))
            dve.wait_ge(sq_done, NT)
            means(0, NT)
            dve.wait_ge(rs_ready, 1)
            for t in range(NT):
                norm(t)
            dve.wait_ge(lam_exp, 1)
            chain(dve.tensor_scalar(LAM[0:1, 1:2], LAM[0:1, 1:2], LAM0, None, ALU.subtract))
            dve.tensor_tensor(LAM[0:1, 0:1], LAM[0:1, 1:2], LAM[0:1, 0:1], ALU.subtract).then_inc(lam_neg, 1)
            for a in range(ADA_FIRST):
                mod(a)
            dve.wait_ge(lam_bc, 1)
            dve.tensor_copy(NLAM, bank[7][:, 0:1]).then_inc(nlam_ready, 1)
            dve.wait_ge(mod_ready, ADA_FIRST)
            turned(0, HT, lambda k, s: MOD[:, 8 + k, s:s + 1], lambda k, s: MOD[:, k, s:s + 1])

            for n_g in (1, 3, 5):
                for t in range(NT):
                    dve.wait_ge(proj_done, 5 * n_g + t + 1)
                    if n_g == 5:
                        r = ROWS[t]
                        ins = dve.tensor_copy(V[0:r, t, 512:D], bank[t][0:r, :])
                    else:
                        dst, scale = (QT[:, 4:8], DB ** -0.5) if n_g == 3 else (KT[:, 0:4], 1.0)
                        if t < 4:
                            ins = dve.tensor_scalar(dst[:, t, 0:TP], bank[t][:, :], scale, None, ALU.mult)
                        else:
                            ins = dve.tensor_scalar(dst[:, :, TP:T], bank[4][:, 0:256].rearrange("p (m c) -> p m c", c=TS), scale, None, ALU.mult)
                    ins.then_inc(proj_dve, 1)

            def a_read(u):
                i, h = UNITS[u]
                r, k = ROWS[i], KEYS[i]
                dve.wait_ge(sa_done, u + 1)
                if u >= 2:
                    dve.wait_ge(wta_done, u - 1)
                for m in range(2):
                    dve.tensor_tensor_reduce(SE[0:r, u % 2, m, 0:k], BIAS[0:r, h, BOFF[i]:BOFF[i] + k], bank[2 * (u % 2) + m][0:r, 0:k], 1.0, 3e38,
                                             ALU.add, ALU.min, MINS[0:r, u % 2, m:m + 1]).then_inc(sa_read, 1)

            def a_weights(u):
                i, h = UNITS[u]
                r, k = ROWS[i], KEYS[i]
                dve.wait_ge(ea_done, 2 * u + 2)
                co = CO[0:r, u % 2, :]
                chain(dve.reciprocal(co, SUMS[0:r, i, h, 1:2]))
                chain(dve.tensor_scalar(co, co, SUMS[0:r, i, h, 0:1], NLAM[0:r, :], ALU.mult, ALU.mult))
                dve.scalar_tensor_tensor(out=SE[0:r, u % 2, 1, 0:k], in0=SE[0:r, u % 2, 1, 0:k], scalar=co, in1=SE[0:r, u % 2, 0, 0:k],
                                         op0=ALU.mult, op1=ALU.add).then_inc(wa_ready, 1)

            for u in range(len(UNITS) + 1):
                if u < len(UNITS):
                    a_read(u)
                if u >= 1:
                    a_weights(u - 1)

            def b_part(h, s):
                if h < HB:
                    return P, ZS[s][0], ZS[s][1], bank[3 * (h % 2) + s]
                return P if s < PT else TS, s * 512, 512, bank[3 * (h % 2) + s]

            def b_keep(h):
                for x, s in enumerate((2, 1, 0)):
                    r, o, w, b = b_part(h, s)
                    v = LK[0:r, h % 2, o:o + w]
                    dve.wait_ge(lk_ln, 3 * h + x + 1)
                    ins = dve.scalar_tensor_tensor(out=v, in0=b[0:r, 0:w], scalar=0.0, in1=v, op0=ALU.max, op1=ALU.add)
                    if h < HB:
                        chain(ins)
                        for c in [ZO[j] for j in ([0], [1], [2, 3])[s]]:
                            d = LK[:, h % 2, c:c + P]
                            ins = dve.tensor_tensor(d, d, UP, ALU.mult)
                    elif s == 2:
                        chain(ins)
                        d = v.rearrange("p (h q) -> p h q", q=TS)
                        ins = dve.tensor_tensor(d, d, UP[0:TS, 0:TS].unsqueeze(1).to_broadcast([TS, HB, TS]), ALU.mult)
                    ins.then_inc(lk_ready, 1)

            for h in range(HB + 1):
                if h < HB:
                    mod(ADA_FIRST + h)
                b_keep(h)

            dve.wait_ge(ob_evac, HB + 1)
            dve.wait_ge(oa_evac, len(UNITS))
            for t in range(NT):
                r = ROWS[t]
                sq = SQ[0:r, t % 2, :]
                chain(dve.tensor_tensor(sq, OA[0:r, t, :], OA[0:r, t, :], ALU.mult))
                dve.tensor_reduce(OS[0:r, t, 0:HA], sq[:, 0:512].rearrange("p (h d) -> p h d", d=P), AX, ALU.add)
                last = dve.tensor_reduce(OS[0:r, t, HA:12], sq[:, 512:D].rearrange("p (h d) -> p h d", d=DB), AX, ALU.add)
            chain(last)
            s0 = SUMS[:, :, :, 0]
            chain(dve.scalar_tensor_tensor(out=s0, in0=s0, scalar=EPS * P, in1=s0, op0=ALU.mult, op1=ALU.mult))
            chain(dve.tensor_tensor(OS[:, :, 0:HA], OS[:, :, 0:HA], s0, ALU.add))
            dve.tensor_scalar(OS[:, :, 0:HA], OS[:, :, 0:HA], 1.0 / P, None, ALU.mult)
            dve.tensor_scalar(OS[:, :, HA:12], OS[:, :, HA:12], 1.0 / DB, EPS, ALU.mult, ALU.add).then_inc(os_ready, 1)
            dve.wait_ge(or_ready, 1)
            for t in range(NT):
                r = ROWS[t]
                a = OA[0:r, t, 0:512].rearrange("p (h d) -> p h d", d=P)
                b = OA[0:r, t, 512:D].rearrange("p (h d) -> p h d", d=DB)
                dve.tensor_tensor(a, a, OR[0:r, t, 0:HA].unsqueeze(2).to_broadcast([r, HA, P]), ALU.mult)
                dve.tensor_tensor(b, b, OR[0:r, t, HA:12].unsqueeze(2).to_broadcast([r, HB, DB]), ALU.mult).then_inc(on_ready, 1)
            turned(1, OT, lambda k, s: GA[:, k // 4:k // 4 + 1], None)
            for g in range(2):
                dve.wait_ge(wo_done, 5 * g + 5)
                dve.tensor_tensor(GO[:, 4 * g:4 * g + 4, TP:T], bank[4 + g][:, 0:256].rearrange("p (m c) -> p m c", c=TS),
                                  MOD[:, 16 + 4 * g:20 + 4 * g, 1:2].to_broadcast([P, 4, TS]), ALU.mult).then_inc(wo_dve, 1)
            dve.wait_ge(new_stored, 64)
            for t in range(NT):
                r = ROWS[t]
                b = 6 if t % 2 == 0 else 0
                dve.wait_ge(got_done, t + 1)
                dve.tensor_tensor(X[0:r, t, 0:512], bank[b][0:r, :], X[0:r, t, 0:512], ALU.add)
                dve.tensor_tensor(X[0:r, t, 512:D], bank[b + 1][0:r, :], X[0:r, t, 512:D], ALU.add).then_inc(x1_ready, 1)
                if t >= 1:
                    dve.wait_ge(sq_done, NT + t)
                    means(t - 1, t)
                    dve.wait_ge(rs_ready, 1 + t)
                    norm(t - 1)
            dve.wait_ge(sq_done, 2 * NT)
            means(4, 5)
            dve.wait_ge(rs_ready, 1 + NT)
            norm(4)
            turned(2, HT, lambda k, s: MOD[:, 32 + k, s:s + 1], lambda k, s: MOD[:, 24 + k, s:s + 1])

            dve.wait_ge(logit_done, 1)
            dve.memset(GS, -3e38)
            dve.memset(GREP, -3e38)
            dve.memset(SELX, -3e38)
            dve.memset(EREP, -3e38)
            dve.memset(SC, 0.5).then_inc(sc_clear, 1)
            dve.wait_ge(sc_ready, 1)
            chain(dve.tensor_tensor(SEL, SC, BR.unsqueeze(1).to_broadcast([P, NT, NE]), ALU.add))
            for t in range(NT):
                for g in range(NG):
                    last = dve.max(G8[:, t * NG + g, :], SEL[:, t, g * EG:g * EG + EG])
            chain(last)
            g8 = G8.rearrange("p (t g) e -> p t g e", g=NG)
            chain(dve.tensor_tensor(GS[:, :, 0:NG], g8[:, :, :, 0], g8[:, :, :, 1], ALU.add))
            for t in range(NT):
                last = dve.max(GTOP[:, t, :], GS[:, t, :])
            chain(last)
            chain(dve.tensor_copy(GREP[:, :, 0:TOPG], GTOP[:, :, 0:TOPG]))
            for t in range(NT):
                last = dve.match_replace(GOUT[:, t, :], GREP[:, t, :], GS[:, t, :], 3e38)
            chain(last)
            chain(dve.tensor_scalar(KEEP, GOUT[:, :, 0:NG], 3e38, None, ALU.is_equal))
            chain(dve.tensor_scalar(NEGK, KEEP, 1.0, BIG, ALU.subtract, ALU.mult))
            for t in range(NT):
                v = SELX[:, t, 0:NE].rearrange("p (g e) -> p g e", e=EG)
                last = dve.tensor_tensor(v, SEL[:, t, :].rearrange("p (g e) -> p g e", e=EG), KEEP[:, t, :].unsqueeze(2).to_broadcast([P, NG, EG]), ALU.mult)
            chain(last)
            for t in range(NT):
                v = SELX[:, t, 0:NE].rearrange("p (g e) -> p g e", e=EG)
                last = dve.tensor_tensor(v, v, NEGK[:, t, :].unsqueeze(2).to_broadcast([P, NG, EG]), ALU.add)
            chain(last)
            for t in range(NT):
                last = dve.max(ETOP[:, t, :], SELX[:, t, :])
            chain(last)
            chain(dve.tensor_copy(EREP[:, :, 0:TOPK], ETOP[:, :, 0:TOPK]))
            for t in range(NT):
                last = dve.match_replace(EOUT[:, t, :], EREP[:, t, :], SELX[:, t, :], 3e38)
            chain(last)
            chain(dve.tensor_scalar(M, EOUT[:, :, 0:NE], 3e38, None, ALU.is_equal))
            dve.memset(M[DB:P, 4, :], 0.0).then_inc(mask_ready, 1)
            for f in range(2):
                dve.wait_ge(sg_silu, f + 1)
                dve.wait_ge(sg_done, 3 + f)
                dve.tensor_tensor(AS[:, f, 0:TP], SG[:, f, 0:TP], bank[2 + f][:, :], ALU.mult)
            dve.wait_ge(sg_silu, 3)
            dve.tensor_tensor(AS[:, :, TP:T], SG[:, :, TP:T], bank[4][:, 2 * TS:4 * TS].rearrange("p (m c) -> p m c", c=TS), ALU.mult).then_inc(as_ready, 1)
            dve.wait_ge(pos_done, 1)
            chain(dve.tensor_scalar(NB_I, bank[7][:, 0:NE], float(SLOT - 1), None, ALU.add))
            chain(dve.tensor_scalar(NB_J, NB_I, 6, None, ALU.logical_shift_right))
            dve.memset(ZE, 0.0)
            chain(dve.tensor_scalar(NB, NB_J, 1.0, None, ALU.max))
            chain(dve.tensor_tensor_scan(INC, NB, ZE, 0.0, ALU.add, ALU.add))
            chain(dve.tensor_tensor(STF[:, 0:NE], INC, NB, ALU.subtract))
            chain(dve.tensor_copy(STF[:, NE:NE + 1], INC[:, NE - 1:NE]))
            dve.tensor_copy(START[:, 0:NE + 1], STF[:, 0:NE + 1]).then_inc(start_ready, 1)
            chain(dve.tensor_scalar(SB, STF[:, 0:NE], float(SLOT), float(SLOT + 1), ALU.mult, ALU.add))
            chain(dve.tensor_tensor(SL, bank[6][:, 0:NT * NE].rearrange("p (t e) -> p t e", e=NE), SB.unsqueeze(1).to_broadcast([P, NT, NE]), ALU.add))
            chain(dve.tensor_tensor(SL, SL, M, ALU.mult))
            for t in range(NT):
                last = dve.max(S8[:, t, :], SL[:, t, :])
            chain(last)
            dve.tensor_scalar(SIDX, S8, 1.0, None, ALU.subtract).then_inc(sidx_ready, 1)
            for s in range(2):
                dve.tensor_copy(G2C[s], MOD[:, 40:48, s:s + 1].to_broadcast([P, KC, P])).then_inc(g2c_ready, 1)
            chain(dve.tensor_tensor(COMB, SC, M, ALU.mult))
            chain(dve.tensor_reduce(DEN, COMB, AX, ALU.add))
            chain(dve.tensor_scalar(DEN, DEN, 1e-38, None, ALU.max))
            chain(dve.reciprocal(RDEN, DEN))
            chain(dve.tensor_scalar(RDEN, RDEN, 2.5, None, ALU.mult))
            chain(dve.tensor_tensor(COMB, COMB, RDEN.unsqueeze(2).to_broadcast([P, NT, NE]), ALU.mult))
            for t in range(NT):
                for k in range(TOPK):
                    chain(dve.scalar_tensor_tensor(out=EJ, in0=SL[:, t, :], scalar=S8[:, t, k:k + 1], in1=COMB[:, t, :], op0=ALU.is_equal, op1=ALU.mult,
                                                   accum_out=W6[:, t, k:k + 1]))
            for s in range(2):
                dve.wait_ge(g2_mm, s + 1)
                dve.tensor_copy(G2[:, s, 0:512], bank[2 * s][:, :])
                dve.tensor_copy(G2[:, s, 512:D], bank[2 * s + 1][:, :]).then_inc(g2_ready, 1)
            dve.wait_ge(h2_stored[0], 48)
            dve.wait_ge(h2_stored[1], 32)
            dve.wait_ge(as_ready, 1)
            dve.memset(YT, 0.0)
            dve.memset(YO, 0.0).then_inc(yo_ready, 1)
            dve.memset(AE, 0.0).then_inc(ae_ready, 1)
            dve.wait_ge(slots_ld, 16)
            dve.tensor_copy(TF[0:IC, :], TI[0:IC, :]).then_inc(tf_ready, 1)
            dve.wait_ge(tt_done, 1)
            chain(dve.tensor_copy(IDX[0:SLOT, 1, :], bank[7][0:SLOT, 0:IC]))
            dve.tensor_scalar(IDX[0:SLOT, 0, :], IDX[0:SLOT, 1, :], 3, None, ALU.logical_shift_right).then_inc(idx_ready, 1)

            hgt = HGT.rearrange("p k s -> p (k s)")
            dve.wait_ge(hgt_done, 1)
            dve.tensor_copy(hgt, bank[1][:, :]).then_inc(hgt_ready, 1)
            items = dve.value_load(START[0:1, NE:NE + 1], min_val=1, max_val=NI)

            def out_rows(i):
                dve.wait_ge(yo_done, i + 1)
                dve.wait_ge(scattered, (i + 1) * 16)
                dve.tensor_copy(YO[0:SLOT, 0:512], bank[2][0:SLOT, :])
                dve.tensor_copy(YO[0:SLOT, 512:D], bank[3][0:SLOT, :]).then_inc(yo_ready, 1)

            with dve.Fori(0, items) as i:
                dve.wait_ge(silu_done, i + 1)
                dve.tensor_tensor(AE.rearrange("p f s -> p (f s)"), SI, bank[0][:, 2 * SLOT:4 * SLOT], ALU.mult).then_inc(ae_ready, 1)
                dve.wait_ge(hgt_done, i + 2)
                dve.tensor_copy(hgt, bank[1][:, :]).then_inc(hgt_ready, 1)
                out_rows(i)
            out_rows(items)

            dve.wait_ge(gf_ld, 16)
            def finish(t):
                r = ROWS[t]
                dve.wait_ge(fin_sq, t + 1)
                dve.tensor_scalar(SS[:, t:t + 1], SS[:, t:t + 1], 1.0 / D, EPS, ALU.mult, ALU.add).then_inc(fin_ms, 1)
                dve.wait_ge(fin_rs, t + 1)
                dve.scalar_tensor_tensor(out=X[0:r, t, :], in0=X[0:r, t, :], scalar=RS[0:r, t:t + 1], in1=GF[0:r, :], op0=ALU.mult, op1=ALU.mult).then_inc(y_ready, 1)

            for t in range(NT):
                r = ROWS[t]
                dve.wait_ge(yb_ld[t % 2], 16 * (t // 2 + 1))
                for k in range(TOPK):
                    ins = dve.scalar_tensor_tensor(out=YA[0:r, t, :], in0=YB[t % 2][0:r, k, :], scalar=W6[0:r, t, k:k + 1], in1=YA[0:r, t, :], op0=ALU.mult, op1=ALU.add)
                    if k < TOPK - 1:
                        chain(ins)
                ins.then_inc(yb_used, 1)
                dve.wait_ge(yb_used, t + 1)
                chain(dve.tensor_tensor(YA[0:r, t, :], YA[0:r, t, :], G2[0:r, t // 4, :], ALU.mult))
                dve.tensor_tensor(X[0:r, t, :], X[0:r, t, :], YA[0:r, t, :], ALU.add).then_inc(fin_x, 1)
                if t:
                    finish(t - 1)
            finish(NT - 1)


_INS = ["x_prompt", "x_sample", "cache_a_k", "cache_a_v", "cache_b_k", "cache_b_v", "c_prompt", "c_sample", "w_ada", "b_ada",
        "w_in", "lam_params", "g_sub_a", "g_sub_b", "w_out", "w_router", "b_router", "w_gate", "w_up", "w_down",
        "w_shared_gate", "w_shared_up", "w_shared_down", "g_final"]
_OUTS = [(1, TP, D), (1, TS, D), (1, 1, TP, HA, P), (1, 1, TP, HA, P), (1, 1, TP, HB, DB), (1, 1, TP, HB, DB),
         (1, 1, TS, HA, P), (1, 1, TS, HA, P), (1, 1, TS, HB, DB), (1, 1, TS, HB, DB)]


def kernel(**inputs):
    import numpy as np
    import concourse.bacc as bacc
    from concourse.bass_utils import run_bass_kernel_spmd

    nc = bacc.Bacc("TRN2", target_bir_lowering=False, num_devices=1)
    arrays, args = {}, []
    for name in _INS:
        a = np.ascontiguousarray(inputs[name])
        arrays[f"in_{name}"] = a
        args.append(nc.dram_tensor(f"in_{name}", a.shape, F32, kind="ExternalInput").ap())
    for i, shape in enumerate(_OUTS):
        args.append(nc.dram_tensor(f"out_{i}", shape, F32, kind="ExternalOutput").ap())
    build(nc, *args)
    r = run_bass_kernel_spmd(nc, [arrays], core_ids=[0])
    return tuple(r.results[0][f"out_{i}"] for i in range(len(_OUTS)))
```

```python
from contextlib import ExitStack

import concourse.bass as bass
from concourse import mybir

F32 = mybir.dt.float32
I32 = mybir.dt.int32
U32 = mybir.dt.uint32
ALU = mybir.AluOpType
ACT = mybir.ActivationFunctionType
AX = mybir.AxisListType.X

P = 128
D = 1024
KC = D // P
TP, TS = 512, 64
T = TP + TS
NT = TP // P + 1
ROWS = [P, P, P, P, TS]
PAST = 256
PT = PAST // P
HA, HB = 4, 8
DB = 64
NE, NG, EG = 64, 8, 8
TOPK, TOPG = 6, 4
FE = 256
EPS = 1e-6
BIG = 1e30
LAM0 = 0.8 - 0.6
ADA_FIRST = 4
SLOT = 64
NI = NE + T * TOPK // SLOT
IC = NI + 3
YK = 8
NONE = 1 << 14


def build(nc, x_prompt, x_sample, cache_a_k, cache_a_v, cache_b_k, cache_b_v, c_prompt, c_sample, w_ada, b_ada,
          w_in, lam_params, g_sub_a, g_sub_b, w_out, w_router, b_router, w_gate, w_up, w_down, w_sg, w_su, w_sd,
          g_final, y_prompt, y_sample, ak_p, av_p, bk_p, bv_p, ak_s, av_s, bk_s, bv_s):
    ctx = ExitStack()
    with ctx:
        sem = lambda name: ctx.enter_context(nc.semaphore(name))

        N_ARENA = 53000
        arena = ctx.enter_context(nc.sbuf_tensor("arena", [P, N_ARENA], F32))
        bank = [ctx.enter_context(nc.psum_tensor(f"bank{i}", [P, 512], F32)) for i in range(8)]
        top = [0]

        def take(n):
            top[0] += n
            assert top[0] <= N_ARENA, top[0]
            return top[0] - n

        def at(base, *shape, dt=F32):
            n = 1
            for s in shape:
                n *= s
            v = arena[:, base:base + n]
            if dt != F32:
                v = v.bitcast(dt)
            if len(shape) == 2:
                v = v.rearrange("p (a b) -> p a b", b=shape[1])
            elif len(shape) == 3:
                v = v.rearrange("p (a b c) -> p a b c", b=shape[1], c=shape[2])
            return v

        a_x = take(NT * D)
        a_h = take(NT * D)
        a_ring = take(3 * 4096)
        a_att = take(KC * T * 2 + KC * PAST + NT * D + PT * D)
        a_tmp = take(7168)
        X = at(a_x, NT, D)
        HT = at(a_h, KC, T)
        OA = at(a_h, NT, D)
        RING = [at(a_ring + 4096 * i, KC, 512) for i in range(3)]
        QT = at(a_att, KC, T)
        OT = QT
        a_kt = a_att + KC * T
        KT = at(a_kt, KC, T)
        GO = KT
        a_ckt = a_kt + KC * T
        CKT = at(a_ckt, KC, PAST)
        a_v = a_ckt + KC * PAST
        V = at(a_v, NT, D)
        XN = V
        CV = at(a_v + NT * D, PT, D)
        BIAS = at(a_tmp, HA, 512)
        KO = at(a_tmp + 2048, 3, 512)
        CK = at(a_tmp + 3584, PT, D)
        SE = [at(a_tmp + 3584, 2, 512), at(a_tmp + 4608, 2, 512), at(take(1024), 2, 512)]
        WT = at(a_tmp + 5632, 2, 512)
        LK = at(a_tmp, 2, 1536)
        AT = at(a_tmp + 3072, 2, 1536)
        H2S = at(a_tmp, 2, D)
        SA = at(a_tmp + 2048, 2, T)
        GU = [RING[0], RING[1], RING[2], at(a_att, KC, 512)]
        DN = [at(a_att + 4096 + 2048 * i, 2, D) for i in (3, 0, 1, 2)]
        WSG, WSD = GU[0], DN[0]
        HG = at(a_tmp, 512)
        HGT = at(a_tmp + 512, 4, 2, SLOT)
        YO = at(a_tmp + 1024, 512)
        SI = at(a_tmp + 1536, P)
        AC = at(a_tmp + 1664, P)
        AE = at(a_tmp + 1792, 2, SLOT)
        G2 = at(a_tmp + 5120, 2, D)
        GF = at(a_tmp + 3200, D)
        YB = [[(0, at(a_ring + 4096, TOPK, D))], [(0, at(a_att, TOPK, D))], [(0, at(a_ring + 10240, 2, D)), (2, at(a_att + 6144, 4, D))]]
        IDENT = at(take(P), P)
        NTRI = at(take(P), P)
        NONES = at(take(P), P)
        UP = at(take(P), P)
        ONES = at(take(P), P)
        SMT = at(take(66), 66)
        CT = at(take(KC * 32), KC, 32)
        MR = at(take(512), 512)
        SEL2 = at(take(2), 2)
        MOD = at(take(96), 48, 2)
        WR = at(take(KC * NE), KC, NE)
        BR = at(take(NE), NE)
        SQ = at(take(512), 512)
        GA = at(take(2), 2)
        SS = at(take(NT), NT)
        RS = at(take(NT), NT)
        HALF = at(take(60), NT, 12)
        SUMS = at(take(NT * HA * 2), NT, HA, 2)
        MINS = at(take(6), 3, 2)
        CO = at(take(3), 3, 1)
        OS = at(take(60), NT, 12)
        OR = at(take(60), NT, 12)
        LAM = at(take(2), 2)
        NLAM = at(take(1), 1)
        a_route = a_v
        small = at(take(P), 1, P)
        SMALL = small[:, 0, :]
        IDX = at(take(2 * IC), 2, IC, dt=U32)
        ICUR = at(take(2), 2, dt=U32)
        START = at(take(NE + 2), NE + 2, dt=I32)
        W6 = at(take(NT * YK), NT, YK)
        LPX = at(take(256), 256)
        LPM = at(take(128), 128)
        r0 = [a_att + 4096 + 4 * 2048]

        def rt(*shape, dt=F32):
            n = 1
            for s in shape:
                n *= s
            r0[0] += n
            assert r0[0] <= a_tmp
            return at(r0[0] - n, *shape, dt=dt)

        SC = rt(NT, NE)
        SEL = rt(NT, NE)
        G8 = rt(NT * NG, 8)
        GS = rt(NT, 12)
        GTOP = rt(NT, 8)
        GREP = rt(NT, 8)
        GOUT = rt(NT, 12)
        KEEP = rt(NT, NG)
        NEGK = rt(NT, NG)
        SELX = rt(NT, NE + 2)
        ETOP = rt(NT, 8)
        EREP = rt(NT, 8)
        EOUT = rt(NT, NE + 2)
        M = rt(NT, NE)
        COMB = rt(NT, NE)
        DEN = rt(NT)
        RDEN = rt(NT)
        NB_I = rt(NE, dt=I32)
        NB_J = rt(NE, dt=I32)
        NB = rt(NE)
        ZE = rt(NE)
        INC = rt(NE)
        STF = rt(NE + 2)
        SB = rt(NE)
        SL = rt(NT, NE)
        S8 = rt(NT, 8)
        SIDX = rt(NT, 8, dt=I32)
        COLI = rt(NT, 8, dt=I32)
        PLI = rt(NT, 8, dt=I32)
        COLF = rt(NT, 8)
        PLF = rt(NT, 8)
        RECI = rt(NT, 8, dt=I32)
        RECF = rt(NT, 8)
        ITEMS = rt(IC)
        PLACES = rt(2, SLOT)
        OHI = [rt(IC) for _ in range(4)]
        OHP = [rt(2, SLOT) for _ in range(4)]
        EJ = rt(TOPK, NE)

        h2_rows = nc.dram_tensor("h2_rows", (T, D), F32, kind="Internal").ap()
        y_rows = nc.dram_tensor("y_rows", (T * YK, D), F32, kind="Internal").ap()

        pe_mark, pool_mark = sem("pe_mark"), sem("pool_mark")
        small_ld, x_ld, misc_ld, ck_ld, cv_ld, sh_ld = map(sem, ("small_ld", "x_ld", "misc_ld", "ck_ld", "cv_ld", "sh_ld"))
        ring_ld = [sem(f"ring_ld{i}") for i in range(3)]
        pool_c, pool_s, dve_s, act_s = map(sem, ("pool_c", "pool_s", "dve_s", "act_s"))
        small_t, smt_ready, c_ready = map(sem, ("small_t", "smt_ready", "c_ready"))
        lam_sum, lam_exp, lam_neg, lam_bc, nlam_ready = map(sem, ("lam_sum", "lam_exp", "lam_neg", "lam_bc", "nlam_ready"))
        ada_done, mr_ready, mod_mm, mod_ready = map(sem, ("ada_done", "mr_ready", "mod_mm", "mod_ready"))
        sq_done, ms_ready, rs_ready, xn_ready = map(sem, ("sq_done", "ms_ready", "rs_ready", "xn_ready"))
        tr_done, tr_dve, tr_act = map(sem, ("tr_done", "tr_dve", "tr_act"))
        proj_done, proj_act, proj_dve = map(sem, ("proj_done", "proj_act", "proj_dve"))
        kb_done, kb_evac, new_stored = map(sem, ("kb_done", "kb_evac", "new_stored"))
        ko_stored = [sem(f"ko_stored{i}") for i in range(3)]
        h2_stored = [sem(f"h2_stored{i}") for i in range(2)]
        bias_ready, sa_done, sa_read, ea_done, wa_ready, wta_done, wta_evac, pva_done, oa_evac = map(
            sem, ("bias_ready", "sa_done", "sa_read", "ea_done", "wa_ready", "wta_done", "wta_evac", "pva_done", "oa_evac"))
        z_half = sem("z_half")
        abs_ready, fade_ready, z_done, lk_ready, p_done, eb_done, at_ready, pvb_done, ob_evac, lk_ln = map(
            sem, ("abs_ready", "fade_ready", "z_done", "lk_ready", "p_done", "eb_done", "at_ready", "pvb_done", "ob_evac", "lk_ln"))
        osa_ready, ora_ready, osb_ready, orb_ready, on_ready = map(sem, ("osa_ready", "ora_ready", "osb_ready", "orb_ready", "on_ready"))
        wo_done, wo_act, wo_dve, got_done, x1_ready = map(sem, ("wo_done", "wo_act", "wo_dve", "got_done", "x1_ready"))
        logit_done, sc_ready, h2t_done, h2_evac = map(sem, ("logit_done", "sc_ready", "h2t_done", "h2_evac"))
        sg_done, sg_silu, as_ready, sd_done, sd_read = map(sem, ("sg_done", "sg_silu", "as_ready", "sd_done", "sd_read"))
        mask_ready, pos_done, start_ready, sidx_ready, rec_ready, ohi_ready, ohp_ready, oh_done, idx_ready = map(
            sem, ("mask_ready", "pos_done", "start_ready", "sidx_ready", "rec_ready", "ohi_ready", "ohp_ready", "oh_done", "idx_ready"))
        g2_mm, g2_ready = sem("g2_mm"), sem("g2_ready")
        exp_ld = [sem(f"exp_ld{i}") for i in range(4)]
        cur_tok, cur_row, gathered, hgt_done, hgt_ready, gu_done, silu_done, ac_ready, at_done, ae_ready, dn_done, yo_ready, \
            scattered = map(sem, ("cur_tok", "cur_row", "gathered", "hgt_done", "hgt_ready", "gu_done", "silu_done", "ac_ready", "at_done",
                                  "ae_ready", "dn_done", "yo_ready", "scattered"))
        gf_ld, yb_used, w6_ready, acc_ready, fin_sq, fin_ms, fin_rs, y_ready, y_stored, fin_g2, fin_x, init_ready, sc_clear = map(
            sem, ("gf_ld", "yb_used", "w6_ready", "acc_ready", "fin_sq", "fin_ms", "fin_rs", "y_ready", "y_stored", "fin_g2", "fin_x",
                  "init_ready", "sc_clear"))
        yb_ld = [sem(f"yb_ld{i}") for i in range(3)]

        block = ctx.enter_context(nc.Block())

        def kp(w):
            return w.rearrange("(k p) n -> p k n", p=P)

        ada_v, in_v, out_v = kp(w_ada[0]), kp(w_in[0]), kp(w_out[0])
        cols = lambda v, n: v[:, :, 512 * n:512 * n + 512]
        groups = [[(cols(ada_v, n), 0, 512)] for n in range(ADA_FIRST)]
        G_IN = len(groups)
        groups += [[(cols(in_v, n), 0, 512)] for n in range(6)]
        G_ADA = len(groups)
        groups += [[(cols(ada_v, n), 0, 512)] for n in range(ADA_FIRST, 12)]
        G_OUT = len(groups)
        groups += [[(cols(out_v, n), 0, 512)] for n in range(2)]

        def ring_count(g):
            return sum(16 * len(groups[i]) for i in range(g % 3, g + 1, 3))

        def used(g):
            if g < G_IN:
                return ada_done, g + 1
            if g < G_ADA:
                return proj_done, 5 * (g - G_IN + 1)
            if g < G_OUT:
                return ada_done, ADA_FIRST + g - G_ADA + 1
            return wo_done, 5 * (g - G_OUT + 1)

        KEYS = [P, 2 * P, 3 * P, 4 * P, PAST + TS]
        BOFF = [384, 256, 128, 0, 128]
        UNITS = [(i, h) for i in range(NT) for h in range(HA)]
        ZO = [0, 512, 896, 1152]
        ZW = [512, 384, 256, 128]
        ZS = [(0, 512), (512, 384), (896, 384)]

        def zbank(h, j):
            b = 3 * (h % 2) + min(j, 2)
            o = 256 if j == 3 else 0
            return bank[b][:, o:o + ZW[j]]

        SDB = [(0, 1), (3, 5), (6, 7), (2, 4), (0, 1)]

        def b_stat(v, h):
            return v[:, 0:4, HA + h] if h < HB else v[0:TS, 4, HA:HA + HB]

        @block.sync
        def _(sp):
            sp.dma_start(SMALL[0:8, :], c_prompt.rearrange("b (k p) -> (b k) p", p=P)).then_inc(small_ld, 16)
            sp.dma_start(SMALL[8:16, :], c_sample.rearrange("b (k p) -> (b k) p", p=P)).then_inc(small_ld, 16)
            sp.dma_start(SMALL[16:64, :], b_ada.rearrange("b (k p) -> (b k) p", p=P)).then_inc(small_ld, 16)
            sp.dma_start(SMALL[64:65, :], g_sub_a).then_inc(small_ld, 16)
            sp.dma_start(SMALL[65:66, 0:DB], g_sub_b).then_inc(small_ld, 16)
            sp.dma_start(SMALL[65:66, DB:P], g_sub_b).then_inc(small_ld, 16)
            sp.dma_start(X[:, 0:4, :], x_prompt[0].rearrange("(t p) d -> p t d", p=P)).then_inc(x_ld, 16)
            sp.dma_start(X[0:TS, 4, :], x_sample[0]).then_inc(x_ld, 16)
            sp.dma_start(LPX[0:1, :], lam_params.rearrange("l a d -> l (a d)")).then_inc(misc_ld, 16)
            sp.dma_start(WR, kp(w_router[0])).then_inc(misc_ld, 16)
            sp.dma_start(BR, b_router.to_broadcast([P, NE])).then_inc(misc_ld, 16)
            for g, parts in enumerate(groups):
                if g == 3:
                    sp.dma_start(CK[:, :, 0:512], cache_a_k[0, 0].rearrange("(j p) h d -> p j (h d)", p=P)).then_inc(ck_ld, 16)
                    sp.dma_start(CK[:, :, 512:D], cache_b_k[0, 0].rearrange("(j p) h d -> p j (h d)", p=P)).then_inc(ck_ld, 16)
                    sp.dma_start(CV[:, :, 0:512], cache_a_v[0, 0].rearrange("(j p) h d -> p j (h d)", p=P)).then_inc(cv_ld, 16)
                    sp.dma_start(CV[:, :, 512:D], cache_b_v[0, 0].rearrange("(j p) h d -> p j (h d)", p=P)).then_inc(cv_ld, 16)
                if g >= 3:
                    sp.wait_ge(*used(g - 3))
                for view, a, b in parts:
                    sp.dma_start(RING[g % 3][:, :, a:b], view).then_inc(ring_ld[g % 3], 16)
            def load_expert(e, j):
                sp.dma_start(GU[j][:, :, 0:FE], w_gate[0, bass.ds(e, 1)].rearrange("e (k p) n -> p (e k) n", p=P)).then_inc(exp_ld[j], 16)
                sp.dma_start(GU[j][:, :, FE:2 * FE], w_up[0, bass.ds(e, 1)].rearrange("e (k p) n -> p (e k) n", p=P)).then_inc(exp_ld[j], 16)
                sp.dma_start(DN[j], w_down[0, bass.ds(e, 1)].rearrange("e (f p) n -> p (e f) n", p=P)).then_inc(exp_ld[j], 16)

            sp.wait_ge(tr_done, 27)
            sp.wait_ge(wo_done, 10)
            for j in range(4):
                load_expert(j, j)
            sp.wait_ge(start_ready, 1)
            with sp.Fori(0, NE // 4 - 1) as g:
                e = g * 4
                for j in range(4):
                    done = sp.value_load(START[0:1, bass.ds(e + (j + 1), 1)], min_val=0, max_val=NI)
                    sp.wait_ge(dn_done, done + 1)
                    load_expert(e + (j + 4), j)
            done = sp.value_load(START[0:1, NE - 3:NE - 2], min_val=0, max_val=NI)
            sp.wait_ge(dn_done, done + 1)
            sp.dma_start(WSG[:, :, 0:FE], kp(w_sg[0])).then_inc(sh_ld, 16)
            sp.dma_start(WSG[:, :, FE:2 * FE], kp(w_su[0])).then_inc(sh_ld, 16)
            sp.dma_start(WSD, w_sd[0].rearrange("(f p) n -> p f n", p=P)).then_inc(sh_ld, 16)
            sp.dma_start(GF, g_final.rearrange("(a n) -> a n", a=1).to_broadcast([P, D])).then_inc(gf_ld, 16)
            items = sp.value_load(START[0:1, NE:NE + 1], min_val=0, max_val=NI)
            sp.wait_ge(scattered, (items + 2) * 16)
            for t in range(NT):
                if t >= 3:
                    sp.wait_ge(fin_x, t - 2)
                r = ROWS[t]
                rows = y_rows[t * P * YK:(t * P + r) * YK, :].rearrange("(p k) d -> p k d", k=YK)
                for k, part in YB[t % 3]:
                    sp.dma_start(part[0:r], rows[:, k:k + part.shape[1], :]).then_inc(yb_ld[t % 3], 16)
            for t in range(NT):
                sp.wait_ge(y_ready, t + 1)
                r = ROWS[t]
                dst = y_prompt[0, t * P:t * P + P, :] if t < 4 else y_sample[0]
                sp.dma_start(dst, X[0:r, t, :]).then_inc(y_stored, 16)
            sp.wait_ge(y_stored, 16 * NT)

        @block.gpsimd
        def _(pool):
            n = [0]

            def chain(ins):
                n[0] += 1
                ins.then_inc(pool_s, 1)
                pool.wait_ge(pool_s, n[0])

            pool.memset(IDENT, 0.0)
            pool.memset(NTRI, -1.0)
            pool.memset(UP, 1.0)
            pool.memset(NONES, -1.0)
            pool.memset(ONES, 1.0)
            chain(pool.memset(HALF, -0.5))
            pool.affine_select(out=IDENT, in_=IDENT, compare_op=ALU.not_equal, fill=1.0, base=0, pattern=[[-1, P]], channel_multiplier=1)
            pool.affine_select(out=NTRI, in_=NTRI, compare_op=ALU.is_ge, fill=0.0, base=0, pattern=[[-1, P]], channel_multiplier=1)
            pool.affine_select(out=UP, in_=UP, compare_op=ALU.is_gt, fill=0.0, base=0, pattern=[[1, P]], channel_multiplier=-1)
            pool.iota(BIAS[:, 0, :], pattern=[[-1, 512]], base=384, channel_multiplier=1, allow_small_or_imprecise_dtypes=True).then_inc(pool_c, 1)
            pool.wait_ge(ms_ready, 1)
            pool.tensor_tensor(RS, SS, HALF[:, 0, 0:NT], ALU.pow).then_inc(rs_ready, 1)
            for a, (kp_o, ks_o, vp_o, vs_o) in enumerate(((ak_p, ak_s, av_p, av_s), (bk_p, bk_s, bv_p, bv_s))):
                if a == 0:
                    pool.wait_ge(proj_act, 10)
                else:
                    pool.wait_ge(proj_dve, 15)
                c = slice(512 * a, 512 * a + 512)
                pool.dma_start(vp_o[0, 0].rearrange("(t p) h d -> p t (h d)", p=P), V[:, 0:4, c]).then_inc(new_stored, 16)
                pool.dma_start(vs_o[0, 0].rearrange("s h d -> s (h d)"), V[0:TS, 4, c]).then_inc(new_stored, 16)
                for t in range(NT):
                    u = NT * a + t
                    pool.wait_ge(kb_evac, u + 1)
                    dst = kp_o[0, 0, t * P:t * P + P] if t < 4 else ks_o[0, 0]
                    pool.dma_start(dst.rearrange("s h d -> s (h d)"), KO[0:ROWS[t], u % 3, :]).then_inc(ko_stored[u % 3], 16)
            def b_rms(h):
                pool.wait_ge(osb_ready, h + 1)
                pool.tensor_tensor(b_stat(OR, h), b_stat(OS, h), b_stat(HALF, h), ALU.pow).then_inc(orb_ready, 1)

            for h in range(HB + 1):
                for s in range(3):
                    pool.wait_ge(eb_done, 3 * h + s + 1)
                    if h < HB:
                        blocks = [ZO[j] for j in ([2, 3], [1], [0])[s]]
                        for o in blocks:
                            v = AT[:, h % 2, o:o + P]
                            last = pool.affine_select(out=v, in_=v, compare_op=ALU.is_gt, fill=0.0, base=0, pattern=[[1, P]], channel_multiplier=-1)
                        last.then_inc(at_ready, 1)
                    elif s == 0:
                        v = AT[0:TS, h % 2, 1024:1536].rearrange("p (h q) -> p h q", q=TS)
                        pool.affine_select(out=v, in_=v, compare_op=ALU.is_gt, fill=0.0, base=0, pattern=[[0, HB], [1, TS]], channel_multiplier=-1).then_inc(at_ready, 1)
                if h == 0:
                    pool.wait_ge(osa_ready, 1)
                    pool.tensor_tensor(OR[:, :, 0:HA], OS[:, :, 0:HA], HALF[:, :, 0:HA], ALU.pow).then_inc(ora_ready, 1)
                if h >= 2:
                    b_rms(h - 2)
            b_rms(HB - 1)
            b_rms(HB)
            for t in range(NT):
                pool.wait_ge(ms_ready, 2 + t)
                pool.tensor_tensor(RS[:, t:t + 1], SS[:, t:t + 1], HALF[:, 0, 0:1], ALU.pow).then_inc(rs_ready, 1)
            pool.wait_ge(tr_done, 27)
            pool.wait_ge(logit_done, 1)
            pool.iota(RECI, pattern=[[2 * P * YK, NT], [2, 8]], base=-NONE, channel_multiplier=2 * YK)
            pool.iota(ITEMS, pattern=[[1, IC]], base=0, channel_multiplier=0, allow_small_or_imprecise_dtypes=True)
            chain(pool.iota(PLACES, pattern=[[0, 2], [1, SLOT]], base=0, channel_multiplier=0, allow_small_or_imprecise_dtypes=True))
            pool.tensor_copy(RECF, RECI).then_inc(rec_ready, 1)
            pool.wait_ge(sidx_ready, 1)
            for u in range(NT * TOPK):
                t, k = divmod(u, TOPK)
                if u >= 4:
                    pool.wait_ge(oh_done, u - 3)
                pool.tensor_scalar(OHI[u % 4], ITEMS, COLF[:, t, k:k + 1], None, ALU.is_equal).then_inc(ohi_ready, 1)
            pool.wait_ge(h2_stored[0], 48)
            pool.wait_ge(h2_stored[1], 32)
            chain(pool.memset(HG, 0.0))
            pool.wait_ge(idx_ready, 1)
            items = pool.value_load(START[0:1, NE:NE + 1], min_val=1, max_val=NI)

            h2_halves = h2_rows.rearrange("t (h d) -> (t h) d", h=2)
            y_halves = y_rows.rearrange("t (h d) -> (t h) d", h=2)

            def gather(i, column):
                pool.tensor_copy(ICUR[:, 0:1], column).then_inc(cur_tok, 1)
                pool.wait_ge(cur_tok, i + 1)
                pool.sem_inc(pool_mark)
                pool.indirect_dma_start(HG, None, h2_halves, bass.IndirectOffsetOnAxis(ap=ICUR[:, 0:1], axis=0),
                                        bounds_check=2 * T - 1, oob_is_err=False).then_inc(gathered, 16)

            def scatter(i):
                pool.tensor_copy(ICUR[:, 1:2], IDX[:, 1, bass.ds(i, 1)]).then_inc(cur_row, 1)
                pool.wait_ge(cur_row, i + 1)
                pool.sem_inc(pool_mark)
                pool.indirect_dma_start(y_halves, bass.IndirectOffsetOnAxis(ap=ICUR[:, 1:2], axis=0), YO, None,
                                        bounds_check=2 * T * YK - 1, oob_is_err=False).then_inc(scattered, 16)

            gather(0, IDX[:, 0, 1:2])
            pool.wait_ge(yo_ready, 1)
            pool.indirect_dma_start(y_halves, bass.IndirectOffsetOnAxis(ap=IDX[:, 1, 0:1], axis=0), YO, None,
                                    bounds_check=2 * T * YK - 1, oob_is_err=False).then_inc(scattered, 16)
            pool.wait_ge(hgt_done, 1)
            gather(1, IDX[:, 0, 2:3])
            with pool.Fori(0, items) as i:
                pool.wait_ge(hgt_done, i + 2)
                pool.sem_inc(pool_mark)
                gather(i + 2, IDX[:, 0, bass.ds(i + 3, 1)])
                pool.wait_ge(yo_ready, i + 2)
                pool.sem_inc(pool_mark)
                scatter(i)
            pool.wait_ge(yo_ready, items + 2)
            pool.sem_inc(pool_mark)
            scatter(items)
            pool.wait_ge(gathered, (items + 2) * 16)
            for t in range(NT + 1):
                if t < NT:
                    r = ROWS[t]
                    acc = YB[t % 3][0][1][0:r, 0, :]
                    pool.wait_ge(acc_ready, t + 1)
                    pool.tensor_tensor(acc, acc, G2[0:r, t // 4, :], ALU.mult).then_inc(fin_g2, 1)
                    pool.wait_ge(fin_g2, t + 1)
                    pool.tensor_tensor(X[0:r, t, :], X[0:r, t, :], acc, ALU.add).then_inc(fin_x, 1)
                if t:
                    pool.wait_ge(fin_ms, t)
                    pool.tensor_tensor(RS[:, t - 1:t], SS[:, t - 1:t], HALF[:, 0, 0:1], ALU.pow).then_inc(fin_rs, 1)
            pool.wait_ge(new_stored, 64)
            for b, c in enumerate((4, 3, 3)):
                pool.wait_ge(ko_stored[b], 16 * c)

        @block.tensor
        def _(pe):
            def back(src, r, b):
                for k in range(KC):
                    last = pe.transpose(bank[b + k // 4][0:r, (k % 4) * P:(k % 4 + 1) * P], src(k), IDENT)
                return last

            def turn(src, r, half=None, sample=None):
                for k in range(KC):
                    if k == 4 and half:
                        pe.wait_ge(*half)
                    if k >= 4:
                        pe.wait_ge(tr_act if k % 2 else tr_dve, (4 if k % 2 else 5) * r + (k - 4) // 2 + 1)
                    for t in range(4):
                        last = pe.transpose(bank[k % 4][:, t * P:t * P + P], src[:, t, k * P:k * P + P], IDENT)
                    last.then_inc(tr_done, 1)
                if sample:
                    pe.wait_ge(*sample)
                for k in range(KC):
                    last = pe.transpose(bank[4][:, k * TS:k * TS + TS], src[0:TS, 4, k * P:k * P + P], IDENT[0:TS, 0:TS])
                last.then_inc(tr_done, 1)

            def turned(r):
                pe.wait_ge(tr_dve, 5 * (r + 1))
                pe.wait_ge(tr_act, 4 * (r + 1))

            def ada(a, g):
                pe.wait_ge(ring_ld[g % 3], ring_count(g))
                if a:
                    pe.wait_ge(mod_ready, a)
                else:
                    pe.wait_ge(c_ready, 1)
                for k in range(KC):
                    q = k % 4
                    last = pe.matmul(bank[6][32 * q:32 * q + 32, :], CT[:, k, :], RING[g % 3][:, k, :], start=(k < 4), stop=(k >= 4),
                                     tile_position=(0, 32 * q))
                last.then_inc(ada_done, 1)

            def ada_turn(a):
                pe.wait_ge(mr_ready, a + 1)
                for m in range(4):
                    last = pe.matmul(bank[6][:, 2 * m:2 * m + 2], MR[:, m * P:m * P + P], SEL2, start=True, stop=True)
                last.then_inc(mod_mm, 1)

            def wide(w, src, m, prompt, sample, done, last_m):
                for k in range(KC):
                    lw = w[:, k, m * P:m * P + P]
                    a = pe.matmul(prompt, lw, src[:, k, 0:TP], start=(k == 0), stop=(k == KC - 1))
                    b = pe.matmul(sample, lw, src[:, k, TP:T], start=(k == 0), stop=(k == KC - 1))
                a.then_inc(done, 1)
                if m == last_m:
                    b.then_inc(done, 1)
                return b

            pe.wait_ge(pool_c, 1)
            pe.wait_ge(small_ld, 96)
            pe.transpose(bank[7][:, 0:66], SMALL[0:66, :], IDENT[0:66, 0:66]).then_inc(small_t, 1)
            for a in range(ADA_FIRST):
                ada(a, a)
                ada_turn(a)
            pe.wait_ge(lam_neg, 1)
            pe.wait_ge(smt_ready, 1)
            pe.matmul(bank[7][:, 0:1], ONES[0:1, :], LAM[0:1, 0:1], start=True, stop=True).then_inc(lam_bc, 1)
            pe.wait_ge(xn_ready, NT)
            turn(XN, 0)
            turned(0)
            for n in range(6):
                g = G_IN + n
                pe.wait_ge(ring_ld[g % 3], ring_count(g))
                w = RING[g % 3]
                for t in range(NT):
                    if n % 3 < 2 and t == 4:
                        continue
                    if n:
                        pe.wait_ge(proj_dve if n % 2 == 0 else proj_act, 5 * ((n - 1) // 2) + t + 1)
                    if n % 3 < 2:
                        if n and t == 0:
                            pe.wait_ge(proj_dve if n % 2 == 0 else proj_act, 5 * ((n - 1) // 2) + 5)
                        wide(w, HT, t, bank[t][:, :], bank[4][:, t * TS:t * TS + TS], proj_done, 3)
                    else:
                        r = ROWS[t]
                        for k in range(KC):
                            last = pe.matmul(bank[t][0:r, :], HT[:, k, t * P:t * P + r], w[:, k, :], start=(k == 0), stop=(k == KC - 1))
                        last.then_inc(proj_done, 1)
                if n % 3 == 2:
                    a = n // 3
                    pe.wait_ge(proj_dve if a == 0 else proj_act, 5 if a == 0 else 15)
                    for t in range(NT):
                        q = NT * a + t
                        if q >= 2:
                            pe.wait_ge(kb_evac, q - 1)
                        else:
                            pe.wait_ge(nlam_ready, 1)
                        b = bank[5 + 2 * (q % 2)]
                        r = ROWS[t]
                        for m in range(4):
                            last = pe.transpose(b[0:r, m * P:m * P + P], KT[:, 4 * a + m, t * P:t * P + r], IDENT)
                        last.then_inc(kb_done, 1)
            pe.wait_ge(ck_ld, 32)
            for j in range(PT):
                for a in range(2):
                    q = 2 * NT + 2 * j + a
                    pe.wait_ge(kb_evac, q - 1)
                    b = bank[5 + 2 * (q % 2)]
                    for m in range(4):
                        last = pe.transpose(b[:, m * P:m * P + P], CK[:, j, 512 * a + m * P:512 * a + m * P + P], IDENT)
                    last.then_inc(kb_done, 1)

            def a_scores(u):
                i, h = UNITS[u]
                r = ROWS[i]
                if u == 0:
                    pe.wait_ge(proj_dve, 15)
                    pe.wait_ge(proj_act, 15)
                if u >= 2:
                    pe.wait_ge(sa_read, 2 * (u - 1))
                if i == 4 and h == 0:
                    pe.wait_ge(kb_evac, 14)
                for m in range(2):
                    b = bank[2 * (u % 2) + m]
                    q = QT[m * DB:m * DB + DB, h, i * P:i * P + r]
                    if i < 4:
                        last = pe.matmul(b[:, 0:KEYS[i]], q, KT[m * DB:m * DB + DB, h, 0:KEYS[i]], start=True, stop=True)
                    else:
                        pe.matmul(b[0:r, 0:PAST], q, CKT[m * DB:m * DB + DB, h, :], start=True, stop=True)
                        last = pe.matmul(b[0:r, PAST:PAST + TS], q, KT[m * DB:m * DB + DB, h, TP:T], start=True, stop=True)
                last.then_inc(sa_done, 1)

            def a_turn(u):
                i, h = UNITS[u]
                r = ROWS[i]
                if u >= 2:
                    pe.wait_ge(wta_evac, u - 1)
                else:
                    pe.wait_ge(kb_evac, 14)
                pe.wait_ge(wa_ready, u + 1)
                for j in range((KEYS[i] + P - 1) // P):
                    w = min(P, KEYS[i] - j * P)
                    last = pe.transpose(bank[4 + u % 2][0:w, j * P:j * P + r], SE[u % 3][0:r, 1, j * P:j * P + w], IDENT[0:r, 0:r])
                last.then_inc(wta_done, 1)

            def a_values(u):
                i, h = UNITS[u]
                r = ROWS[i]
                nj = (KEYS[i] + P - 1) // P
                if u >= 2:
                    pe.wait_ge(oa_evac, u - 1)
                pe.wait_ge(wta_evac, u + 1)
                for j in range(nj):
                    w = min(P, KEYS[i] - j * P)
                    v = V[:, j, h * P:h * P + P] if i < 4 else (CV[:, j, h * P:h * P + P] if j < PT else V[0:TS, 4, h * P:h * P + P])
                    last = pe.matmul(bank[6 + u % 2][0:r, 0:P], WT[0:w, u % 2, j * P:j * P + r], v, start=(j == 0), stop=(j == nj - 1))
                last.then_inc(pva_done, 1)

            pe.wait_ge(cv_ld, 32)
            for u in range(len(UNITS) + 3):
                if u < len(UNITS):
                    a_scores(u)
                if 2 <= u <= len(UNITS) + 1:
                    a_turn(u - 2)
                if u >= 3:
                    a_values(u - 3)

            def b_scores(h):
                if h == 0:
                    pe.wait_ge(oa_evac, len(UNITS))
                if h >= 2:
                    pe.wait_ge(eb_done, 3 * (h - 1))
                for j in ((2, 3, 1, 0) if h < HB else (2, 1, 0)):
                    if h < HB:
                        o = h % 2 * DB
                        last = pe.matmul(zbank(h, j), KT[o:o + DB, 4 + h // 2, j * P:j * P + P], QT[o:o + DB, 4 + h // 2, j * P:TP],
                                         start=(j < 3), stop=True, skip_group_check=True)
                        if j != 2:
                            last.then_inc(z_done, 1)
                    else:
                        r = P if j < PT else TS
                        for x, g in enumerate((0, 2, 4, 6, 1, 3, 5, 7)):
                            o = g % 2 * DB
                            if x == 4:
                                last.then_inc(z_half, 1)
                                pe.wait_ge(z_half, 3 - j)
                            k = CKT[o:o + DB, 4 + g // 2, j * P:j * P + P] if j < PT else KT[o:o + DB, 4 + g // 2, TP:T]
                            last = pe.matmul(bank[3 * (h % 2) + j][0:r, g * TS:g * TS + TS], k, QT[o:o + DB, 4 + g // 2, TP:T],
                                             start=(g == 0), stop=True, skip_group_check=True)
                        last.then_inc(z_done, 1)

            def b_sums(h):
                for j in ((3, 2, 1, 0) if h < HB else (2, 1, 0)):
                    s = min(j, 2)
                    pe.wait_ge(lk_ready, 3 * h + 3 - s)
                    if h < HB:
                        out = zbank(h, j)
                        last = pe.matmul(out, NTRI, LK[:, h % 2, ZO[j]:ZO[j] + ZW[j]], start=False, stop=True, skip_group_check=True)
                        for l in range(j + 1, 4):
                            last = pe.matmul(out[:, (l - j) * P:ZW[j]], NONES, LK[:, h % 2, ZO[l]:ZO[l] + ZW[l]], start=False, stop=True, skip_group_check=True)
                        if j != 3:
                            last.then_inc(p_done, 1)
                    else:
                        r = P if j < PT else TS
                        out = bank[3 * (h % 2) + j][0:r, :]
                        last = pe.matmul(out, NTRI[0:r, 0:r], LK[0:r, h % 2, j * 512:j * 512 + 512], start=False, stop=True, skip_group_check=True)
                        for l in range(j + 1, 3):
                            rl = P if l < PT else TS
                            last = pe.matmul(out, NONES[0:rl, 0:r], LK[0:rl, h % 2, l * 512:l * 512 + 512], start=False, stop=True, skip_group_check=True)
                        last.then_inc(p_done, 1)

            def b_values(h):
                if h >= 1:
                    pe.wait_ge(ob_evac, h)
                pe.wait_ge(at_ready, 3 * h + 3 if h < HB else 3 * HB + 1)
                if h < HB:
                    for i in range(4):
                        for j in range(i + 1):
                            o = ZO[j] + (i - j) * P
                            last = pe.matmul(bank[7][:, i * DB:i * DB + DB], AT[:, h % 2, o:o + P], V[:, j, 512 + h * DB:512 + h * DB + DB],
                                             start=(j == 0), stop=(j == i))
                else:
                    pe.wait_ge(eb_done, 3 * HB + 3)
                    for g in range(HB):
                        c = slice(512 + g * DB, 512 + g * DB + DB)
                        for j in range(3):
                            r = P if j < PT else TS
                            v = CV[:, j, c] if j < PT else V[0:TS, 4, c]
                            last = pe.matmul(bank[7][0:TS, g * DB:g * DB + DB], AT[0:r, h % 2, j * 512 + g * TS:j * 512 + g * TS + TS], v,
                                             start=(j == 0), stop=(j == 2))
                last.then_inc(pvb_done, 1)

            for h in range(HB + 3):
                if h <= HB:
                    b_scores(h)
                if 1 <= h <= HB:
                    ada_turn(ADA_FIRST + h - 1)
                if 1 <= h <= HB + 1:
                    b_sums(h - 1)
                if h >= 2:
                    b_values(h - 2)
                if h < HB:
                    ada(ADA_FIRST + h, G_ADA + h)

            pe.wait_ge(eb_done, 3 * (HB + 1))
            pe.wait_ge(on_ready, NT)
            turn(OA, 1, half=(on_ready, NT + HB), sample=(on_ready, NT + HB + 1))
            turned(1)
            for m in range(8):
                g = G_OUT + m // 4
                if m % 4 == 0:
                    pe.wait_ge(ring_ld[g % 3], ring_count(g))
                if m >= 4:
                    pe.wait_ge(wo_act, m - 3)
                wide(RING[g % 3], OT, m % 4, bank[m % 4][:, :], bank[4 + m // 4][:, (m % 4) * TS:(m % 4) * TS + TS], wo_done, 3)
            pe.wait_ge(wo_act, 8)
            pe.wait_ge(wo_dve, 2)
            for t in range(NT):
                if t >= 2:
                    pe.wait_ge(x1_ready, t - 1)
                r = ROWS[t]
                back(lambda k: GO[:, k, t * P:t * P + r], r, 6 if t % 2 == 0 else 0).then_inc(got_done, 1)
            pe.wait_ge(xn_ready, 2 * NT)
            turn(XN, 2)
            turned(2)
            pe.wait_ge(misc_ld, 48)
            for t in range(NT):
                r = ROWS[t]
                for k in range(KC):
                    last = pe.matmul(bank[5][0:r, t * NE:t * NE + NE], HT[:, k, t * P:t * P + r], WR[:, k, :], start=(k == 0), stop=(k == KC - 1))
            last.then_inc(logit_done, 1)
            for t in range(NT):
                if t >= 2:
                    pe.wait_ge(h2_evac, t - 1)
                r = ROWS[t]
                back(lambda k: HT[:, k, t * P:t * P + r], r, 6 if t % 2 == 0 else 0).then_inc(h2t_done, 1)
            pe.wait_ge(mask_ready, 1)
            pe.wait_ge(h2_evac, NT)
            for t in range(NT):
                pe.matmul(bank[6][:, t * NE:t * NE + NE], UP, M[:, t, :], start=True, stop=(t == 0))
                for l in range(t):
                    pe.matmul(bank[6][:, t * NE:t * NE + NE], ONES, M[:, l, :], start=False, stop=(l == t - 1))
            for t in range(NT):
                last = pe.matmul(bank[7][:, 0:NE], ONES, M[:, t, :], start=(t == 0), stop=(t == NT - 1))
            last.then_inc(pos_done, 1)
            for u in range(NT * TOPK):
                pe.wait_ge(ohi_ready, u + 1)
                pe.wait_ge(ohp_ready, u + 1)
                pe.matmul(bank[7][:, 0:IC], OHP[u % 4].rearrange("p h s -> p (h s)"), OHI[u % 4], start=(u == 0), stop=(u == NT * TOPK - 1)).then_inc(oh_done, 1)
            for s in range(2):
                for k in range(KC):
                    last = pe.matmul(bank[(4, 2)[s] + k // 4][:, (k % 4) * P:(k % 4 + 1) * P], MOD[:, 40 + k, s:s + 1].to_broadcast([P, P]), IDENT, start=True, stop=True)
                last.then_inc(g2_mm, 1)

            def turn_in():
                for c in range(4):
                    last = pe.transpose(bank[1][:, c * P:c * P + P], HG[:, c * P:c * P + P], IDENT)
                last.then_inc(hgt_done, 1)

            def gate_up(j):
                for k in range(KC):
                    w = GU[j][:, k, :].rearrange("p (g f) -> p g f", f=FE)
                    for n in range(2):
                        last = pe.matmul(bank[0][n * SLOT:n * SLOT + SLOT, 0:2 * P].rearrange("p (g f) -> p g f", f=P), HGT[:, k % 4, k // 4, :],
                                         w[:, :, n * P:n * P + P], start=(k == 0), stop=(k == KC - 1))
                last.then_inc(gu_done, 1)

            def down(j):
                for f in range(2):
                    for n in range(2):
                        last = pe.matmul(bank[3][n * SLOT:n * SLOT + SLOT, :], AE[:, f, :], DN[j][:, f, 512 * n:512 * n + 512], start=(f == 0), stop=(f == 1))
                last.then_inc(dn_done, 1)

            def item(i, j, before):
                pe.wait_ge(hgt_ready, i + 1)
                gate_up(j)
                pe.wait_ge(gathered, (i + 2) * 16)
                pe.sem_inc(pe_mark)
                turn_in()
                pe.wait_ge(ae_ready, i + 1)
                pe.wait_ge(yo_ready, i + 1)
                down(before)
                pe.wait_ge(ac_ready, i + 1)
                pe.sem_inc(pe_mark)
                pe.transpose(bank[2][:, 0:P], AC, IDENT).then_inc(at_done, 1)

            pe.wait_ge(g2_ready, 2)
            pe.wait_ge(gathered, 16)
            turn_in()
            pe.wait_ge(exp_ld[3], 48)
            with pe.Fori(0, NE // 4) as g:
                e = g * 4
                for j in range(4):
                    lo = pe.value_load(START[0:1, bass.ds(e + j, 1)], min_val=0, max_val=NI - 1)
                    hi = pe.value_load(START[0:1, bass.ds(e + (j + 1), 1)], min_val=1, max_val=NI)
                    pe.wait_ge(exp_ld[j], (g + 1) * 48)
                    pe.sem_inc(pe_mark)
                    item(lo, j, (j + 3) % 4)
                    with pe.If_lt(pe.to_reg(lo + 1), pe.to_reg(hi)):
                        with pe.Fori(lo + 1, hi) as i:
                            item(i, j, j)
            items = pe.value_load(START[0:1, NE:NE + 1], min_val=1, max_val=NI)
            pe.wait_ge(ae_ready, items + 1)
            pe.wait_ge(yo_ready, items + 1)
            down(3)
            pe.wait_ge(sh_ld, 48)
            for m in range(4):
                wide(WSG, HT, m, bank[(5, 6, 7, 2)[m]][:, :], bank[4][:, m * TS:m * TS + TS], sg_done, 3)
            pe.wait_ge(hgt_ready, items + 1)
            pe.wait_ge(yo_ready, items + 2)
            pe.wait_ge(as_ready, 1)
            for t in range(NT):
                if t == 4:
                    pe.wait_ge(sd_read, 1)
                r = ROWS[t]
                for n in range(2):
                    for f in range(2):
                        last = pe.matmul(bank[SDB[t][n]][0:r, :], SA[:, f, t * P:t * P + r], WSD[:, f, 512 * n:512 * n + 512], start=(f == 0), stop=(f == 1))
                last.then_inc(sd_done, 1)

        @block.scalar
        def _(act):
            n = [0]

            def chain(ins):
                n[0] += 1
                ins.then_inc(act_s, 1)
                act.wait_ge(act_s, n[0])

            def squares(t, junk, done, before):
                r = ROWS[t]
                act.wait_ge(done, before)
                act.activation(at(junk, D)[0:r, :], X[0:r, t, :], ACT.Square, accum_out=SS[0:r, t:t + 1]).then_inc(done, 1)

            def turned(r, dst, scale, shift):
                for k in range(1, KC, 2):
                    act.wait_ge(tr_done, 9 * r + k + 1)
                    act.activation(dst[:, k, 0:TP], bank[k % 4][:, :], ACT.Identity, scale=scale(k), bias=shift(k) if shift else 0.0).then_inc(tr_act, 1)

            act.wait_ge(x_ld, 32)
            act.wait_ge(init_ready, 1)
            for t in range(NT):
                squares(t, a_tmp + 5632, sq_done, t)
            act.wait_ge(smt_ready, 1)
            act.activation(CT[:, :, 0:2], SMT[:, 0:16].rearrange("p (s k) -> p k s", k=KC), ACT.Silu).then_inc(c_ready, 1)
            act.wait_ge(lam_sum, 1)
            act.activation(LAM[0:1, :], LAM[0:1, :], ACT.Exp).then_inc(lam_exp, 1)
            act.wait_ge(mod_ready, ADA_FIRST)
            turned(0, HT, lambda k: MOD[:, 8 + k, 0:1], lambda k: MOD[:, k, 0:1])

            def keys_out(q):
                act.wait_ge(kb_done, q + 1)
                b = bank[5 + 2 * (q % 2)]
                if q < 2 * NT:
                    if q >= 3:
                        act.wait_ge(ko_stored[q % 3], 16 * (q // 3))
                    r = ROWS[q % NT]
                    act.copy(KO[0:r, q % 3, :], b[0:r, :]).then_inc(kb_evac, 1)
                else:
                    j, a = divmod(q - 2 * NT, 2)
                    act.copy(CKT[:, 4 * a:4 * a + 4, j * P:j * P + P], b.rearrange("p (m c) -> p m c", c=P)).then_inc(kb_evac, 1)

            for n_g in (0, 2, 4):
                for t in range(NT):
                    act.wait_ge(proj_done, 5 * n_g + t + 1)
                    if n_g == 2:
                        r = ROWS[t]
                        ins = act.copy(V[0:r, t, 0:512], bank[t][0:r, :])
                    else:
                        dst, scale = (QT[:, 0:4], -DB ** -0.5) if n_g == 0 else (KT[:, 4:8], 1.0)
                        if t < 4:
                            ins = act.activation(dst[:, t, 0:TP], bank[t][:, :], ACT.Copy, scale=scale)
                        else:
                            ins = act.activation(dst[:, :, TP:T], bank[4][:, 0:256].rearrange("p (m c) -> p m c", c=TS), ACT.Copy, scale=scale)
                    ins.then_inc(proj_act, 1)
                if n_g == 2:
                    for q in range(NT):
                        keys_out(q)
            for q in range(NT, 2 * NT + 4):
                keys_out(q)

            def a_exp(u):
                i, h = UNITS[u]
                r = ROWS[i]
                for m in range(2):
                    act.wait_ge(sa_read, 2 * u + m + 1)
                    s = SE[u % 3][0:r, m, 0:KEYS[i]]
                    act.activation(s, s, ACT.Exp, scale=-1.0, bias=MINS[0:r, u % 3, m:m + 1], accum_out=SUMS[0:r, i, h, m:m + 1]).then_inc(ea_done, 1)

            def a_turned(u):
                i, h = UNITS[u]
                act.wait_ge(wta_done, u + 1)
                if u >= 2:
                    act.wait_ge(pva_done, u - 1)
                b = bank[4 + u % 2]
                if i < 4:
                    act.copy(WT[:, u % 2, 0:KEYS[i]], b[:, 0:KEYS[i]]).then_inc(wta_evac, 1)
                else:
                    for j in range(3):
                        w = P if j < PT else TS
                        ins = act.copy(WT[0:w, u % 2, j * P:j * P + TS], b[0:w, j * P:j * P + TS])
                    ins.then_inc(wta_evac, 1)

            def a_out(u):
                i, h = UNITS[u]
                r = ROWS[i]
                act.wait_ge(pva_done, u + 1)
                if u:
                    act.wait_ge(oa_evac, u)
                act.activation(SQ[0:r, 0:P], bank[6 + u % 2][0:r, 0:P], ACT.Square, accum_out=OS[0:r, i, h:h + 1])
                act.copy(OA[0:r, i, h * P:h * P + P], bank[6 + u % 2][0:r, 0:P]).then_inc(oa_evac, 1)

            for u in range(len(UNITS) + 3):
                if u < len(UNITS):
                    a_exp(u)
                if 2 <= u <= len(UNITS) + 1:
                    a_turned(u - 2)
                if u >= 3:
                    a_out(u - 3)

            def b_part(h, s):
                if h < HB:
                    return P, ZS[s][0], ZS[s][1], bank[3 * (h % 2) + s]
                return P if s < PT else TS, s * 512, 512, bank[3 * (h % 2) + s]

            def b_fade(h):
                for x, s in enumerate((2, 1, 0)):
                    r, o, w, b = b_part(h, s)
                    v = LK[0:r, h % 2, o:o + w]
                    act.wait_ge(abs_ready, 3 * h + x + 1)
                    act.activation(v, v, ACT.Exp, scale=-1.0).then_inc(fade_ready, 1)

            def b_log(h):
                for x, s in enumerate((2, 1, 0)):
                    r, o, w, b = b_part(h, s)
                    v = LK[0:r, h % 2, o:o + w]
                    act.wait_ge(fade_ready, 3 * h + x + 1)
                    act.activation(v, v, ACT.Ln, bias=1.0).then_inc(lk_ln, 1)

            def b_exp(h):
                for x, s in enumerate((2, 1, 0)):
                    r, o, w, b = b_part(h, s)
                    act.wait_ge(p_done, 3 * h + x + 1)
                    if h >= 2 and x == 0:
                        act.wait_ge(pvb_done, h - 1)
                    act.activation(AT[0:r, h % 2, o:o + w], b[0:r, 0:w], ACT.Exp).then_inc(eb_done, 1)

            def b_out(h):
                act.wait_ge(pvb_done, h + 1)
                if h < HB:
                    act.copy(OA[:, 0:4, 512 + h * DB:512 + h * DB + DB], bank[7][:, 0:4 * DB].rearrange("p (t d) -> p t d", d=DB)).then_inc(ob_evac, 1)
                else:
                    act.copy(OA[0:TS, 4, 512:D], bank[7][0:TS, :]).then_inc(ob_evac, 1)

            for h in range(HB + 3):
                if h <= HB:
                    b_fade(h)
                if 1 <= h <= HB + 1:
                    b_exp(h - 1)
                if h <= HB:
                    b_log(h)
                if h >= 2:
                    b_out(h - 2)

            turned(1, OT, lambda k: GA[:, k // 4:k // 4 + 1], None)
            for m in range(8):
                act.wait_ge(wo_done, m + m // 4 + 1)
                act.activation(GO[:, m, 0:TP], bank[m % 4][:, :], ACT.Identity, scale=MOD[:, 16 + m, 0:1]).then_inc(wo_act, 1)
            for t in range(NT):
                act.wait_ge(x1_ready, t + 1)
                squares(t, a_tmp + 2048, sq_done, NT + t)
            turned(2, HT, lambda k: MOD[:, 32 + k, 0:1], lambda k: MOD[:, 24 + k, 0:1])
            act.wait_ge(logit_done, 1)
            act.wait_ge(sc_clear, 1)
            act.activation(SC[:, 0:4, :], bank[5][:, 0:4 * NE].rearrange("p (t e) -> p t e", e=NE), ACT.Sigmoid)
            act.activation(SC[0:TS, 4, :], bank[5][0:TS, 4 * NE:NT * NE], ACT.Sigmoid).then_inc(sc_ready, 1)
            for t in range(NT):
                r = ROWS[t]
                b = 6 if t % 2 == 0 else 0
                act.wait_ge(h2t_done, t + 1)
                if t >= 2:
                    act.wait_ge(h2_stored[t % 2], 16 * (t // 2))
                act.copy(H2S[0:r, t % 2, 0:512], bank[b][0:r, :])
                act.copy(H2S[0:r, t % 2, 512:D], bank[b + 1][0:r, :]).then_inc(h2_evac, 1)
                act.wait_ge(h2_evac, t + 1)
                act.dma_start(h2_rows[t * P:t * P + r, :], H2S[0:r, t % 2, :]).then_inc(h2_stored[t % 2], 16)
            for s in range(2):
                act.wait_ge(g2_mm, s + 1)
                for n in range(2):
                    ins = act.copy(G2[:, s, 512 * n:512 * n + 512], bank[(4, 2)[s] + n][:, :])
                ins.then_inc(g2_ready, 1)
            act.wait_ge(h2_stored[0], 48)
            act.wait_ge(h2_stored[1], 32)
            act.activation(AE.rearrange("p f s -> p (f s)"), IDENT, ACT.Copy, scale=0.0).then_inc(ae_ready, 1)
            act.wait_ge(start_ready, 1)
            items = act.value_load(START[0:1, NE:NE + 1], min_val=1, max_val=NI)
            with act.Fori(0, items) as i:
                act.wait_ge(gu_done, i + 1)
                act.activation(SI, bank[0][:, 0:P], ACT.Silu).then_inc(silu_done, 1)
                act.wait_ge(at_done, i + 1)
                act.wait_ge(dn_done, i + 1)
                act.copy(AE.rearrange("p f s -> p (f s)"), bank[2][:, 0:P]).then_inc(ae_ready, 1)
            for m in range(2):
                act.wait_ge(sg_done, m + 1)
                act.activation(SA[:, m, 0:TP], bank[5 + m][:, :], ACT.Silu).then_inc(sg_silu, 1)
            act.wait_ge(sg_done, 5)
            act.activation(SA[:, :, TP:T], bank[4][:, 0:2 * TS].rearrange("p (m c) -> p m c", c=TS), ACT.Silu).then_inc(sg_silu, 1)
            for t in range(NT):
                act.wait_ge(fin_x, t + 1)
                squares(t, a_tmp, fin_sq, t)

        @block.vector
        def _(dve):
            n = [0]

            def chain(ins):
                n[0] += 1
                ins.then_inc(dve_s, 1)
                dve.wait_ge(dve_s, n[0])

            def mod_rows(a):
                dve.wait_ge(ada_done, a + 1)
                if a:
                    dve.wait_ge(mod_mm, a)
                dve.tensor_copy(MR, bank[6][:, :]).then_inc(mr_ready, 1)

            def mod(a):
                dve.wait_ge(mod_mm, a + 1)
                dve.scalar_tensor_tensor(out=MOD[:, 4 * a:4 * a + 4, :], in0=bank[6][:, 0:8].rearrange("p (m s) -> p m s", s=2),
                                         scalar=1.0 if a in (2, 3, 8, 9) else 0.0,
                                         in1=SMT[:, 16 + 4 * a:20 + 4 * a].unsqueeze(2).to_broadcast([P, 4, 2]), op0=ALU.add, op1=ALU.add).then_inc(mod_ready, 1)

            def means(t0, t1):
                dve.tensor_scalar(SS[:, t0:t1], SS[:, t0:t1], 1.0 / D, EPS, ALU.mult, ALU.add).then_inc(ms_ready, 1)

            def norm(t):
                r = ROWS[t]
                dve.tensor_scalar(XN[0:r, t, :], X[0:r, t, :], RS[0:r, t:t + 1], None, ALU.mult).then_inc(xn_ready, 1)

            def turned(r, dst, scale, shift):
                for k in range(0, KC, 2):
                    dve.wait_ge(tr_done, 9 * r + k + 1)
                    if shift:
                        dve.tensor_scalar(dst[:, k, 0:TP], bank[k % 4][:, :], scale(k, 0), shift(k, 0), ALU.mult, ALU.add).then_inc(tr_dve, 1)
                    else:
                        dve.tensor_scalar(dst[:, k, 0:TP], bank[k % 4][:, :], scale(k, 0), None, ALU.mult).then_inc(tr_dve, 1)
                dve.wait_ge(tr_done, 9 * r + 9)
                for k in range(KC):
                    b = bank[4][:, k * TS:k * TS + TS]
                    if shift:
                        ins = dve.tensor_scalar(dst[:, k, TP:T], b, scale(k, 1), shift(k, 1), ALU.mult, ALU.add)
                    else:
                        ins = dve.tensor_scalar(dst[:, k, TP:T], b, scale(k, 1), None, ALU.mult)
                ins.then_inc(tr_dve, 1)

            dve.memset(CT, 0.0)
            dve.memset(SUMS, 1.0)
            dve.memset(OS, 1.0)
            dve.memset(SS, 1.0).then_inc(init_ready, 1)
            dve.wait_ge(small_t, 1)
            dve.tensor_copy(SMT, bank[7][:, 0:66]).then_inc(smt_ready, 1)
            dve.wait_ge(misc_ld, 48)
            lp = LPX[0:1, :].rearrange("o (a b d) -> o a b d", b=2, d=DB)
            lm = LPM[0:1, :].rearrange("o (a d) -> o a d", d=DB)
            chain(dve.tensor_tensor(lm, lp[:, :, 0, :], lp[:, :, 1, :], ALU.mult))
            dve.tensor_reduce(LAM[0:1, :], lm, AX, ALU.add).then_inc(lam_sum, 1)
            dve.wait_ge(smt_ready, 1)
            dve.tensor_scalar(GA[:, 0:1], SMT[:, 64:65], 1.0 - LAM0, None, ALU.mult)
            dve.tensor_copy(GA[:, 1:2], SMT[:, 65:66])
            dve.wait_ge(pool_c, 1)
            chain(dve.tensor_reduce(SEL2, IDENT.rearrange("p (q s) -> p s q", s=32)[:, 0:2, :], AX, ALU.add))
            chain(dve.scalar_tensor_tensor(out=BIAS[:, 0, :], in0=BIAS[:, 0, :], scalar=-1.0, in1=BIAS[:, 0, :], op0=ALU.mult, op1=ALU.max))
            for h in (1, 2, 3):
                ins = dve.tensor_scalar(BIAS[:, h, :], BIAS[:, 0, :], 2.0 ** (-8.0 * (h + 1) / HA), None, ALU.mult)
            chain(ins)
            chain(dve.tensor_scalar(BIAS[:, 0, :], BIAS[:, 0, :], 2.0 ** (-8.0 / HA), None, ALU.mult))
            chain(dve.memset(BIAS[0:DB, :, 448:512], BIG))
            dve.wait_ge(sq_done, NT)
            means(0, NT)
            dve.wait_ge(rs_ready, 1)
            for t in range(NT):
                norm(t)
            dve.wait_ge(lam_exp, 1)
            chain(dve.tensor_scalar(LAM[0:1, 1:2], LAM[0:1, 1:2], LAM0, None, ALU.subtract))
            dve.tensor_tensor(LAM[0:1, 0:1], LAM[0:1, 1:2], LAM[0:1, 0:1], ALU.subtract).then_inc(lam_neg, 1)
            for a in range(ADA_FIRST):
                mod_rows(a)
                mod(a)
            dve.wait_ge(lam_bc, 1)
            dve.tensor_copy(NLAM, bank[7][:, 0:1]).then_inc(nlam_ready, 1)
            dve.wait_ge(mod_ready, ADA_FIRST)
            turned(0, HT, lambda k, s: MOD[:, 8 + k, s:s + 1], lambda k, s: MOD[:, k, s:s + 1])

            for n_g in (1, 3, 5):
                for t in range(NT):
                    dve.wait_ge(proj_done, 5 * n_g + t + 1)
                    if n_g == 5:
                        r = ROWS[t]
                        ins = dve.tensor_copy(V[0:r, t, 512:D], bank[t][0:r, :])
                    else:
                        dst, scale = (QT[:, 4:8], DB ** -0.5) if n_g == 3 else (KT[:, 0:4], 1.0)
                        if t < 4:
                            ins = dve.tensor_scalar(dst[:, t, 0:TP], bank[t][:, :], scale, None, ALU.mult)
                        else:
                            ins = dve.tensor_scalar(dst[:, :, TP:T], bank[4][:, 0:256].rearrange("p (m c) -> p m c", c=TS), scale, None, ALU.mult)
                    ins.then_inc(proj_dve, 1)

            def a_read(u):
                i, h = UNITS[u]
                r, k = ROWS[i], KEYS[i]
                dve.wait_ge(sa_done, u + 1)
                if u >= 3:
                    dve.wait_ge(wta_done, u - 2)
                for m in range(2):
                    dve.tensor_tensor_reduce(SE[u % 3][0:r, m, 0:k], BIAS[0:r, h, BOFF[i]:BOFF[i] + k], bank[2 * (u % 2) + m][0:r, 0:k], 1.0, 3e38,
                                             ALU.add, ALU.min, MINS[0:r, u % 3, m:m + 1]).then_inc(sa_read, 1)

            def a_weights(u):
                i, h = UNITS[u]
                r, k = ROWS[i], KEYS[i]
                dve.wait_ge(ea_done, 2 * u + 2)
                co = CO[0:r, u % 3, :]
                chain(dve.reciprocal(co, SUMS[0:r, i, h, 1:2]))
                chain(dve.tensor_scalar(co, co, SUMS[0:r, i, h, 0:1], NLAM[0:r, :], ALU.mult, ALU.mult))
                dve.scalar_tensor_tensor(out=SE[u % 3][0:r, 1, 0:k], in0=SE[u % 3][0:r, 1, 0:k], scalar=co, in1=SE[u % 3][0:r, 0, 0:k],
                                         op0=ALU.mult, op1=ALU.add).then_inc(wa_ready, 1)

            for u in range(len(UNITS) + 1):
                if u < len(UNITS):
                    a_read(u)
                if u >= 1:
                    a_weights(u - 1)

            def b_part(h, s):
                if h < HB:
                    return P, ZS[s][0], ZS[s][1], bank[3 * (h % 2) + s]
                return P if s < PT else TS, s * 512, 512, bank[3 * (h % 2) + s]

            def b_abs(h):
                for x, s in enumerate((2, 1, 0)):
                    r, o, w, b = b_part(h, s)
                    dve.wait_ge(z_done, 3 * h + x + 1)
                    if h >= 2 and x == 0:
                        dve.wait_ge(p_done, 3 * (h - 1))
                    dve.tensor_scalar(LK[0:r, h % 2, o:o + w].bitcast(I32), b[0:r, 0:w].bitcast(I32), 0x7FFFFFFF, None,
                                      ALU.bitwise_and).then_inc(abs_ready, 1)

            def b_keep(h):
                for x, s in enumerate((2, 1, 0)):
                    r, o, w, b = b_part(h, s)
                    v = LK[0:r, h % 2, o:o + w]
                    dve.wait_ge(lk_ln, 3 * h + x + 1)
                    ins = dve.scalar_tensor_tensor(out=v, in0=b[0:r, 0:w], scalar=0.0, in1=v, op0=ALU.max, op1=ALU.add)
                    if h < HB:
                        chain(ins)
                        for c in [ZO[j] for j in ([0], [1], [2, 3])[s]]:
                            d = LK[:, h % 2, c:c + P]
                            ins = dve.tensor_tensor(d, d, UP, ALU.mult)
                    elif s == 2:
                        chain(ins)
                        d = v.rearrange("p (h q) -> p h q", q=TS)
                        ins = dve.tensor_tensor(d, d, UP[0:TS, 0:TS].unsqueeze(1).to_broadcast([TS, HB, TS]), ALU.mult)
                    ins.then_inc(lk_ready, 1)

            def a_mean():
                dve.wait_ge(oa_evac, len(UNITS))
                s0 = SUMS[:, :, :, 0]
                chain(dve.scalar_tensor_tensor(out=s0, in0=s0, scalar=EPS * P, in1=s0, op0=ALU.mult, op1=ALU.mult))
                chain(dve.tensor_tensor(OS[:, :, 0:HA], OS[:, :, 0:HA], s0, ALU.add))
                dve.tensor_scalar(OS[:, :, 0:HA], OS[:, :, 0:HA], 1.0 / P, None, ALU.mult).then_inc(osa_ready, 1)

            def a_norm(t):
                dve.wait_ge(ora_ready, 1)
                r = ROWS[t]
                a = OA[0:r, t, 0:512].rearrange("p (h d) -> p h d", d=P)
                dve.tensor_tensor(a, a, OR[0:r, t, 0:HA].unsqueeze(2).to_broadcast([r, HA, P]), ALU.mult).then_inc(on_ready, 1)

            def b_heads(h):
                return OA[:, 0:4, 512 + h * DB:512 + h * DB + DB] if h < HB else OA[0:TS, 4, 512:D].rearrange("p (h d) -> p h d", d=DB)

            def b_mean(h):
                dve.wait_ge(ob_evac, h + 1)
                o, m = b_heads(h), b_stat(OS, h)
                sq = (SQ[:, 0:4 * DB] if h < HB else SQ[0:TS, :]).rearrange("p (h d) -> p h d", d=DB)
                chain(dve.tensor_tensor(sq, o, o, ALU.mult))
                chain(dve.tensor_reduce(m, sq, AX, ALU.add))
                dve.tensor_scalar(m, m, 1.0 / DB, EPS, ALU.mult, ALU.add).then_inc(osb_ready, 1)

            def b_norm(h):
                dve.wait_ge(orb_ready, h + 1)
                o = b_heads(h)
                dve.tensor_tensor(o, o, b_stat(OR, h).unsqueeze(2).to_broadcast([P, 4, DB] if h < HB else [TS, HB, DB]), ALU.mult).then_inc(on_ready, 1)

            for b, c in enumerate((4, 3, 3)):
                dve.wait_ge(ko_stored[b], 16 * c)
            for h in range(HB + 1):
                b_abs(h)
                if h:
                    mod(ADA_FIRST + h - 1)
                b_keep(h)
                if h < HB:
                    mod_rows(ADA_FIRST + h)
                if h == 0:
                    a_mean()
                if 2 <= h < 2 + NT:
                    a_norm(h - 2)
                if h >= 3:
                    b_mean(h - 3)
                if h >= 4:
                    b_norm(h - 4)
            b_mean(HB - 2)
            b_norm(HB - 3)
            b_mean(HB - 1)
            b_norm(HB - 2)
            b_norm(HB - 1)
            b_mean(HB)
            b_norm(HB)

            turned(1, OT, lambda k, s: GA[:, k // 4:k // 4 + 1], None)
            for g in range(2):
                dve.wait_ge(wo_done, 5 * g + 5)
                dve.tensor_tensor(GO[:, 4 * g:4 * g + 4, TP:T], bank[4 + g][:, 0:256].rearrange("p (m c) -> p m c", c=TS),
                                  MOD[:, 16 + 4 * g:20 + 4 * g, 1:2].to_broadcast([P, 4, TS]), ALU.mult).then_inc(wo_dve, 1)
            dve.wait_ge(new_stored, 64)
            for t in range(NT):
                r = ROWS[t]
                b = 6 if t % 2 == 0 else 0
                dve.wait_ge(got_done, t + 1)
                dve.tensor_tensor(X[0:r, t, 0:512], bank[b][0:r, :], X[0:r, t, 0:512], ALU.add)
                dve.tensor_tensor(X[0:r, t, 512:D], bank[b + 1][0:r, :], X[0:r, t, 512:D], ALU.add).then_inc(x1_ready, 1)
                if t >= 1:
                    dve.wait_ge(sq_done, NT + t)
                    means(t - 1, t)
                    dve.wait_ge(rs_ready, 1 + t)
                    norm(t - 1)
            dve.wait_ge(sq_done, 2 * NT)
            means(4, 5)
            dve.wait_ge(rs_ready, 1 + NT)
            norm(4)
            turned(2, HT, lambda k, s: MOD[:, 32 + k, s:s + 1], lambda k, s: MOD[:, 24 + k, s:s + 1])

            dve.wait_ge(logit_done, 1)
            dve.memset(GS, -3e38)
            dve.memset(GREP, -3e38)
            dve.memset(SELX, -3e38)
            dve.memset(EREP, -3e38)
            dve.memset(SC, 0.5).then_inc(sc_clear, 1)
            dve.wait_ge(sc_ready, 1)
            chain(dve.tensor_tensor(SEL, SC, BR.unsqueeze(1).to_broadcast([P, NT, NE]), ALU.add))
            for t in range(NT):
                for g in range(NG):
                    last = dve.max(G8[:, t * NG + g, :], SEL[:, t, g * EG:g * EG + EG])
            chain(last)
            g8 = G8.rearrange("p (t g) e -> p t g e", g=NG)
            chain(dve.tensor_tensor(GS[:, :, 0:NG], g8[:, :, :, 0], g8[:, :, :, 1], ALU.add))
            for t in range(NT):
                last = dve.max(GTOP[:, t, :], GS[:, t, :])
            chain(last)
            chain(dve.tensor_copy(GREP[:, :, 0:TOPG], GTOP[:, :, 0:TOPG]))
            for t in range(NT):
                last = dve.match_replace(GOUT[:, t, :], GREP[:, t, :], GS[:, t, :], 3e38)
            chain(last)
            chain(dve.tensor_scalar(KEEP, GOUT[:, :, 0:NG], 3e38, None, ALU.is_equal))
            chain(dve.tensor_scalar(NEGK, KEEP, 1.0, BIG, ALU.subtract, ALU.mult))
            for t in range(NT):
                v = SELX[:, t, 0:NE].rearrange("p (g e) -> p g e", e=EG)
                last = dve.tensor_tensor(v, SEL[:, t, :].rearrange("p (g e) -> p g e", e=EG), KEEP[:, t, :].unsqueeze(2).to_broadcast([P, NG, EG]), ALU.mult)
            chain(last)
            for t in range(NT):
                v = SELX[:, t, 0:NE].rearrange("p (g e) -> p g e", e=EG)
                last = dve.tensor_tensor(v, v, NEGK[:, t, :].unsqueeze(2).to_broadcast([P, NG, EG]), ALU.add)
            chain(last)
            for t in range(NT):
                last = dve.max(ETOP[:, t, :], SELX[:, t, :])
            chain(last)
            chain(dve.tensor_copy(EREP[:, :, 0:TOPK], ETOP[:, :, 0:TOPK]))
            for t in range(NT):
                last = dve.match_replace(EOUT[:, t, :], EREP[:, t, :], SELX[:, t, :], 3e38)
            chain(last)
            chain(dve.tensor_scalar(M, EOUT[:, :, 0:NE], 3e38, None, ALU.is_equal))
            dve.memset(M[DB:P, 4, :], 0.0).then_inc(mask_ready, 1)
            dve.wait_ge(pos_done, 1)
            chain(dve.tensor_scalar(NB_I, bank[7][:, 0:NE], float(SLOT - 1), None, ALU.add))
            chain(dve.tensor_scalar(NB_J, NB_I, 6, None, ALU.logical_shift_right))
            dve.memset(ZE, 0.0)
            chain(dve.tensor_scalar(NB, NB_J, 1.0, None, ALU.max))
            chain(dve.tensor_tensor_scan(INC, NB, ZE, 0.0, ALU.add, ALU.add))
            chain(dve.tensor_tensor(STF[:, 0:NE], INC, NB, ALU.subtract))
            chain(dve.tensor_copy(STF[:, NE:NE + 1], INC[:, NE - 1:NE]))
            dve.tensor_copy(START[:, 0:NE + 1], STF[:, 0:NE + 1]).then_inc(start_ready, 1)
            chain(dve.tensor_scalar(SB, STF[:, 0:NE], float(SLOT), float(SLOT + 1), ALU.mult, ALU.add))
            chain(dve.tensor_tensor(SL, bank[6][:, 0:NT * NE].rearrange("p (t e) -> p t e", e=NE), SB.unsqueeze(1).to_broadcast([P, NT, NE]), ALU.add))
            chain(dve.tensor_tensor(SL, SL, M, ALU.mult))
            for t in range(NT):
                last = dve.max(S8[:, t, :], SL[:, t, :])
            chain(last)
            chain(dve.tensor_scalar(SIDX, S8, 1.0, None, ALU.subtract))
            dve.tensor_scalar(COLI, SIDX, 6, None, ALU.logical_shift_right)
            chain(dve.tensor_scalar(PLI, SIDX, SLOT - 1, None, ALU.bitwise_and))
            dve.tensor_copy(COLF, COLI)
            chain(dve.tensor_copy(PLF, PLI))
            dve.memset(ICUR, 0).then_inc(sidx_ready, 1)
            dve.wait_ge(rec_ready, 1)
            for u in range(NT * TOPK):
                t, k = divmod(u, TOPK)
                if u >= 4:
                    dve.wait_ge(oh_done, u - 3)
                dve.tensor_scalar(OHP[u % 4], PLACES, PLF[:, t, k:k + 1], RECF[:, t, k:k + 1], ALU.is_equal, ALU.mult).then_inc(ohp_ready, 1)
            dve.wait_ge(h2_stored[0], 48)
            dve.wait_ge(h2_stored[1], 32)
            dve.memset(YO, 0.0).then_inc(yo_ready, 1)
            dve.wait_ge(oh_done, NT * TOPK)
            dve.tensor_scalar(IDX[0:SLOT, 1, :], bank[7][0:SLOT, 0:IC], float(NONE), None, ALU.add)
            chain(dve.tensor_scalar(IDX[SLOT:P, 1, :], bank[7][SLOT:P, 0:IC], float(NONE + 1), None, ALU.add))
            chain(dve.tensor_scalar(IDX[:, 0, :], IDX[:, 1, :], 4, 1, ALU.logical_shift_right, ALU.logical_shift_left))
            dve.tensor_scalar(IDX[SLOT:P, 0, :], IDX[SLOT:P, 0, :], 1, None, ALU.bitwise_or).then_inc(idx_ready, 1)

            hgt = HGT.rearrange("p c h s -> p (c h s)")
            dve.wait_ge(hgt_done, 1)
            dve.tensor_copy(hgt, bank[1][:, :]).then_inc(hgt_ready, 1)
            items = dve.value_load(START[0:1, NE:NE + 1], min_val=1, max_val=NI)

            def out_rows(i):
                dve.wait_ge(dn_done, i + 1)
                dve.wait_ge(scattered, (i + 1) * 16)
                dve.tensor_copy(YO, bank[3][:, :]).then_inc(yo_ready, 1)

            with dve.Fori(0, items) as i:
                dve.wait_ge(silu_done, i + 1)
                dve.tensor_tensor(AC, SI, bank[0][:, P:2 * P], ALU.mult).then_inc(ac_ready, 1)
                dve.wait_ge(hgt_done, i + 2)
                dve.tensor_copy(hgt, bank[1][:, :]).then_inc(hgt_ready, 1)
                out_rows(i)
            out_rows(items)

            chain(dve.tensor_tensor(COMB, SC, M, ALU.mult))
            chain(dve.tensor_reduce(DEN, COMB, AX, ALU.add))
            chain(dve.tensor_scalar(DEN, DEN, 1e-38, None, ALU.max))
            chain(dve.reciprocal(RDEN, DEN))
            chain(dve.tensor_scalar(RDEN, RDEN, 2.5, None, ALU.mult))
            chain(dve.tensor_tensor(COMB, COMB, RDEN.unsqueeze(2).to_broadcast([P, NT, NE]), ALU.mult))
            for t in range(NT):
                for k in range(TOPK):
                    ins = dve.scalar_tensor_tensor(out=EJ[:, k, :], in0=SL[:, t, :], scalar=S8[:, t, k:k + 1], in1=COMB[:, t, :],
                                                   op0=ALU.is_equal, op1=ALU.mult, accum_out=W6[:, t, k:k + 1])
                chain(ins)

            def finish(t):
                r = ROWS[t]
                dve.wait_ge(fin_sq, t + 1)
                dve.tensor_scalar(SS[:, t:t + 1], SS[:, t:t + 1], 1.0 / D, EPS, ALU.mult, ALU.add).then_inc(fin_ms, 1)
                dve.wait_ge(fin_rs, t + 1)
                dve.scalar_tensor_tensor(out=X[0:r, t, :], in0=X[0:r, t, :], scalar=RS[0:r, t:t + 1], in1=GF[0:r, :], op0=ALU.mult, op1=ALU.mult).then_inc(y_ready, 1)

            def routed(t):
                r = ROWS[t]
                parts = YB[t % 3]
                dve.wait_ge(yb_ld[t % 3], 16 * len(parts) * (t // 3 + 1))
                acc = parts[0][1][0:r, 0, :]
                chain(dve.tensor_scalar(acc, acc, W6[0:r, t, 0:1], None, ALU.mult))
                for first, part in parts:
                    for k in range(max(first, 1), first + part.shape[1]):
                        chain(dve.scalar_tensor_tensor(out=acc, in0=part[0:r, k - first, :], scalar=W6[0:r, t, k:k + 1], in1=acc, op0=ALU.mult, op1=ALU.add))

            def shared(t):
                r = ROWS[t]
                acc = YB[t % 3][0][1][0:r, 0, :]
                dve.wait_ge(sd_done, t + 1)
                for n in range(2):
                    a = acc[:, 512 * n:512 * n + 512]
                    ins = dve.tensor_tensor(a, a, bank[SDB[t][n]][0:r, :], ALU.add)
                ins.then_inc(acc_ready, 1)

            routed(0)
            for f in range(2):
                dve.wait_ge(sg_silu, f + 1)
                dve.wait_ge(sg_done, 3 + f)
                dve.tensor_tensor(SA[:, f, 0:TP], SA[:, f, 0:TP], bank[(7, 2)[f]][:, :], ALU.mult)
            dve.wait_ge(sg_silu, 3)
            dve.tensor_tensor(SA[:, :, TP:T], SA[:, :, TP:T], bank[4][:, 2 * TS:4 * TS].rearrange("p (m c) -> p m c", c=TS), ALU.mult).then_inc(as_ready, 1)
            dve.wait_ge(gf_ld, 16)
            for t in range(NT):
                if t:
                    routed(t)
                shared(t)
                if t == 0:
                    dve.wait_ge(acc_ready, 1)
                    dve.sem_inc(sd_read)
                if t:
                    finish(t - 1)
            finish(NT - 1)


_INS = ["x_prompt", "x_sample", "cache_a_k", "cache_a_v", "cache_b_k", "cache_b_v", "c_prompt", "c_sample", "w_ada", "b_ada",
        "w_in", "lam_params", "g_sub_a", "g_sub_b", "w_out", "w_router", "b_router", "w_gate", "w_up", "w_down",
        "w_shared_gate", "w_shared_up", "w_shared_down", "g_final"]
_OUTS = [(1, TP, D), (1, TS, D), (1, 1, TP, HA, P), (1, 1, TP, HA, P), (1, 1, TP, HB, DB), (1, 1, TP, HB, DB),
         (1, 1, TS, HA, P), (1, 1, TS, HA, P), (1, 1, TS, HB, DB), (1, 1, TS, HB, DB)]


def kernel(**inputs):
    import numpy as np
    import concourse.bacc as bacc
    from concourse.bass_utils import run_bass_kernel_spmd

    nc = bacc.Bacc("TRN2", target_bir_lowering=False, num_devices=1)
    arrays, args = {}, []
    for name in _INS:
        a = np.ascontiguousarray(inputs[name])
        arrays[f"in_{name}"] = a
        args.append(nc.dram_tensor(f"in_{name}", a.shape, F32, kind="ExternalInput").ap())
    for i, shape in enumerate(_OUTS):
        args.append(nc.dram_tensor(f"out_{i}", shape, F32, kind="ExternalOutput").ap())
    build(nc, *args)
    r = run_bass_kernel_spmd(nc, [arrays], core_ids=[0])
    return tuple(r.results[0][f"out_{i}"] for i in range(len(_OUTS)))
```

```python
from contextlib import ExitStack

import concourse.bass as bass
from concourse import mybir

F32 = mybir.dt.float32
I32 = mybir.dt.int32
U32 = mybir.dt.uint32
ALU = mybir.AluOpType
ACT = mybir.ActivationFunctionType
AX = mybir.AxisListType.X

P = 128
D = 1024
KC = D // P
TP, TS = 512, 64
T = TP + TS
TH = T // 2
NT = TP // P + 1
ROWS = [P, P, P, P, TS]
PAST = 256
PT = PAST // P
HA, HB = 4, 8
DB = 64
NE, NG, EG = 64, 8, 8
TOPK, TOPG = 6, 4
FE = 256
EPS = 1e-6
BIG = 1e30
LAM0 = 0.8 - 0.6
ADA_FIRST = 4
SLOT = 64
NI = NE + T * TOPK // SLOT
IC = NI + 4
YK = 8
NONE = 1 << 14


def build(nc, x_prompt, x_sample, cache_a_k, cache_a_v, cache_b_k, cache_b_v, c_prompt, c_sample, w_ada, b_ada,
          w_in, lam_params, g_sub_a, g_sub_b, w_out, w_router, b_router, w_gate, w_up, w_down, w_sg, w_su, w_sd,
          g_final, y_prompt, y_sample, ak_p, av_p, bk_p, bv_p, ak_s, av_s, bk_s, bv_s):
    ctx = ExitStack()
    with ctx:
        sem = lambda name: ctx.enter_context(nc.semaphore(name))

        N_ARENA = 53000
        arena = ctx.enter_context(nc.sbuf_tensor("arena", [P, N_ARENA], F32))
        bank = [ctx.enter_context(nc.psum_tensor(f"bank{i}", [P, 512], F32)) for i in range(8)]
        top = [0]

        def take(n):
            top[0] += n
            assert top[0] <= N_ARENA, top[0]
            return top[0] - n

        def at(base, *shape, dt=F32):
            n = 1
            for s in shape:
                n *= s
            v = arena[:, base:base + n]
            if dt != F32:
                v = v.bitcast(dt)
            if len(shape) == 2:
                v = v.rearrange("p (a b) -> p a b", b=shape[1])
            elif len(shape) == 3:
                v = v.rearrange("p (a b c) -> p a b c", b=shape[1], c=shape[2])
            return v

        a_x = take(NT * D)
        a_h = take(NT * D)
        a_ring = take(3 * 4096)
        a_att = take(KC * T * 2 + KC * PAST + NT * D + PT * D)
        a_tmp = take(7168)
        X = at(a_x, NT, D)
        HT = at(a_h, KC, T)
        OA = at(a_h, NT, D)
        RING = [at(a_ring + 4096 * i, KC, 512) for i in range(3)]
        QT = at(a_att, KC, T)
        OT = QT
        a_kt = a_att + KC * T
        KT = at(a_kt, KC, T)
        a_ckt = a_kt + KC * T
        CKT = at(a_ckt, KC, PAST)
        a_v = a_ckt + KC * PAST
        V = at(a_v, NT, D)
        XN = V
        CV = at(a_v + NT * D, PT, D)
        BIAS = at(a_tmp, HA, 512)
        KO = [at(a_tmp + o, 512) for o in (2048, 2560, 3072, 5632, 6144, 6656)]
        CK = at(a_tmp + 3584, PT, D)
        SE = [at(a_tmp + 3584, 2, 512), at(a_tmp + 4608, 2, 512), at(take(1024), 2, 512)]
        WT = at(a_tmp + 5632, 2, 512)
        LK = at(a_tmp, 2, 1536)
        LS = at(a_tmp + 6144, 3, P)
        AT = at(a_tmp + 3072, 2, 1536)
        H2S = at(a_tmp, NT, D)
        SA = at(a_tmp + 2048, 2, T)
        GU = [RING[0], RING[1], RING[2], at(a_att, KC, 512)]
        DN = [at(a_att + 4096 + 2048 * i, 2, D) for i in (3, 0, 1, 2)]
        WSG, WSD = GU[0], DN[0]
        HG = [at(a_tmp + 512 * i, 512) for i in range(2)]
        YO = [at(a_tmp + 1024 + 512 * i, 512) for i in range(2)]
        HGT = at(a_tmp + 2048, 4, 2, SLOT)
        HGS = at(a_tmp + 2560, 512)
        SI = at(a_tmp + 4224, P)
        AC = at(a_tmp + 4352, P)
        AE = at(a_tmp + 4480, 2, SLOT)
        G1 = at(a_tmp + 5120, 2, D)
        G2 = at(a_tmp + 5120, 2, D)
        GF = at(a_tmp + 3200, D)
        IDENT = at(take(P), P)
        NTRI = at(take(P), P)
        NONES = at(take(P), P)
        UP = at(take(P), P)
        ONES = at(take(P), P)
        SMT = at(take(66), 66)
        CT = at(take(KC * 32), KC, 32)
        MR = at(take(512), 512)
        SEL2 = at(take(2), 2)
        MOD = at(take(96), 48, 2)
        WR = at(take(KC * NE), KC, NE)
        BR = at(take(NE), NE)
        SQ = at(take(512), 512)
        GA = at(take(2), 2)
        SS = at(take(NT), NT)
        RS = at(take(NT), NT)
        HALF = at(take(60), NT, 12)
        SUMS = at(take(NT * HA * 2), NT, HA, 2)
        MINS = at(take(6), 3, 2)
        CO = at(take(3), 3, 1)
        OS = at(take(60), NT, 12)
        OR = at(take(60), NT, 12)
        LAM = at(take(2), 2)
        NLAM = at(take(1), 1)
        SMALL = at(take(P), P)
        IDX = at(take(2 * IC), 2, IC, dt=U32)
        ICUR = at(take(4), 4, dt=U32)
        START = at(take(NE + 2), NE + 2, dt=I32)
        W6 = at(take(NT * YK), NT, YK)
        LPX = at(take(256), 256)
        LPM = at(take(128), 128)
        r0 = [a_att + 4096 + 4 * 2048]

        def rt(*shape, dt=F32):
            n = 1
            for s in shape:
                n *= s
            r0[0] += n
            assert r0[0] <= a_tmp
            return at(r0[0] - n, *shape, dt=dt)

        SC = rt(NT, NE)
        SEL = rt(NT, NE)
        G8 = rt(NT * NG, 8)
        GS = rt(NT, 12)
        GTOP = rt(NT, 8)
        GREP = rt(NT, 8)
        GOUT = rt(NT, 12)
        KEEP = rt(NT, NG)
        NEGK = rt(NT, NG)
        SELX = rt(NT, NE + 2)
        ETOP = rt(NT, 8)
        EREP = rt(NT, 8)
        EOUT = rt(NT, NE + 2)
        M = rt(NT, NE)
        LT = at(a_tmp + 6144, 256 + TS)
        MS = at(a_tmp + 5120, NT + 1, NE)
        COMB = rt(NT, NE)
        DEN = rt(NT)
        RDEN = rt(NT)
        NB_I = rt(NE, dt=I32)
        NB_J = rt(NE, dt=I32)
        NB = rt(NE)
        ZE = rt(NE)
        INC = rt(NE)
        STF = rt(NE + 2)
        SB = rt(NE)
        SL = rt(NT, NE)
        S8 = rt(NT, 8)
        SIDX = rt(NT, 8, dt=I32)
        COLI = rt(NT, 8, dt=I32)
        PLI = rt(NT, 8, dt=I32)
        COLF = rt(NT, 8)
        PLF = rt(NT, 8)
        RECI = rt(NT, 8, dt=I32)
        RECF = rt(NT, 8)
        ITEMS = rt(IC)
        PLACES = rt(SLOT)
        oh_base = r0[0]
        OHI = [rt(TOPK, IC) for _ in range(2)]
        OHP = [rt(TOPK, SLOT) for _ in range(2)]
        EJ = at(a_tmp + 4736, TOPK, NE)
        YB = [[(0, at(a_ring + 4096, TOPK, D))],
              [(0, at(a_att, TOPK, D))],
              [(0, at(a_ring + 10240, 2, D)), (2, at(a_att + 6144, 4, D))],
              [(0, at(a_ring, 4, D)), (4, at(a_tmp, 2, D))],
              [(0, at(a_h, 5, D)), (5, at(oh_base, 1, D))]]

        h2_rows = nc.dram_tensor("h2_rows", (T, D), F32, kind="Internal").ap()
        y_rows = nc.dram_tensor("y_rows", (T * YK, D), F32, kind="Internal").ap()

        pe_mark, pool_mark = sem("pe_mark"), sem("pool_mark")
        small_ld, x_ld, lam_ld, router_ld, ck_ld, cv_ld, sh_ld = map(sem, ("small_ld", "x_ld", "lam_ld", "router_ld", "ck_ld", "cv_ld", "sh_ld"))
        ring_ld = [sem(f"ring_ld{i}") for i in range(3)]
        pool_c, pool_s, dve_s, act_s = map(sem, ("pool_c", "pool_s", "dve_s", "act_s"))
        small_t, smt_ready, c_ready = map(sem, ("small_t", "smt_ready", "c_ready"))
        lam_sum, lam_exp, lam_neg, lam_bc, nlam_ready = map(sem, ("lam_sum", "lam_exp", "lam_neg", "lam_bc", "nlam_ready"))
        ada_done, mr_ready, mod_mm, mod_ready = map(sem, ("ada_done", "mr_ready", "mod_mm", "mod_ready"))
        sq_done, ms_ready, rs_ready, xn_ready = map(sem, ("sq_done", "ms_ready", "rs_ready", "xn_ready"))
        tr_done, tr_dve, tr_act = map(sem, ("tr_done", "tr_dve", "tr_act"))
        proj_done, proj_act, proj_dve = map(sem, ("proj_done", "proj_act", "proj_dve"))
        kb_done, kb_evac, new_stored = map(sem, ("kb_done", "kb_evac", "new_stored"))
        ko_stored = [sem(f"ko_stored{i}") for i in range(6)]
        h2_stored = sem("h2_stored")
        sa_done, sa_read, ea_done, wa_ready, wta_done, wta_evac, pva_done, oa_evac = map(
            sem, ("sa_done", "sa_read", "ea_done", "wa_ready", "wta_done", "wta_evac", "pva_done", "oa_evac"))
        z_half = sem("z_half")
        abs_ready, fade_ready, ls_ready, z_done, lk_ready, p_done, eb_done, at_ready, pvb_done, ob_evac, lk_ln = map(
            sem, ("abs_ready", "fade_ready", "ls_ready", "z_done", "lk_ready", "p_done", "eb_done", "at_ready", "pvb_done", "ob_evac", "lk_ln"))
        osa_ready, ora_ready, osb_ready, orb_ready, on_ready = map(sem, ("osa_ready", "ora_ready", "osb_ready", "orb_ready", "on_ready"))
        g1_mm, g1_ready, wo_done, x1_part, x1_ready = map(sem, ("g1_mm", "g1_ready", "wo_done", "x1_part", "x1_ready"))
        lt_done, lt_evac, logit_done, sc_ready, h2t_done, h2_evac = map(sem, ("lt_done", "lt_evac", "logit_done", "sc_ready", "h2t_done", "h2_evac"))
        sg_done, sg_silu, as_ready, sd_done = map(sem, ("sg_done", "sg_silu", "as_ready", "sd_done"))
        mask_ready, pos_done, start_ready, sidx_ready, rec_ready, ohi_ready, ohi_rest, ohp_ready, oh_done, idx_ready = map(
            sem, ("mask_ready", "pos_done", "start_ready", "sidx_ready", "rec_ready", "ohi_ready", "ohi_rest", "ohp_ready", "oh_done", "idx_ready"))
        g2_mm, g2_ready = sem("g2_mm"), sem("g2_ready")
        exp_ld = [sem(f"exp_ld{i}") for i in range(4)]
        gathered = [sem(f"gathered{i}") for i in range(2)]
        scattered = [sem(f"scattered{i}") for i in range(2)]
        cur_tok, cur_row, hgt_done, hgt_ready, gu_done, silu_done, ac_ready, at_done, ae_ready, dn_done, yo_ready, \
            hg_staged = map(sem, ("cur_tok", "cur_row", "hgt_done", "hgt_ready", "gu_done", "silu_done", "ac_ready", "at_done",
                                  "ae_ready", "dn_done", "yo_ready", "hg_staged"))
        gf_ld, yb_first, w6_ready, acc_ready, fin_sq, fin_ms, fin_rs, y_ready, y_stored, fin_g2, fin_x, fin_last, init_ready, sc_clear = map(
            sem, ("gf_ld", "yb_first", "w6_ready", "acc_ready", "fin_sq", "fin_ms", "fin_rs", "y_ready", "y_stored", "fin_g2", "fin_x", "fin_last",
                  "init_ready", "sc_clear"))
        yb_ld = [sem(f"yb_ld{i}") for i in range(NT)]

        block = ctx.enter_context(nc.Block())

        def kp(w):
            return w.rearrange("(k p) n -> p k n", p=P)

        ada_v, in_v, out_v = kp(w_ada[0]), kp(w_in[0]), kp(w_out[0])
        cols = lambda v, n: v[:, :, 512 * n:512 * n + 512]
        groups = [[(cols(ada_v, n), 0, 512)] for n in range(ADA_FIRST)]
        G_IN = len(groups)
        groups += [[(cols(in_v, n), 0, 512)] for n in range(6)]
        G_ADA = len(groups)
        groups += [[(cols(ada_v, n), 0, 512)] for n in range(ADA_FIRST, 12)]
        G_OUT = len(groups)
        groups += [[(cols(out_v, n), 0, 512)] for n in range(2)]

        def ring_count(g):
            return sum(16 * len(groups[i]) for i in range(g % 3, g + 1, 3))

        def used(g):
            if g < G_IN:
                return ada_done, g + 1
            if g < G_ADA:
                return proj_done, 5 * (g - G_IN + 1)
            return ada_done, ADA_FIRST + g - G_ADA + 1

        KEYS = [P, 2 * P, 3 * P, 4 * P, PAST + TS]
        BOFF = [384, 256, 128, 0, 128]
        UNITS = [(i, h) for i in range(NT) for h in range(HA)]
        ZO = [0, 512, 896, 1152]
        ZW = [512, 384, 256, 128]
        ZS = [(0, 512), (512, 384), (896, 384)]

        def zbank(h, j):
            b = 3 * (h % 2) + min(j, 2)
            o = 256 if j == 3 else 0
            return bank[b][:, o:o + ZW[j]]

        WOB = [(0, 1), (2, 3), (5, 6), (0, 1)]
        SGB = [(5, 6), (7, 2), (4, 0), (1, 3)]
        SDB = [(0, 1), (3, 5), (6, 7), (2, 4), (0, 1)]

        def b_stat(v, h):
            return v[:, 0:4, HA + h] if h < HB else v[0:TS, 4, HA:HA + HB]

        @block.sync
        def _(sp):
            sp.dma_start(SMALL[0:8, :], c_prompt.rearrange("b (k p) -> (b k) p", p=P)).then_inc(small_ld, 16)
            sp.dma_start(SMALL[8:16, :], c_sample.rearrange("b (k p) -> (b k) p", p=P)).then_inc(small_ld, 16)
            sp.dma_start(SMALL[16:64, :], b_ada.rearrange("b (k p) -> (b k) p", p=P)).then_inc(small_ld, 16)
            sp.dma_start(SMALL[64:65, :], g_sub_a).then_inc(small_ld, 16)
            sp.dma_start(SMALL[65:66, 0:DB], g_sub_b).then_inc(small_ld, 16)
            sp.dma_start(SMALL[65:66, DB:P], g_sub_b).then_inc(small_ld, 16)
            sp.dma_start(X[:, 0:4, :], x_prompt[0].rearrange("(t p) d -> p t d", p=P)).then_inc(x_ld, 16)
            sp.dma_start(X[0:TS, 4, :], x_sample[0]).then_inc(x_ld, 16)
            sp.dma_start(LPX[0:1, :], lam_params.rearrange("l a d -> l (a d)")).then_inc(lam_ld, 16)
            for g, parts in enumerate(groups):
                if g == G_IN + 2:
                    sp.dma_start(WR, kp(w_router[0])).then_inc(router_ld, 16)
                    sp.dma_start(BR, b_router.to_broadcast([P, NE])).then_inc(router_ld, 16)
                    sp.dma_start(CK[:, :, 0:512], cache_a_k[0, 0].rearrange("(j p) h d -> p j (h d)", p=P)).then_inc(ck_ld, 16)
                    sp.dma_start(CK[:, :, 512:D], cache_b_k[0, 0].rearrange("(j p) h d -> p j (h d)", p=P)).then_inc(ck_ld, 16)
                    sp.dma_start(CV[:, :, 0:512], cache_a_v[0, 0].rearrange("(j p) h d -> p j (h d)", p=P)).then_inc(cv_ld, 16)
                    sp.dma_start(CV[:, :, 512:D], cache_b_v[0, 0].rearrange("(j p) h d -> p j (h d)", p=P)).then_inc(cv_ld, 16)
                if g == G_ADA + 2:
                    sp.wait_ge(oa_evac, 1)
                if g >= 3:
                    sp.wait_ge(*used(g - 3))
                for view, a, b in parts:
                    sp.dma_start(RING[g % 3][:, :, a:b], view).then_inc(ring_ld[g % 3], 16)
            def load_wide(e, j):
                sp.dma_start(GU[j][:, :, 0:FE], w_gate[0, bass.ds(e, 1)].rearrange("e (k p) n -> p (e k) n", p=P)).then_inc(exp_ld[j], 16)
                sp.dma_start(GU[j][:, :, FE:2 * FE], w_up[0, bass.ds(e, 1)].rearrange("e (k p) n -> p (e k) n", p=P)).then_inc(exp_ld[j], 16)

            def load_down(e, j):
                sp.dma_start(DN[j], w_down[0, bass.ds(e, 1)].rearrange("e (f p) n -> p (e f) n", p=P)).then_inc(exp_ld[j], 16)

            sp.wait_ge(wo_done, NT)
            for j in range(4):
                load_wide(j, j)
            sp.wait_ge(tr_done, 27)
            sp.wait_ge(h2_stored, 16 * NT)
            for j in range(4):
                load_down(j, j)
            sp.wait_ge(start_ready, 1)

            def refill(e, j, down):
                first = sp.value_load(START[0:1, bass.ds(e + 1, 1)], min_val=1, max_val=NI)
                sp.wait_ge(gu_done, first)
                load_wide(e + 4, j)
                if down:
                    first = sp.value_load(START[0:1, bass.ds(e, 1)], min_val=1, max_val=NI)
                    sp.wait_ge(dn_done, first + 1)
                    load_down(e + 3, (j + 3) % 4)

            for j in range(4):
                refill(j, j, j > 0)
            with sp.Fori(0, NE // 4 - 2) as g:
                for j in range(4):
                    refill(g * 4 + (j + 4), j, True)
            first = sp.value_load(START[0:1, NE - 4:NE - 3], min_val=1, max_val=NI)
            sp.wait_ge(dn_done, first + 1)
            load_down(NE - 1, 3)
            first = sp.value_load(START[0:1, NE - 3:NE - 2], min_val=1, max_val=NI)
            sp.wait_ge(dn_done, first + 1)
            sp.dma_start(WSG[:, :, 0:FE], kp(w_sg[0])).then_inc(sh_ld, 16)
            sp.dma_start(WSG[:, :, FE:2 * FE], kp(w_su[0])).then_inc(sh_ld, 16)
            sp.dma_start(WSD, w_sd[0].rearrange("(f p) n -> p f n", p=P)).then_inc(sh_ld, 16)
            sp.dma_start(GF, g_final.rearrange("(a n) -> a n", a=1).to_broadcast([P, D])).then_inc(gf_ld, 16)
            pairs = sp.value_load(START[0:1, NE + 1:NE + 2], min_val=1, max_val=NI // 2)
            sp.wait_ge(scattered[0], (pairs + 2) * 16)
            sp.wait_ge(scattered[1], (pairs + 1) * 16)
            for t in range(NT):
                if t == 3:
                    sp.wait_ge(sg_done, 4)
                    sp.wait_ge(w6_ready, 1)
                    sp.wait_ge(sg_silu, 1)
                r = ROWS[t]
                rows = y_rows[t * P * YK:(t * P + r) * YK, :].rearrange("(p k) d -> p k d", k=YK)
                for k, part in YB[t]:
                    sp.dma_start(part[0:r], rows[:, k:k + part.shape[1], :]).then_inc(yb_ld[t], 16)
            for t in range(NT):
                sp.wait_ge(y_ready, t + 1)
                r = ROWS[t]
                dst = y_prompt[0, t * P:t * P + P, :] if t < 4 else y_sample[0]
                sp.dma_start(dst, X[0:r, t, :]).then_inc(y_stored, 16)
            sp.wait_ge(y_stored, 16 * NT)

        @block.gpsimd
        def _(pool):
            n = [0]

            def chain(ins):
                n[0] += 1
                ins.then_inc(pool_s, 1)
                pool.wait_ge(pool_s, n[0])

            pool.memset(IDENT, 0.0)
            pool.memset(NTRI, -1.0)
            pool.memset(UP, 1.0)
            pool.memset(NONES, -1.0)
            pool.memset(ONES, 1.0)
            chain(pool.memset(HALF, -0.5))
            pool.affine_select(out=IDENT, in_=IDENT, compare_op=ALU.not_equal, fill=1.0, base=0, pattern=[[-1, P]], channel_multiplier=1)
            pool.affine_select(out=NTRI, in_=NTRI, compare_op=ALU.is_ge, fill=0.0, base=0, pattern=[[-1, P]], channel_multiplier=1)
            pool.affine_select(out=UP, in_=UP, compare_op=ALU.is_gt, fill=0.0, base=0, pattern=[[1, P]], channel_multiplier=-1)
            pool.iota(BIAS[:, 0, :], pattern=[[-1, 512]], base=384, channel_multiplier=1, allow_small_or_imprecise_dtypes=True).then_inc(pool_c, 1)
            pool.wait_ge(ms_ready, 1)
            pool.tensor_tensor(RS, SS, HALF[:, 0, 0:NT], ALU.pow).then_inc(rs_ready, 1)
            for a, (kp_o, ks_o, vp_o, vs_o) in enumerate(((ak_p, ak_s, av_p, av_s), (bk_p, bk_s, bv_p, bv_s))):
                if a == 0:
                    pool.wait_ge(proj_act, 10)
                else:
                    pool.wait_ge(proj_dve, 15)
                c = slice(512 * a, 512 * a + 512)
                pool.dma_start(vp_o[0, 0].rearrange("(t p) h d -> p t (h d)", p=P), V[:, 0:4, c]).then_inc(new_stored, 16)
                pool.dma_start(vs_o[0, 0].rearrange("s h d -> s (h d)"), V[0:TS, 4, c]).then_inc(new_stored, 16)
                for t in range(NT):
                    u = NT * a + t
                    pool.wait_ge(kb_evac, u + 1)
                    dst = kp_o[0, 0, t * P:t * P + P] if t < 4 else ks_o[0, 0]
                    pool.dma_start(dst.rearrange("s h d -> s (h d)"), KO[u % 6][0:ROWS[t], :]).then_inc(ko_stored[u % 6], 16)
            def b_rms(h):
                pool.wait_ge(osb_ready, h + 1)
                pool.tensor_tensor(b_stat(OR, h), b_stat(OS, h), b_stat(HALF, h), ALU.pow).then_inc(orb_ready, 1)

            def later_logs(h):
                if h:
                    pool.wait_ge(p_done, 3 * h)
                else:
                    for b, c in enumerate((2, 2, 2, 2, 1, 1)):
                        pool.wait_ge(ko_stored[b], 16 * c)
                    pool.wait_ge(pva_done, len(UNITS))
                lk = LK[:, h % 2, :]
                pool.wait_ge(lk_ready, 3 * h + 1)
                pool.tensor_tensor(LS[:, 0, :], lk[:, ZO[2] + P:ZO[2] + 2 * P], lk[:, ZO[3]:ZO[3] + P], ALU.add).then_inc(ls_ready, 1)
                pool.wait_ge(lk_ready, 3 * h + 2)
                pool.wait_ge(ls_ready, 2 * h + 1)
                pool.tensor_tensor(LS[:, 1, :], lk[:, ZO[1] + P:ZO[1] + 2 * P], lk[:, ZO[2]:ZO[2] + P], ALU.add)
                pool.tensor_tensor(LS[:, 2, :], lk[:, ZO[1] + 2 * P:ZO[1] + 3 * P], LS[:, 0, :], ALU.add).then_inc(ls_ready, 1)

            for h in range(HB + 1):
                if h < HB:
                    later_logs(h)
                for s in range(3):
                    pool.wait_ge(eb_done, 3 * h + s + 1)
                    if h < HB:
                        blocks = [ZO[j] for j in ([2, 3], [1], [0])[s]]
                        for o in blocks:
                            v = AT[:, h % 2, o:o + P]
                            last = pool.affine_select(out=v, in_=v, compare_op=ALU.is_gt, fill=0.0, base=0, pattern=[[1, P]], channel_multiplier=-1)
                        last.then_inc(at_ready, 1)
                    elif s == 0:
                        v = AT[0:TS, h % 2, 1024:1536].rearrange("p (h q) -> p h q", q=TS)
                        pool.affine_select(out=v, in_=v, compare_op=ALU.is_gt, fill=0.0, base=0, pattern=[[0, HB], [1, TS]], channel_multiplier=-1).then_inc(at_ready, 1)
                if h == 0:
                    pool.wait_ge(osa_ready, 1)
                    pool.tensor_tensor(OR[:, :, 0:HA], OS[:, :, 0:HA], HALF[:, :, 0:HA], ALU.pow).then_inc(ora_ready, 1)
                if h >= 2:
                    b_rms(h - 2)
            b_rms(HB - 1)
            b_rms(HB)
            for t in range(NT):
                pool.wait_ge(ms_ready, 2 + t)
                pool.tensor_tensor(RS[:, t:t + 1], SS[:, t:t + 1], HALF[:, 0, 0:1], ALU.pow).then_inc(rs_ready, 1)
            pool.wait_ge(tr_done, 27)
            pool.wait_ge(logit_done, 1)
            pool.iota(RECI, pattern=[[2 * P * YK, NT], [2, 8]], base=-NONE, channel_multiplier=2 * YK)
            pool.iota(ITEMS, pattern=[[1, IC]], base=0, channel_multiplier=0, allow_small_or_imprecise_dtypes=True)
            chain(pool.iota(PLACES, pattern=[[1, SLOT]], base=0, channel_multiplier=0, allow_small_or_imprecise_dtypes=True))
            pool.tensor_copy(RECF, RECI).then_inc(rec_ready, 1)
            pool.wait_ge(sidx_ready, 1)
            for t in (0, 2):
                if t:
                    pool.wait_ge(oh_done, TOPK * (t - 1))
                for k in range(TOPK):
                    pool.tensor_scalar(OHI[0][:, k, :], ITEMS, COLF[:, t, k:k + 1], None, ALU.is_equal).then_inc(ohi_ready, 1)
            pool.wait_ge(h2_stored, 16 * NT)
            pool.memset(HG[0], 0.0)
            chain(pool.memset(HG[1], 0.0))
            pool.wait_ge(idx_ready, 1)
            pairs = pool.value_load(START[0:1, NE + 1:NE + 2], min_val=1, max_val=NI // 2)
            h2_halves = h2_rows.rearrange("t (h d) -> (t h) d", h=2)
            y_halves = y_rows.rearrange("t (h d) -> (t h) d", h=2)

            def gather(i, x, column):
                pool.tensor_copy(ICUR[:, x:x + 1], column).then_inc(cur_tok, 1)
                pool.wait_ge(cur_tok, i + 1)
                pool.sem_inc(pool_mark)
                pool.indirect_dma_start(HG[x], None, h2_halves, bass.IndirectOffsetOnAxis(ap=ICUR[:, x:x + 1], axis=0),
                                        bounds_check=2 * T - 1, oob_is_err=False).then_inc(gathered[x], 16)

            def scatter(i, x):
                pool.tensor_copy(ICUR[:, 2 + x:3 + x], IDX[:, 1, bass.ds(i, 1)]).then_inc(cur_row, 1)
                pool.wait_ge(cur_row, i + 1)
                pool.sem_inc(pool_mark)
                pool.indirect_dma_start(y_halves, bass.IndirectOffsetOnAxis(ap=ICUR[:, 2 + x:3 + x], axis=0), YO[x], None,
                                        bounds_check=2 * T * YK - 1, oob_is_err=False).then_inc(scattered[x], 16)

            gather(0, 0, IDX[:, 0, 1:2])
            gather(1, 1, IDX[:, 0, 2:3])
            pool.wait_ge(yo_ready, 1)
            for x in range(2):
                pool.indirect_dma_start(y_halves, bass.IndirectOffsetOnAxis(ap=IDX[:, 1, 0:1], axis=0), YO[x], None,
                                        bounds_check=2 * T * YK - 1, oob_is_err=False).then_inc(scattered[x], 16)
            pool.wait_ge(hg_staged, 1)
            gather(2, 0, IDX[:, 0, 3:4])
            with pool.Fori(0, pairs) as g:
                for x in range(2):
                    i = g * 2 + x
                    pool.wait_ge(hg_staged, i + 2)
                    pool.sem_inc(pool_mark)
                    gather(i + 3, 1 - x, IDX[:, 0, bass.ds(i + 4, 1)])
                    pool.wait_ge(yo_ready, i + 2)
                    pool.sem_inc(pool_mark)
                    scatter(i, x)
            pool.wait_ge(yo_ready, pairs * 2 + 2)
            pool.sem_inc(pool_mark)
            scatter(pairs * 2, 0)
            pool.wait_ge(gathered[0], (pairs + 2) * 16)
            pool.wait_ge(gathered[1], (pairs + 1) * 16)
            for t in range(NT + 1):
                if t < 3:
                    r = ROWS[t]
                    acc = YB[t][0][1][0:r, 0, :]
                    pool.wait_ge(acc_ready, t + 1)
                    pool.tensor_tensor(acc, acc, G2[0:r, t // 4, :], ALU.mult).then_inc(fin_g2, 1)
                    pool.wait_ge(fin_g2, t + 1)
                    pool.tensor_tensor(X[0:r, t, :], X[0:r, t, :], acc, ALU.add).then_inc(fin_x, 1)
                if t:
                    pool.wait_ge(fin_ms, t)
                    pool.tensor_tensor(RS[:, t - 1:t], SS[:, t - 1:t], HALF[:, 0, 0:1], ALU.pow).then_inc(fin_rs, 1)
            pool.wait_ge(new_stored, 64)
            for b, c in enumerate((2, 2, 2, 2, 1, 1)):
                pool.wait_ge(ko_stored[b], 16 * c)

        @block.tensor
        def _(pe):
            def back(src, r, b):
                for k in range(KC):
                    last = pe.transpose(bank[b + k // 4][0:r, (k % 4) * P:(k % 4 + 1) * P], src(k), IDENT)
                return last

            def turn_chunk(src, k):
                for t in range(4):
                    last = pe.transpose(bank[k % 4][:, t * P:t * P + P], src[:, t, k * P:k * P + P], IDENT)
                last.then_inc(tr_done, 1)

            def turn(src, r, half=None, sample=None, begun=0):
                for k in range(begun, KC):
                    if k == 4 and half:
                        pe.wait_ge(*half)
                    if k >= 4:
                        pe.wait_ge(tr_act if k % 2 else tr_dve, (4 if k % 2 else 5) * r + (k - 4) // 2 + 1)
                    turn_chunk(src, k)
                if sample:
                    pe.wait_ge(*sample)
                for k in range(KC):
                    last = pe.transpose(bank[4][:, k * TS:k * TS + TS], src[0:TS, 4, k * P:k * P + P], IDENT[0:TS, 0:TS])
                last.then_inc(tr_done, 1)

            def turned(r):
                pe.wait_ge(tr_dve, 5 * (r + 1))
                pe.wait_ge(tr_act, 4 * (r + 1))

            def ada(a, g):
                pe.wait_ge(ring_ld[g % 3], ring_count(g))
                if a:
                    pe.wait_ge(mod_ready, a)
                else:
                    pe.wait_ge(c_ready, 1)
                for k in range(KC):
                    q = k % 4
                    last = pe.matmul(bank[6][32 * q:32 * q + 32, :], CT[:, k, :], RING[g % 3][:, k, :], start=(k < 4), stop=(k >= 4),
                                     tile_position=(0, 32 * q))
                last.then_inc(ada_done, 1)

            def ada_turn(a):
                pe.wait_ge(mr_ready, a + 1)
                for m in range(4):
                    last = pe.matmul(bank[6][:, 2 * m:2 * m + 2], MR[:, m * P:m * P + P], SEL2, start=True, stop=True)
                last.then_inc(mod_mm, 1)

            def wide(w, src, m, a, b):
                for k in range(KC):
                    lw = w[:, k, m * P:m * P + P]
                    pe.matmul(bank[a][:, 0:TH], lw, src[:, k, 0:TH], start=(k == 0), stop=(k == KC - 1))
                    last = pe.matmul(bank[b][:, 0:TH], lw, src[:, k, TH:T], start=(k == 0), stop=(k == KC - 1))
                return last

            pe.wait_ge(pool_c, 1)
            pe.wait_ge(small_ld, 96)
            pe.transpose(bank[7][:, 0:66], SMALL[0:66, :], IDENT[0:66, 0:66]).then_inc(small_t, 1)
            for a in range(ADA_FIRST):
                if a == ADA_FIRST - 1:
                    pe.wait_ge(xn_ready, NT)
                    for k in range(4):
                        turn_chunk(XN, k)
                ada(a, a)
                ada_turn(a)
            pe.wait_ge(lam_neg, 1)
            pe.wait_ge(smt_ready, 1)
            pe.matmul(bank[7][:, 0:1], ONES[0:1, :], LAM[0:1, 0:1], start=True, stop=True).then_inc(lam_bc, 1)
            turn(XN, 0, begun=4)
            turned(0)
            def keys_back(a, t):
                if t == 0:
                    pe.wait_ge(proj_dve if a == 0 else proj_act, 5 if a == 0 else 15)
                q = NT * a + t
                if q >= 2:
                    pe.wait_ge(kb_evac, q - 1)
                else:
                    pe.wait_ge(nlam_ready, 1)
                b = bank[5 + 2 * (q % 2)]
                r = ROWS[t]
                for m in range(4):
                    last = pe.transpose(b[0:r, m * P:m * P + P], KT[:, 4 * a + m, t * P:t * P + r], IDENT)
                last.then_inc(kb_done, 1)

            for n in range(6):
                g = G_IN + n
                pe.wait_ge(ring_ld[g % 3], ring_count(g))
                w = RING[g % 3]
                before, base = (proj_dve if n % 2 == 0 else proj_act), 5 * ((n - 1) // 2)
                own, own_base = (proj_act if n % 2 == 0 else proj_dve), 5 * (n // 2)
                for t in range(NT if n % 3 == 2 else 4):
                    if n % 3 < 2:
                        if t >= 2:
                            pe.wait_ge(own, own_base + t - 1)
                        elif n == 3:
                            pe.wait_ge(before, base + 2 * t + 2)
                        elif n:
                            pe.wait_ge(before, base + (3 if t == 0 else 5))
                        wide(w, HT, t, 2 * (t % 2), 2 * (t % 2) + 1).then_inc(proj_done, 2 if t == 3 else 1)
                    else:
                        pe.wait_ge(before, base + (3 if t < 2 else 5))
                        r = ROWS[t]
                        for k in range(KC):
                            if t < 4:
                                last = pe.matmul(bank[t][:, :], HT[:, k, t * P:t * P + P], w[:, k, :], start=(k == 0), stop=(k == KC - 1))
                            else:
                                for x in range(2):
                                    last = pe.matmul(bank[4][x * TS:x * TS + TS, 0:256], HT[:, k, TP:T], w[:, k, 256 * x:256 * x + 256],
                                                     start=(k == 0), stop=(k == KC - 1))
                        last.then_inc(proj_done, 1)
                        if t:
                            keys_back(n // 3, t - 1)
                if n % 3 == 2:
                    keys_back(n // 3, NT - 1)
            pe.wait_ge(ck_ld, 32)
            for j in range(PT):
                for a in range(2):
                    q = 2 * NT + 2 * j + a
                    pe.wait_ge(kb_evac, q - 1)
                    b = bank[5 + 2 * (q % 2)]
                    for m in range(4):
                        last = pe.transpose(b[:, m * P:m * P + P], CK[:, j, 512 * a + m * P:512 * a + m * P + P], IDENT)
                    last.then_inc(kb_done, 1)

            def a_scores(u):
                i, h = UNITS[u]
                r = ROWS[i]
                if u == 0:
                    pe.wait_ge(proj_dve, 15)
                    pe.wait_ge(proj_act, 15)
                if u >= 2:
                    pe.wait_ge(sa_read, 2 * (u - 1))
                if i == 4 and h == 0:
                    pe.wait_ge(kb_evac, 14)
                for m in range(2):
                    b = bank[2 * (u % 2) + m]
                    q = QT[m * DB:m * DB + DB, h, i * P:i * P + r]
                    if i < 4:
                        last = pe.matmul(b[:, 0:KEYS[i]], q, KT[m * DB:m * DB + DB, h, 0:KEYS[i]], start=True, stop=True)
                    else:
                        pe.matmul(b[0:r, 0:PAST], q, CKT[m * DB:m * DB + DB, h, :], start=True, stop=True)
                        last = pe.matmul(b[0:r, PAST:PAST + TS], q, KT[m * DB:m * DB + DB, h, TP:T], start=True, stop=True)
                last.then_inc(sa_done, 1)

            def a_turn(u):
                i, h = UNITS[u]
                r = ROWS[i]
                if u >= 2:
                    pe.wait_ge(wta_evac, u - 1)
                else:
                    pe.wait_ge(kb_evac, 14)
                pe.wait_ge(wa_ready, u + 1)
                for j in range((KEYS[i] + P - 1) // P):
                    w = min(P, KEYS[i] - j * P)
                    last = pe.transpose(bank[4 + u % 2][0:w, j * P:j * P + r], SE[u % 3][0:r, 1, j * P:j * P + w], IDENT[0:r, 0:r])
                last.then_inc(wta_done, 1)

            def a_values(u):
                i, h = UNITS[u]
                r = ROWS[i]
                nj = (KEYS[i] + P - 1) // P
                if u >= 2:
                    pe.wait_ge(oa_evac, u - 1)
                pe.wait_ge(wta_evac, u + 1)
                for j in range(nj):
                    w = min(P, KEYS[i] - j * P)
                    v = V[:, j, h * P:h * P + P] if i < 4 else (CV[:, j, h * P:h * P + P] if j < PT else V[0:TS, 4, h * P:h * P + P])
                    last = pe.matmul(bank[6 + u % 2][0:r, 0:P], WT[0:w, u % 2, j * P:j * P + r], v, start=(j == 0), stop=(j == nj - 1))
                last.then_inc(pva_done, 1)

            pe.wait_ge(cv_ld, 32)
            for u in range(len(UNITS) + 3):
                if u < len(UNITS):
                    a_scores(u)
                if 2 <= u <= len(UNITS) + 1:
                    a_turn(u - 2)
                if u >= 3:
                    a_values(u - 3)

            def b_scores(h):
                if h == 0:
                    pe.wait_ge(oa_evac, len(UNITS))
                if h >= 2:
                    pe.wait_ge(eb_done, 3 * (h - 1))
                for j in ((2, 3, 1, 0) if h < HB else (2, 1, 0)):
                    if h < HB:
                        o = h % 2 * DB
                        last = pe.matmul(zbank(h, j), KT[o:o + DB, 4 + h // 2, j * P:j * P + P], QT[o:o + DB, 4 + h // 2, j * P:TP],
                                         start=(j < 3), stop=True, skip_group_check=True)
                        if j != 2:
                            last.then_inc(z_done, 1)
                    else:
                        r = P if j < PT else TS
                        for x, g in enumerate((0, 2, 4, 6, 1, 3, 5, 7)):
                            o = g % 2 * DB
                            if x == 4:
                                last.then_inc(z_half, 1)
                                pe.wait_ge(z_half, 3 - j)
                            k = CKT[o:o + DB, 4 + g // 2, j * P:j * P + P] if j < PT else KT[o:o + DB, 4 + g // 2, TP:T]
                            last = pe.matmul(bank[3 * (h % 2) + j][0:r, g * TS:g * TS + TS], k, QT[o:o + DB, 4 + g // 2, TP:T],
                                             start=(g == 0), stop=True, skip_group_check=True)
                        last.then_inc(z_done, 1)

            def b_sums(h):
                for j in ((3, 2, 1, 0) if h < HB else (2, 1, 0)):
                    s = min(j, 2)
                    pe.wait_ge(lk_ready, 3 * h + 3 - s)
                    if h < HB:
                        out = zbank(h, j)
                        last = pe.matmul(out, NTRI, LK[:, h % 2, ZO[j]:ZO[j] + ZW[j]], start=False, stop=True, skip_group_check=True)
                        if j < 3:
                            last = pe.matmul(out[:, P:2 * P], NONES, LK[:, h % 2, ZO[j + 1]:ZO[j + 1] + P], start=False, stop=True, skip_group_check=True)
                        if j < 2:
                            pe.wait_ge(ls_ready, 2 * h + 2 - j)
                            later = LS[:, 0, :] if j == 1 else LS[:, 1:3, :].rearrange("p a b -> p (a b)")
                            last = pe.matmul(out[:, 2 * P:ZW[j]], NONES, later, start=False, stop=True, skip_group_check=True)
                        if j != 3:
                            last.then_inc(p_done, 1)
                    else:
                        r = P if j < PT else TS
                        out = bank[3 * (h % 2) + j][0:r, :]
                        last = pe.matmul(out, NTRI[0:r, 0:r], LK[0:r, h % 2, j * 512:j * 512 + 512], start=False, stop=True, skip_group_check=True)
                        for l in range(j + 1, 3):
                            rl = P if l < PT else TS
                            last = pe.matmul(out, NONES[0:rl, 0:r], LK[0:rl, h % 2, l * 512:l * 512 + 512], start=False, stop=True, skip_group_check=True)
                        last.then_inc(p_done, 1)

            def b_values(h):
                if h >= 1:
                    pe.wait_ge(ob_evac, h)
                pe.wait_ge(at_ready, 3 * h + 3 if h < HB else 3 * HB + 1)
                if h < HB:
                    for i in range(4):
                        for j in range(i + 1):
                            o = ZO[j] + (i - j) * P
                            last = pe.matmul(bank[7][:, i * DB:i * DB + DB], AT[:, h % 2, o:o + P], V[:, j, 512 + h * DB:512 + h * DB + DB],
                                             start=(j == 0), stop=(j == i))
                else:
                    pe.wait_ge(eb_done, 3 * HB + 3)
                    for g in range(HB):
                        c = slice(512 + g * DB, 512 + g * DB + DB)
                        for j in range(3):
                            r = P if j < PT else TS
                            v = CV[:, j, c] if j < PT else V[0:TS, 4, c]
                            last = pe.matmul(bank[7][0:TS, g * DB:g * DB + DB], AT[0:r, h % 2, j * 512 + g * TS:j * 512 + g * TS + TS], v,
                                             start=(j == 0), stop=(j == 2))
                last.then_inc(pvb_done, 1)

            for h in range(HB + 3):
                if h <= HB:
                    b_scores(h)
                if 1 <= h <= HB:
                    ada_turn(ADA_FIRST + h - 1)
                if 1 <= h <= HB + 1:
                    b_sums(h - 1)
                if h >= 2:
                    b_values(h - 2)
                if h < HB:
                    ada(ADA_FIRST + h, G_ADA + h)

            def on_rows(first, s, a, b):
                for k in range(KC):
                    last = pe.matmul(bank[(a, b)[k // 4]][:, (k % 4) * P:(k % 4 + 1) * P], MOD[:, first + k, s:s + 1].to_broadcast([P, P]), IDENT, start=True, stop=True)
                return last

            pe.wait_ge(eb_done, 3 * (HB + 1))
            pe.wait_ge(on_ready, NT)
            turn(OA, 1, half=(on_ready, NT + HB), sample=(on_ready, NT + HB + 1))
            pe.wait_ge(mod_ready, 12)
            on_rows(16, 0, 5, 6).then_inc(g1_mm, 1)
            turned(1)
            on_rows(16, 1, 7, 4).then_inc(g1_mm, 1)
            for n in range(2):
                pe.wait_ge(ring_ld[(G_OUT + n) % 3], ring_count(G_OUT + n))
            w = [RING[(G_OUT + n) % 3] for n in range(2)]
            for t in range(4):
                if t == 2:
                    pe.wait_ge(g1_ready, 1)
                if t == 3:
                    pe.wait_ge(x1_ready, 1)
                for n in range(2):
                    for k in range(KC):
                        last = pe.matmul(bank[WOB[t][n]][:, :], OT[:, k, t * P:t * P + P], w[n][:, k, :], start=(k == 0), stop=(k == KC - 1))
                last.then_inc(wo_done, 1)
            pe.wait_ge(g1_ready, 2)
            for k in range(KC):
                for n in range(2):
                    last = pe.matmul(bank[7][n * TS:n * TS + TS, :], OT[:, k, TP:T], w[n][:, k, :], start=(k == 0), stop=(k == KC - 1))
            last.then_inc(wo_done, 1)
            pe.wait_ge(xn_ready, NT + 4)
            turn(XN, 2, sample=(xn_ready, 2 * NT))
            turned(2)
            pe.wait_ge(router_ld, 32)
            for k in range(KC):
                for c, dst, src in ((0, slice(0, 256), slice(0, 256)), (NE, slice(0, 256), slice(256, TP)), (0, slice(256, 256 + TS), slice(TP, T))):
                    last = pe.matmul(bank[5][c:c + NE, dst], WR[:, k, :], HT[:, k, src], start=(k == 0 and dst.start == 0), stop=(k == KC - 1), skip_group_check=True)
            last.then_inc(lt_done, 1)
            pe.wait_ge(lt_evac, 1)
            for j in range(2):
                pe.transpose(bank[4][:, j * P:j * P + P], LT[:, j * P:j * P + P], IDENT)
            last = pe.transpose(bank[4][0:TS, 2 * P:2 * P + NE], LT[0:NE, 256:256 + TS], IDENT[0:NE, 0:NE])
            last.then_inc(logit_done, 1)
            for t in range(NT):
                if t >= 2:
                    pe.wait_ge(h2_evac, t - 1)
                r = ROWS[t]
                back(lambda k: HT[:, k, t * P:t * P + r], r, 6 if t % 2 == 0 else 0).then_inc(h2t_done, 1)
            pe.wait_ge(mask_ready, 1)
            pe.wait_ge(h2_evac, NT)
            pe.matmul(bank[6][:, 0:NT * NE], UP, M.rearrange("p t e -> p (t e)"), start=True, stop=False)
            pe.matmul(bank[6][:, 0:NT * NE], ONES, MS[:, 0:NT, :].rearrange("p t e -> p (t e)"), start=False, stop=True)
            pe.matmul(bank[7][:, 0:NE], ONES, MS[:, NT, :], start=True, stop=True).then_inc(pos_done, 1)
            for u in range(NT * TOPK):
                t, k = divmod(u, TOPK)
                if t in (0, 2):
                    pe.wait_ge(ohi_ready, t // 2 * TOPK + k + 1)
                else:
                    pe.wait_ge(ohi_rest, {1: 1, 3: 2, 4: 3}[t])
                pe.wait_ge(ohp_ready, t + 1)
                for half in range(2):
                    last = pe.matmul(bank[7][half * SLOT:half * SLOT + SLOT, 0:IC], OHP[t % 2][:, k, :], OHI[t % 2][:, k, :], start=(u == 0), stop=(u == NT * TOPK - 1))
                last.then_inc(oh_done, 1)
            for s in range(2):
                on_rows(40, s, (4, 2)[s], (4, 2)[s] + 1).then_inc(g2_mm, 1)

            def turn_in():
                for c in range(4):
                    last = pe.transpose(bank[1][:, c * P:c * P + P], HGS[:, c * P:c * P + P], IDENT)
                last.then_inc(hgt_done, 1)

            def gate_up(j):
                for k in range(KC):
                    w = GU[j][:, k, :].rearrange("p (g f) -> p g f", f=FE)
                    for n in range(2):
                        last = pe.matmul(bank[0][n * SLOT:n * SLOT + SLOT, 0:2 * P].rearrange("p (g f) -> p g f", f=P), HGT[:, k % 4, k // 4, :],
                                         w[:, :, n * P:n * P + P], start=(k == 0), stop=(k == KC - 1))
                last.then_inc(gu_done, 1)

            def down(j):
                for f in range(2):
                    for n in range(2):
                        last = pe.matmul(bank[3][n * SLOT:n * SLOT + SLOT, :], AE[:, f, :], DN[j][:, f, 512 * n:512 * n + 512], start=(f == 0), stop=(f == 1))
                last.then_inc(dn_done, 1)

            def item(i, j, before):
                pe.wait_ge(hgt_ready, i + 1)
                gate_up(j)
                pe.wait_ge(hg_staged, i + 2)
                pe.sem_inc(pe_mark)
                turn_in()
                pe.wait_ge(ae_ready, i + 1)
                pe.wait_ge(yo_ready, i + 1)
                down(before)
                pe.wait_ge(ac_ready, i + 1)
                pe.sem_inc(pe_mark)
                pe.transpose(bank[2][:, 0:P], AC, IDENT).then_inc(at_done, 1)

            pe.wait_ge(g2_ready, 2)
            pe.wait_ge(hg_staged, 1)
            turn_in()
            pe.wait_ge(exp_ld[3], 48)
            with pe.Fori(0, NE // 4) as g:
                e = g * 4
                for j in range(4):
                    lo = pe.value_load(START[0:1, bass.ds(e + j, 1)], min_val=0, max_val=NI - 1)
                    hi = pe.value_load(START[0:1, bass.ds(e + (j + 1), 1)], min_val=1, max_val=NI)
                    pe.wait_ge(exp_ld[j], (g + 1) * 48)
                    pe.sem_inc(pe_mark)
                    item(lo, j, (j + 3) % 4)
                    with pe.If_lt(pe.to_reg(lo + 1), pe.to_reg(hi)):
                        with pe.Fori(lo + 1, hi) as i:
                            item(i, j, j)
            items = pe.value_load(START[0:1, NE:NE + 1], min_val=1, max_val=NI)
            pe.wait_ge(ae_ready, items + 1)
            pe.wait_ge(yo_ready, items + 1)
            down(3)
            pe.wait_ge(sh_ld, 48)
            for m in range(4):
                if m == 2:
                    pe.wait_ge(hgt_ready, items + 1)
                    pe.wait_ge(yo_ready, items + 2)
                wide(WSG, HT, m, *SGB[m]).then_inc(sg_done, 1)
            pe.wait_ge(as_ready, 1)
            for t in range(NT):
                if t == 4:
                    pe.wait_ge(acc_ready, 1)
                r = ROWS[t]
                for f, n in ((0, 0), (1, 0), (0, 1), (1, 1)) if t < 4 else ((0, 0), (0, 1), (1, 0), (1, 1)):
                    out = bank[SDB[t][n]][0:r, :] if t < 4 else bank[SDB[t][0]][n * TS:n * TS + TS, :]
                    last = pe.matmul(out, SA[:, f, t * P:t * P + r], WSD[:, f, 512 * n:512 * n + 512], start=(f == 0), stop=(f == 1))
                last.then_inc(sd_done, 1)

        @block.scalar
        def _(act):
            n = [0]

            def chain(ins):
                n[0] += 1
                ins.then_inc(act_s, 1)
                act.wait_ge(act_s, n[0])

            def squares(t, junk, done, before):
                r = ROWS[t]
                act.wait_ge(done, before)
                act.activation(junk[0:r, :], X[0:r, t, :], ACT.Square, accum_out=SS[0:r, t:t + 1]).then_inc(done, 1)

            def turned(r, dst, scale, shift, ks=range(1, KC, 2)):
                for k in ks:
                    act.wait_ge(tr_done, 9 * r + k + 1)
                    act.activation(dst[:, k, 0:TP], bank[k % 4][:, :], ACT.Identity, scale=scale(k), bias=shift(k) if shift else 0.0).then_inc(tr_act, 1)

            act.wait_ge(smt_ready, 1)
            act.activation(CT[:, :, 0:2], SMT[:, 0:16].rearrange("p (s k) -> p k s", k=KC), ACT.Silu).then_inc(c_ready, 1)
            act.wait_ge(x_ld, 32)
            act.wait_ge(init_ready, 1)
            for t in range(NT):
                squares(t, at(a_tmp + 5632, D), sq_done, t)
            act.wait_ge(lam_sum, 1)
            act.activation(LAM[0:1, :], LAM[0:1, :], ACT.Exp).then_inc(lam_exp, 1)
            act.wait_ge(mod_ready, ADA_FIRST)
            turned(0, HT, lambda k: MOD[:, 8 + k, 0:1], lambda k: MOD[:, k, 0:1])

            def keys_out(q):
                act.wait_ge(kb_done, q + 1)
                b = bank[5 + 2 * (q % 2)]
                if q < 2 * NT:
                    if q >= 6:
                        act.wait_ge(ko_stored[q % 6], 16)
                    r = ROWS[q % NT]
                    act.copy(KO[q % 6][0:r, :], b[0:r, :]).then_inc(kb_evac, 1)
                else:
                    j, a = divmod(q - 2 * NT, 2)
                    act.copy(CKT[:, 4 * a:4 * a + 4, j * P:j * P + P], b.rearrange("p (m c) -> p m c", c=P)).then_inc(kb_evac, 1)

            for n_g in (0, 2, 4):
                for t in range(NT if n_g == 2 else 4):
                    act.wait_ge(proj_done, 5 * n_g + t + (2 if n_g != 2 and t == 3 else 1))
                    if n_g == 2:
                        if t < 4:
                            ins = act.copy(V[:, t, 0:512], bank[t][:, :])
                        else:
                            for x in range(2):
                                ins = act.copy(V[0:TS, 4, 256 * x:256 * x + 256], bank[4][x * TS:x * TS + TS, 0:256])
                    else:
                        dst, scale = (QT[:, 0:4], -DB ** -0.5) if n_g == 0 else (KT[:, 4:8], 1.0)
                        for x in range(2):
                            ins = act.activation(dst[:, t, x * TH:x * TH + TH], bank[2 * (t % 2) + x][:, 0:TH], ACT.Copy, scale=scale)
                    ins.then_inc(proj_act, 2 if n_g != 2 and t == 3 else 1)
                    if n_g == 2 and t:
                        keys_out(t - 1)
                if n_g == 2:
                    keys_out(NT - 1)
            for q in range(NT, 2 * NT + 4):
                keys_out(q)

            def a_exp(u):
                i, h = UNITS[u]
                r = ROWS[i]
                for m in range(2):
                    act.wait_ge(sa_read, 2 * u + m + 1)
                    s = SE[u % 3][0:r, m, 0:KEYS[i]]
                    act.activation(s, s, ACT.Exp, scale=-1.0, bias=MINS[0:r, u % 3, m:m + 1], accum_out=SUMS[0:r, i, h, m:m + 1]).then_inc(ea_done, 1)

            def a_turned(u):
                i, h = UNITS[u]
                if u == 0:
                    for b, c in ((3, 2), (4, 1), (5, 1)):
                        act.wait_ge(ko_stored[b], 16 * c)
                act.wait_ge(wta_done, u + 1)
                if u >= 2:
                    act.wait_ge(pva_done, u - 1)
                b = bank[4 + u % 2]
                if i < 4:
                    act.copy(WT[:, u % 2, 0:KEYS[i]], b[:, 0:KEYS[i]]).then_inc(wta_evac, 1)
                else:
                    for j in range(3):
                        w = P if j < PT else TS
                        ins = act.copy(WT[0:w, u % 2, j * P:j * P + TS], b[0:w, j * P:j * P + TS])
                    ins.then_inc(wta_evac, 1)

            def a_out(u):
                i, h = UNITS[u]
                r = ROWS[i]
                act.wait_ge(pva_done, u + 1)
                if u:
                    act.wait_ge(oa_evac, u)
                act.activation(SQ[0:r, 0:P], bank[6 + u % 2][0:r, 0:P], ACT.Square, accum_out=OS[0:r, i, h:h + 1])
                act.copy(OA[0:r, i, h * P:h * P + P], bank[6 + u % 2][0:r, 0:P]).then_inc(oa_evac, 1)

            for u in range(len(UNITS) + 3):
                if u < len(UNITS):
                    a_exp(u)
                if 2 <= u <= len(UNITS) + 1:
                    a_turned(u - 2)
                if u >= 3:
                    a_out(u - 3)

            def b_part(h, s):
                if h < HB:
                    return P, ZS[s][0], ZS[s][1], bank[3 * (h % 2) + s]
                return P if s < PT else TS, s * 512, 512, bank[3 * (h % 2) + s]

            def b_fade(h):
                for x, s in enumerate((2, 1, 0)):
                    r, o, w, b = b_part(h, s)
                    v = LK[0:r, h % 2, o:o + w]
                    act.wait_ge(abs_ready, 3 * h + x + 1)
                    act.activation(v, v, ACT.Exp, scale=-1.0).then_inc(fade_ready, 1)

            def b_log(h):
                for x, s in enumerate((2, 1, 0)):
                    r, o, w, b = b_part(h, s)
                    v = LK[0:r, h % 2, o:o + w]
                    act.wait_ge(fade_ready, 3 * h + x + 1)
                    act.activation(v, v, ACT.Ln, bias=1.0).then_inc(lk_ln, 1)

            def b_exp(h):
                for x, s in enumerate((2, 1, 0)):
                    r, o, w, b = b_part(h, s)
                    act.wait_ge(p_done, 3 * h + x + 1)
                    if h >= 2 and x == 0:
                        act.wait_ge(pvb_done, h - 1)
                    act.activation(AT[0:r, h % 2, o:o + w], b[0:r, 0:w], ACT.Exp).then_inc(eb_done, 1)

            def b_out(h):
                act.wait_ge(pvb_done, h + 1)
                if h < HB:
                    act.copy(OA[:, 0:4, 512 + h * DB:512 + h * DB + DB], bank[7][:, 0:4 * DB].rearrange("p (t d) -> p t d", d=DB)).then_inc(ob_evac, 1)
                else:
                    act.copy(OA[0:TS, 4, 512:D], bank[7][0:TS, :]).then_inc(ob_evac, 1)

            for h in range(HB + 3):
                if h <= HB:
                    b_fade(h)
                if 1 <= h <= HB + 1:
                    b_exp(h - 1)
                if h <= HB:
                    b_log(h)
                if h >= 2:
                    b_out(h - 2)

            turned(1, OT, lambda k: GA[:, k // 4:k // 4 + 1], None)
            for s in range(2):
                act.wait_ge(g1_mm, s + 1)
                for x in range(2):
                    ins = act.copy(G1[:, s, 512 * x:512 * x + 512], bank[((5, 6), (7, 4))[s][x]][:, :])
                ins.then_inc(g1_ready, 1)
            for t in range(NT):
                if t == 4:
                    turned(2, HT, lambda k: MOD[:, 32 + k, 0:1], lambda k: MOD[:, 24 + k, 0:1], (1, 3))
                act.wait_ge(x1_ready, t + 1)
                squares(t, at(a_tmp + 2048, D), sq_done, NT + t)
            turned(2, HT, lambda k: MOD[:, 32 + k, 0:1], lambda k: MOD[:, 24 + k, 0:1], (5, 7))
            act.wait_ge(lt_done, 1)
            act.copy(LT[0:NE, :], bank[5][0:NE, 0:256 + TS])
            act.copy(LT[NE:P, 0:256], bank[5][NE:P, 0:256]).then_inc(lt_evac, 1)
            act.wait_ge(logit_done, 1)
            act.wait_ge(sc_clear, 1)
            act.activation(SC[:, 0:4, :].rearrange("p (h j) e -> p j h e", j=2), bank[4][:, 0:4 * NE].rearrange("p (j h e) -> p j h e", h=2, e=NE), ACT.Sigmoid)
            act.activation(SC[0:TS, 4, :], bank[4][0:TS, 4 * NE:NT * NE], ACT.Sigmoid).then_inc(sc_ready, 1)
            for t in range(NT):
                r = ROWS[t]
                b = 6 if t % 2 == 0 else 0
                act.wait_ge(h2t_done, t + 1)
                act.copy(H2S[0:r, t, 0:512], bank[b][0:r, :])
                act.copy(H2S[0:r, t, 512:D], bank[b + 1][0:r, :]).then_inc(h2_evac, 1)
                act.wait_ge(h2_evac, t + 1)
                act.dma_start(h2_rows[t * P:t * P + r, :], H2S[0:r, t, :]).then_inc(h2_stored, 16)
            for s in range(2):
                act.wait_ge(g2_mm, s + 1)
                for n in range(2):
                    ins = act.copy(G2[:, s, 512 * n:512 * n + 512], bank[(4, 2)[s] + n][:, :])
                ins.then_inc(g2_ready, 1)
            act.wait_ge(h2_stored, 16 * NT)
            act.activation(AE.rearrange("p f s -> p (f s)"), IDENT, ACT.Copy, scale=0.0).then_inc(ae_ready, 1)
            act.wait_ge(start_ready, 1)
            pairs = act.value_load(START[0:1, NE + 1:NE + 2], min_val=1, max_val=NI // 2)

            def stage(i, x, count):
                act.wait_ge(gathered[x], count)
                act.copy(HGS, HG[x]).then_inc(hg_staged, 1)

            stage(0, 0, 16)
            act.wait_ge(hgt_done, 1)
            stage(1, 1, 16)
            with act.Fori(0, pairs) as g:
                for x in range(2):
                    i = g * 2 + x
                    act.wait_ge(gu_done, i + 1)
                    act.activation(SI, bank[0][:, 0:P], ACT.Silu).then_inc(silu_done, 1)
                    act.wait_ge(at_done, i + 1)
                    act.wait_ge(dn_done, i + 1)
                    act.copy(AE.rearrange("p f s -> p (f s)"), bank[2][:, 0:P]).then_inc(ae_ready, 1)
                    act.wait_ge(hgt_done, i + 2)
                    stage(i + 2, x, (g + 2) * 16)
            def first_term(t):
                acc = YB[t][0][1][0:ROWS[t], 0, :]
                act.wait_ge(w6_ready, 1)
                act.wait_ge(yb_ld[t], 16 * len(YB[t]))
                act.activation(acc, acc, ACT.Copy, scale=W6[0:ROWS[t], t, 0:1]).then_inc(yb_first, 1)

            act.wait_ge(hg_staged, pairs * 2 + 2)
            act.wait_ge(hgt_ready, pairs * 2 + 1)
            for m in range(2):
                act.wait_ge(sg_done, m + 1)
                for x in range(2):
                    ins = act.activation(SA[:, m, x * TH:x * TH + TH], bank[SGB[m][x]][:, 0:TH], ACT.Silu)
                ins.then_inc(sg_silu, 1)
            first_term(0)
            first_term(1)
            first_term(2)
            first_term(3)
            for t in range(NT):
                if t < 3:
                    act.wait_ge(fin_x, t + 1)
                else:
                    act.wait_ge(fin_last, t - 2)
                squares(t, YB[t][0][1][:, 1, :], fin_sq, t)
                if t == 0:
                    first_term(4)

        @block.vector
        def _(dve):
            n = [0]

            def chain(ins):
                n[0] += 1
                ins.then_inc(dve_s, 1)
                dve.wait_ge(dve_s, n[0])

            def mod_rows(a):
                dve.wait_ge(ada_done, a + 1)
                if a:
                    dve.wait_ge(mod_mm, a)
                dve.tensor_copy(MR, bank[6][:, :]).then_inc(mr_ready, 1)

            def mod(a):
                dve.wait_ge(mod_mm, a + 1)
                dve.scalar_tensor_tensor(out=MOD[:, 4 * a:4 * a + 4, :], in0=bank[6][:, 0:8].rearrange("p (m s) -> p m s", s=2),
                                         scalar=1.0 if a in (2, 3, 8, 9) else 0.0,
                                         in1=SMT[:, 16 + 4 * a:20 + 4 * a].unsqueeze(2).to_broadcast([P, 4, 2]), op0=ALU.add, op1=ALU.add).then_inc(mod_ready, 1)

            def means(t0, t1):
                dve.tensor_scalar(SS[:, t0:t1], SS[:, t0:t1], 1.0 / D, EPS, ALU.mult, ALU.add).then_inc(ms_ready, 1)

            def norm(t):
                r = ROWS[t]
                dve.tensor_scalar(XN[0:r, t, :], X[0:r, t, :], RS[0:r, t:t + 1], None, ALU.mult).then_inc(xn_ready, 1)

            def turned(r, dst, scale, shift, ks=range(0, KC, 2)):
                for k in ks:
                    dve.wait_ge(tr_done, 9 * r + k + 1)
                    if shift:
                        dve.tensor_scalar(dst[:, k, 0:TP], bank[k % 4][:, :], scale(k, 0), shift(k, 0), ALU.mult, ALU.add).then_inc(tr_dve, 1)
                    else:
                        dve.tensor_scalar(dst[:, k, 0:TP], bank[k % 4][:, :], scale(k, 0), None, ALU.mult).then_inc(tr_dve, 1)
                if KC - 2 not in ks:
                    return
                dve.wait_ge(tr_done, 9 * r + 9)
                for k in range(KC):
                    b = bank[4][:, k * TS:k * TS + TS]
                    if shift:
                        ins = dve.tensor_scalar(dst[:, k, TP:T], b, scale(k, 1), shift(k, 1), ALU.mult, ALU.add)
                    else:
                        ins = dve.tensor_scalar(dst[:, k, TP:T], b, scale(k, 1), None, ALU.mult)
                ins.then_inc(tr_dve, 1)

            dve.memset(CT, 0.0)
            dve.memset(SUMS, 1.0)
            dve.memset(OS, 1.0)
            dve.memset(SS, 1.0).then_inc(init_ready, 1)
            dve.wait_ge(small_t, 1)
            dve.tensor_copy(SMT, bank[7][:, 0:66]).then_inc(smt_ready, 1)
            dve.wait_ge(lam_ld, 16)
            lp = LPX[0:1, :].rearrange("o (a b d) -> o a b d", b=2, d=DB)
            lm = LPM[0:1, :].rearrange("o (a d) -> o a d", d=DB)
            chain(dve.tensor_tensor(lm, lp[:, :, 0, :], lp[:, :, 1, :], ALU.mult))
            dve.tensor_reduce(LAM[0:1, :], lm, AX, ALU.add).then_inc(lam_sum, 1)
            dve.wait_ge(smt_ready, 1)
            dve.tensor_scalar(GA[:, 0:1], SMT[:, 64:65], 1.0 - LAM0, None, ALU.mult)
            dve.tensor_copy(GA[:, 1:2], SMT[:, 65:66])
            dve.wait_ge(pool_c, 1)
            chain(dve.tensor_reduce(SEL2, IDENT.rearrange("p (q s) -> p s q", s=32)[:, 0:2, :], AX, ALU.add))
            chain(dve.scalar_tensor_tensor(out=BIAS[:, 0, :], in0=BIAS[:, 0, :], scalar=-1.0, in1=BIAS[:, 0, :], op0=ALU.mult, op1=ALU.max))
            for h in (1, 2, 3):
                ins = dve.tensor_scalar(BIAS[:, h, :], BIAS[:, 0, :], 2.0 ** (-8.0 * (h + 1) / HA), None, ALU.mult)
            chain(ins)
            chain(dve.tensor_scalar(BIAS[:, 0, :], BIAS[:, 0, :], 2.0 ** (-8.0 / HA), None, ALU.mult))
            chain(dve.memset(BIAS[0:DB, :, 448:512], BIG))
            dve.wait_ge(sq_done, NT)
            means(0, NT)
            dve.wait_ge(rs_ready, 1)
            for t in range(NT):
                norm(t)
            dve.wait_ge(lam_exp, 1)
            chain(dve.tensor_scalar(LAM[0:1, 1:2], LAM[0:1, 1:2], LAM0, None, ALU.subtract))
            dve.tensor_tensor(LAM[0:1, 0:1], LAM[0:1, 1:2], LAM[0:1, 0:1], ALU.subtract).then_inc(lam_neg, 1)
            for a in range(ADA_FIRST):
                mod_rows(a)
                mod(a)
            dve.wait_ge(lam_bc, 1)
            dve.tensor_copy(NLAM, bank[7][:, 0:1]).then_inc(nlam_ready, 1)
            dve.wait_ge(mod_ready, ADA_FIRST)
            turned(0, HT, lambda k, s: MOD[:, 8 + k, s:s + 1], lambda k, s: MOD[:, k, s:s + 1])

            for n_g in (1, 3, 5):
                for t in range(NT if n_g == 5 else 4):
                    dve.wait_ge(proj_done, 5 * n_g + t + (2 if n_g != 5 and t == 3 else 1))
                    if n_g == 5:
                        if t < 4:
                            ins = dve.tensor_copy(V[:, t, 512:D], bank[t][:, :])
                        else:
                            for x in range(2):
                                ins = dve.tensor_copy(V[0:TS, 4, 512 + 256 * x:768 + 256 * x], bank[4][x * TS:x * TS + TS, 0:256])
                    else:
                        dst, scale = (QT[:, 4:8], DB ** -0.5) if n_g == 3 else (KT[:, 0:4], 1.0)
                        for x in range(2):
                            ins = dve.tensor_scalar(dst[:, t, x * TH:x * TH + TH], bank[2 * (t % 2) + x][:, 0:TH], scale, None, ALU.mult)
                    ins.then_inc(proj_dve, 2 if n_g != 5 and t == 3 else 1)

            def a_read(u):
                i, h = UNITS[u]
                r, k = ROWS[i], KEYS[i]
                dve.wait_ge(sa_done, u + 1)
                if u >= 3:
                    dve.wait_ge(wta_done, u - 2)
                for m in range(2):
                    dve.tensor_tensor_reduce(SE[u % 3][0:r, m, 0:k], BIAS[0:r, h, BOFF[i]:BOFF[i] + k], bank[2 * (u % 2) + m][0:r, 0:k], 1.0, 3e38,
                                             ALU.add, ALU.min, MINS[0:r, u % 3, m:m + 1]).then_inc(sa_read, 1)

            def a_weights(u):
                i, h = UNITS[u]
                r, k = ROWS[i], KEYS[i]
                dve.wait_ge(ea_done, 2 * u + 2)
                co = CO[0:r, u % 3, :]
                chain(dve.reciprocal(co, SUMS[0:r, i, h, 1:2]))
                chain(dve.tensor_scalar(co, co, SUMS[0:r, i, h, 0:1], NLAM[0:r, :], ALU.mult, ALU.mult))
                dve.scalar_tensor_tensor(out=SE[u % 3][0:r, 1, 0:k], in0=SE[u % 3][0:r, 1, 0:k], scalar=co, in1=SE[u % 3][0:r, 0, 0:k],
                                         op0=ALU.mult, op1=ALU.add).then_inc(wa_ready, 1)

            for u in range(len(UNITS) + 1):
                if u < len(UNITS):
                    a_read(u)
                if u >= 1:
                    a_weights(u - 1)

            def b_part(h, s):
                if h < HB:
                    return P, ZS[s][0], ZS[s][1], bank[3 * (h % 2) + s]
                return P if s < PT else TS, s * 512, 512, bank[3 * (h % 2) + s]

            def b_abs(h):
                for x, s in enumerate((2, 1, 0)):
                    r, o, w, b = b_part(h, s)
                    dve.wait_ge(z_done, 3 * h + x + 1)
                    if h >= 2 and x == 0:
                        dve.wait_ge(p_done, 3 * (h - 1))
                    dve.tensor_scalar(LK[0:r, h % 2, o:o + w].bitcast(I32), b[0:r, 0:w].bitcast(I32), 0x7FFFFFFF, None,
                                      ALU.bitwise_and).then_inc(abs_ready, 1)

            def b_keep(h):
                for x, s in enumerate((2, 1, 0)):
                    r, o, w, b = b_part(h, s)
                    v = LK[0:r, h % 2, o:o + w]
                    dve.wait_ge(lk_ln, 3 * h + x + 1)
                    ins = dve.scalar_tensor_tensor(out=v, in0=b[0:r, 0:w], scalar=0.0, in1=v, op0=ALU.max, op1=ALU.add)
                    if h < HB:
                        chain(ins)
                        for c in [ZO[j] for j in ([0], [1], [2, 3])[s]]:
                            d = LK[:, h % 2, c:c + P]
                            ins = dve.tensor_tensor(d, d, UP, ALU.mult)
                    elif s == 2:
                        chain(ins)
                        d = v.rearrange("p (h q) -> p h q", q=TS)
                        ins = dve.tensor_tensor(d, d, UP[0:TS, 0:TS].unsqueeze(1).to_broadcast([TS, HB, TS]), ALU.mult)
                    ins.then_inc(lk_ready, 1)

            def a_mean():
                dve.wait_ge(oa_evac, len(UNITS))
                s0 = SUMS[:, :, :, 0]
                chain(dve.scalar_tensor_tensor(out=s0, in0=s0, scalar=EPS * P, in1=s0, op0=ALU.mult, op1=ALU.mult))
                chain(dve.tensor_tensor(OS[:, :, 0:HA], OS[:, :, 0:HA], s0, ALU.add))
                dve.tensor_scalar(OS[:, :, 0:HA], OS[:, :, 0:HA], 1.0 / P, None, ALU.mult).then_inc(osa_ready, 1)

            def a_norm(t):
                dve.wait_ge(ora_ready, 1)
                r = ROWS[t]
                a = OA[0:r, t, 0:512].rearrange("p (h d) -> p h d", d=P)
                dve.tensor_tensor(a, a, OR[0:r, t, 0:HA].unsqueeze(2).to_broadcast([r, HA, P]), ALU.mult).then_inc(on_ready, 1)

            def b_heads(h):
                return OA[:, 0:4, 512 + h * DB:512 + h * DB + DB] if h < HB else OA[0:TS, 4, 512:D].rearrange("p (h d) -> p h d", d=DB)

            def b_mean(h):
                dve.wait_ge(ob_evac, h + 1)
                o, m = b_heads(h), b_stat(OS, h)
                sq = (SQ[:, 0:4 * DB] if h < HB else SQ[0:TS, :]).rearrange("p (h d) -> p h d", d=DB)
                chain(dve.tensor_tensor(sq, o, o, ALU.mult))
                chain(dve.tensor_reduce(m, sq, AX, ALU.add))
                dve.tensor_scalar(m, m, 1.0 / DB, EPS, ALU.mult, ALU.add).then_inc(osb_ready, 1)

            def b_norm(h):
                dve.wait_ge(orb_ready, h + 1)
                o = b_heads(h)
                dve.tensor_tensor(o, o, b_stat(OR, h).unsqueeze(2).to_broadcast([P, 4, DB] if h < HB else [TS, HB, DB]), ALU.mult).then_inc(on_ready, 1)

            for b, c in enumerate((2, 2, 2, 2, 1, 1)):
                dve.wait_ge(ko_stored[b], 16 * c)
            for h in range(HB + 1):
                b_abs(h)
                if h:
                    mod(ADA_FIRST + h - 1)
                b_keep(h)
                if h < HB:
                    mod_rows(ADA_FIRST + h)
                if h == 0:
                    a_mean()
                if 2 <= h < 2 + NT:
                    a_norm(h - 2)
                if h >= 3:
                    b_mean(h - 3)
                if h >= 4:
                    b_norm(h - 4)
            b_mean(HB - 2)
            b_norm(HB - 3)
            b_mean(HB - 1)
            b_norm(HB - 2)
            b_norm(HB - 1)
            b_mean(HB)
            b_norm(HB)

            turned(1, OT, lambda k, s: GA[:, k // 4:k // 4 + 1], None)
            dve.wait_ge(new_stored, 64)
            scale2, shift2 = lambda k, s: MOD[:, 32 + k, s:s + 1], lambda k, s: MOD[:, 24 + k, s:s + 1]
            for t in range(NT):
                if t == 4:
                    turned(2, HT, scale2, shift2, (0, 2))
                r = ROWS[t]
                dve.wait_ge(wo_done, t + 1)
                dve.wait_ge(g1_ready, t // 4 + 1)
                for x in range(2):
                    c = slice(512 * x, 512 * x + 512)
                    b = bank[WOB[t][x]] if t < 4 else bank[7][x * TS:x * TS + TS, :]
                    ins = dve.tensor_tensor(XN[0:r, t, c], b[0:r, :], G1[0:r, t // 4, c], ALU.mult)
                ins.then_inc(x1_part, 1)
                dve.wait_ge(x1_part, t + 1)
                dve.tensor_tensor(X[0:r, t, :], X[0:r, t, :], XN[0:r, t, :], ALU.add).then_inc(x1_ready, 1)
                dve.wait_ge(sq_done, NT + t + 1)
                means(t, t + 1)
                dve.wait_ge(rs_ready, 2 + t)
                norm(t)
            turned(2, HT, scale2, shift2, (4, 6))

            dve.wait_ge(logit_done, 1)
            dve.memset(GS, -3e38)
            dve.memset(GREP, -3e38)
            dve.memset(SELX, -3e38)
            dve.memset(MS[:, 0, :], 0.0)
            dve.memset(EREP, -3e38)
            dve.memset(SC, 0.5).then_inc(sc_clear, 1)
            dve.wait_ge(sc_ready, 1)
            chain(dve.tensor_tensor(SEL, SC, BR.unsqueeze(1).to_broadcast([P, NT, NE]), ALU.add))
            for t in range(NT):
                for g in range(NG):
                    last = dve.max(G8[:, t * NG + g, :], SEL[:, t, g * EG:g * EG + EG])
            chain(last)
            g8 = G8.rearrange("p (t g) e -> p t g e", g=NG)
            chain(dve.tensor_tensor(GS[:, :, 0:NG], g8[:, :, :, 0], g8[:, :, :, 1], ALU.add))
            for t in range(NT):
                last = dve.max(GTOP[:, t, :], GS[:, t, :])
            chain(last)
            chain(dve.tensor_copy(GREP[:, :, 0:TOPG], GTOP[:, :, 0:TOPG]))
            for t in range(NT):
                last = dve.match_replace(GOUT[:, t, :], GREP[:, t, :], GS[:, t, :], 3e38)
            chain(last)
            chain(dve.tensor_scalar(KEEP, GOUT[:, :, 0:NG], 3e38, None, ALU.is_equal))
            chain(dve.tensor_scalar(NEGK, KEEP, 1.0, BIG, ALU.subtract, ALU.mult))
            for t in range(NT):
                v = SELX[:, t, 0:NE].rearrange("p (g e) -> p g e", e=EG)
                last = dve.tensor_tensor(v, SEL[:, t, :].rearrange("p (g e) -> p g e", e=EG), KEEP[:, t, :].unsqueeze(2).to_broadcast([P, NG, EG]), ALU.mult)
            chain(last)
            for t in range(NT):
                v = SELX[:, t, 0:NE].rearrange("p (g e) -> p g e", e=EG)
                last = dve.tensor_tensor(v, v, NEGK[:, t, :].unsqueeze(2).to_broadcast([P, NG, EG]), ALU.add)
            chain(last)
            for t in range(NT):
                last = dve.max(ETOP[:, t, :], SELX[:, t, :])
            chain(last)
            chain(dve.tensor_copy(EREP[:, :, 0:TOPK], ETOP[:, :, 0:TOPK]))
            for t in range(NT):
                last = dve.match_replace(EOUT[:, t, :], EREP[:, t, :], SELX[:, t, :], 3e38)
            chain(last)
            chain(dve.tensor_scalar(M, EOUT[:, :, 0:NE], 3e38, None, ALU.is_equal))
            chain(dve.memset(M[DB:P, 4, :], 0.0))
            for t in range(NT):
                ins = dve.tensor_tensor(MS[:, t + 1, :], MS[:, t, :], M[:, t, :], ALU.add)
                if t < NT - 1:
                    chain(ins)
            ins.then_inc(mask_ready, 1)
            dve.wait_ge(pos_done, 1)
            chain(dve.tensor_scalar(NB_I, bank[7][:, 0:NE], float(SLOT - 1), None, ALU.add))
            chain(dve.tensor_scalar(NB_J, NB_I, 6, None, ALU.logical_shift_right))
            dve.memset(ZE, 0.0)
            chain(dve.tensor_scalar(NB, NB_J, 1.0, None, ALU.max))
            chain(dve.tensor_tensor_scan(INC, NB, ZE, 0.0, ALU.add, ALU.add))
            chain(dve.tensor_tensor(STF[:, 0:NE], INC, NB, ALU.subtract))
            chain(dve.tensor_scalar(NB_I[:, 0:1], INC[:, NE - 1:NE], 1.0, None, ALU.add))
            dve.tensor_scalar(START[:, NE:NE + 1], NB_I[:, 0:1], 1, 1, ALU.logical_shift_right, ALU.logical_shift_left)
            dve.tensor_scalar(START[:, NE + 1:NE + 2], NB_I[:, 0:1], 1, None, ALU.logical_shift_right)
            dve.tensor_copy(START[:, 0:NE], STF[:, 0:NE]).then_inc(start_ready, 1)
            chain(dve.tensor_scalar(SB, STF[:, 0:NE], float(SLOT), float(SLOT + 1), ALU.mult, ALU.add))
            chain(dve.tensor_tensor(SL, bank[6][:, 0:NT * NE].rearrange("p (t e) -> p t e", e=NE), SB.unsqueeze(1).to_broadcast([P, NT, NE]), ALU.add))
            chain(dve.tensor_tensor(SL, SL, M, ALU.mult))
            for t in range(NT):
                last = dve.max(S8[:, t, :], SL[:, t, :])
            chain(last)
            chain(dve.tensor_scalar(SIDX, S8, 1.0, None, ALU.subtract))
            dve.tensor_scalar(COLI, SIDX, 6, None, ALU.logical_shift_right)
            chain(dve.tensor_scalar(PLI, SIDX, SLOT - 1, None, ALU.bitwise_and))
            dve.tensor_copy(COLF, COLI)
            chain(dve.tensor_copy(PLF, PLI))
            dve.memset(ICUR, 0).then_inc(sidx_ready, 1)
            dve.wait_ge(rec_ready, 1)
            for t in range(NT):
                if t >= 2:
                    dve.wait_ge(oh_done, TOPK * (t - 1))
                if t not in (0, 2):
                    dve.tensor_tensor(OHI[t % 2], ITEMS.unsqueeze(1).to_broadcast([P, TOPK, IC]), COLF[:, t, 0:TOPK].unsqueeze(2).to_broadcast([P, TOPK, IC]),
                                      ALU.is_equal).then_inc(ohi_rest, 1)
                each = [P, TOPK, SLOT]
                chain(dve.tensor_tensor(OHP[t % 2], PLACES.unsqueeze(1).to_broadcast(each), PLF[:, t, 0:TOPK].unsqueeze(2).to_broadcast(each), ALU.is_equal))
                dve.tensor_tensor(OHP[t % 2], OHP[t % 2], RECF[:, t, 0:TOPK].unsqueeze(2).to_broadcast(each), ALU.mult).then_inc(ohp_ready, 1)
            dve.wait_ge(h2_stored, 16 * NT)
            dve.memset(YO[0], 0.0)
            dve.memset(YO[1], 0.0).then_inc(yo_ready, 1)
            dve.wait_ge(oh_done, NT * TOPK)
            dve.tensor_scalar(IDX[0:SLOT, 1, :], bank[7][0:SLOT, 0:IC], float(NONE), None, ALU.add)
            chain(dve.tensor_scalar(IDX[SLOT:P, 1, :], bank[7][SLOT:P, 0:IC], float(NONE + 1), None, ALU.add))
            chain(dve.tensor_scalar(IDX[:, 0, :], IDX[:, 1, :], 4, 1, ALU.logical_shift_right, ALU.logical_shift_left))
            dve.tensor_scalar(IDX[SLOT:P, 0, :], IDX[SLOT:P, 0, :], 1, None, ALU.bitwise_or).then_inc(idx_ready, 1)

            hgt = HGT.rearrange("p c h s -> p (c h s)")
            dve.wait_ge(hgt_done, 1)
            dve.tensor_copy(hgt, bank[1][:, :]).then_inc(hgt_ready, 1)
            pairs = dve.value_load(START[0:1, NE + 1:NE + 2], min_val=1, max_val=NI // 2)

            def out_rows(i, x, count):
                dve.wait_ge(dn_done, i + 1)
                dve.wait_ge(scattered[x], count)
                dve.tensor_copy(YO[x], bank[3][:, :]).then_inc(yo_ready, 1)

            with dve.Fori(0, pairs) as g:
                for x in range(2):
                    i = g * 2 + x
                    dve.wait_ge(silu_done, i + 1)
                    dve.tensor_tensor(AC, SI, bank[0][:, P:2 * P], ALU.mult).then_inc(ac_ready, 1)
                    dve.wait_ge(hgt_done, i + 2)
                    dve.tensor_copy(hgt, bank[1][:, :]).then_inc(hgt_ready, 1)
                    out_rows(i, x, (g + 1) * 16)
            out_rows(pairs * 2, 0, (pairs + 1) * 16)
            chain(dve.tensor_tensor(COMB, SC, M, ALU.mult))
            chain(dve.tensor_reduce(DEN, COMB, AX, ALU.add))
            chain(dve.tensor_scalar(DEN, DEN, 1e-38, None, ALU.max))
            chain(dve.reciprocal(RDEN, DEN))
            chain(dve.tensor_scalar(RDEN, RDEN, 2.5, None, ALU.mult))
            chain(dve.tensor_tensor(COMB, COMB, RDEN.unsqueeze(2).to_broadcast([P, NT, NE]), ALU.mult))
            for t in range(NT):
                for k in range(TOPK):
                    ins = dve.scalar_tensor_tensor(out=EJ[:, k, :], in0=SL[:, t, :], scalar=S8[:, t, k:k + 1], in1=COMB[:, t, :],
                                                   op0=ALU.is_equal, op1=ALU.mult, accum_out=W6[:, t, k:k + 1])
                chain(ins)
            dve.sem_inc(w6_ready)

            def finish(t):
                r = ROWS[t]
                dve.wait_ge(fin_sq, t + 1)
                dve.tensor_scalar(SS[:, t:t + 1], SS[:, t:t + 1], 1.0 / D, EPS, ALU.mult, ALU.add).then_inc(fin_ms, 1)
                dve.wait_ge(fin_rs, t + 1)
                dve.scalar_tensor_tensor(out=X[0:r, t, :], in0=X[0:r, t, :], scalar=RS[0:r, t:t + 1], in1=GF[0:r, :], op0=ALU.mult, op1=ALU.mult).then_inc(y_ready, 1)

            def routed(t):
                r = ROWS[t]
                parts = YB[t]
                dve.wait_ge(yb_ld[t], 16 * len(parts))
                acc = parts[0][1][0:r, 0, :]
                dve.wait_ge(yb_first, t + 1)
                for first, part in parts:
                    for k in range(max(first, 1), first + part.shape[1]):
                        chain(dve.scalar_tensor_tensor(out=acc, in0=part[0:r, k - first, :], scalar=W6[0:r, t, k:k + 1], in1=acc, op0=ALU.mult, op1=ALU.add))

            def shared(t):
                r = ROWS[t]
                acc = YB[t][0][1][0:r, 0, :]
                dve.wait_ge(sd_done, t + 1)
                for n in range(2):
                    a = acc[:, 512 * n:512 * n + 512]
                    ins = dve.tensor_tensor(a, a, bank[SDB[t][n]][0:r, :] if t < 4 else bank[SDB[t][0]][n * TS:n * TS + TS, :], ALU.add)
                ins.then_inc(acc_ready, 1)

            routed(0)
            routed(1)
            for f in range(2):
                dve.wait_ge(sg_silu, f + 1)
                dve.wait_ge(sg_done, 3 + f)
                for x in range(2):
                    a = SA[:, f, x * TH:x * TH + TH]
                    ins = dve.tensor_tensor(a, a, bank[SGB[2 + f][x]][:, 0:TH], ALU.mult)
            ins.then_inc(as_ready, 1)
            dve.wait_ge(gf_ld, 16)
            routed(2)
            shared(0)
            routed(3)
            shared(1)
            shared(2)
            routed(4)
            shared(3)
            finish(0)
            shared(4)
            for t in (3, 4):
                r = ROWS[t]
                acc = YB[t][0][1][0:r, 0, :]
                dve.wait_ge(acc_ready, t + 1)
                chain(dve.tensor_tensor(acc, acc, G2[0:r, t // 4, :], ALU.mult))
                dve.tensor_tensor(X[0:r, t, :], X[0:r, t, :], acc, ALU.add).then_inc(fin_last, 1)
            for t in range(1, NT):
                finish(t)


_INS = ["x_prompt", "x_sample", "cache_a_k", "cache_a_v", "cache_b_k", "cache_b_v", "c_prompt", "c_sample", "w_ada", "b_ada",
        "w_in", "lam_params", "g_sub_a", "g_sub_b", "w_out", "w_router", "b_router", "w_gate", "w_up", "w_down",
        "w_shared_gate", "w_shared_up", "w_shared_down", "g_final"]
_OUTS = [(1, TP, D), (1, TS, D), (1, 1, TP, HA, P), (1, 1, TP, HA, P), (1, 1, TP, HB, DB), (1, 1, TP, HB, DB),
         (1, 1, TS, HA, P), (1, 1, TS, HA, P), (1, 1, TS, HB, DB), (1, 1, TS, HB, DB)]


def kernel(**inputs):
    import numpy as np
    import concourse.bacc as bacc
    from concourse.bass_utils import run_bass_kernel_spmd

    nc = bacc.Bacc("TRN2", target_bir_lowering=False, num_devices=1)
    arrays, args = {}, []
    for name in _INS:
        a = np.ascontiguousarray(inputs[name])
        arrays[f"in_{name}"] = a
        args.append(nc.dram_tensor(f"in_{name}", a.shape, F32, kind="ExternalInput").ap())
    for i, shape in enumerate(_OUTS):
        args.append(nc.dram_tensor(f"out_{i}", shape, F32, kind="ExternalOutput").ap())
    build(nc, *args)
    r = run_bass_kernel_spmd(nc, [arrays], core_ids=[0])
    return tuple(r.results[0][f"out_{i}"] for i in range(len(_OUTS)))
```
